# Optimizing a Trainium2 kernel written in Bass

```python
import numpy as np
import jax
import jax.numpy as jnp
from jax import lax

D_MODEL = 1024
BATCH = 1
SEQ = 512
DEPTH = 2

EPS = 1e-6
ROPE_THETA = 10000.0
NEG = -1e30
TINY = 1e-30
Q_BLOCK = 128

NSA_HEADS = 8
NSA_KV_GROUPS = 2
NSA_HEAD_DIM = 64
CMP_BLOCK = 32
CMP_STRIDE = 16
CMP_HIDDEN = 4 * NSA_HEAD_DIM
SLC_BLOCK = 64
SLC_TOPK = 16
N_LOCAL_FORCED = 2
FORCE_BONUS = 1e4
SLC_Q_BLOCK = 64
WINDOW = 512

MLA_HEADS = 8
MLA_Q_LORA = 256
MLA_KV_LORA = 128
MLA_NOPE = 64
MLA_ROPE = 32
MLA_V = 64

D_FF = 4 * D_MODEL

NSA_Q_COLS = NSA_HEADS * NSA_HEAD_DIM
NSA_KV_COLS = 2 * NSA_KV_GROUPS * NSA_HEAD_DIM
NSA_GATE_COLS = 3 * NSA_HEADS
IN_SPLITS = (NSA_Q_COLS, NSA_KV_COLS, NSA_KV_COLS, NSA_KV_COLS, NSA_GATE_COLS,
             MLA_Q_LORA, MLA_KV_LORA, MLA_ROPE, D_MODEL, D_MODEL)
IN_COLS = sum(IN_SPLITS)

kernel_name = 'hybrid_nsa_mla_gated_block'

def rms_norm(x, g):
    xf = x.astype(jnp.float32)
    y = xf * lax.rsqrt(jnp.mean(xf * xf, axis=-1, keepdims=True) + EPS)
    return (y * g.astype(jnp.float32)).astype(x.dtype)

def rope(x, pos):
    d = x.shape[-1]
    inv = ROPE_THETA ** (-jnp.arange(0, d, 2, dtype=jnp.float32) / d)
    ang = pos.astype(jnp.float32)[:, None] * inv[None, :]
    cos, sin = jnp.cos(ang), jnp.sin(ang)
    x1, x2 = jnp.split(x.astype(jnp.float32), 2, axis=-1)
    out = jnp.concatenate([x1 * cos - x2 * sin, x1 * sin + x2 * cos], axis=-1)
    return out.astype(x.dtype)

def masked_softmax(s, mask):
    sf = jnp.where(mask, s.astype(jnp.float32), NEG)
    m = jnp.max(sf, axis=-1, keepdims=True)
    e = jnp.where(mask, jnp.exp(sf - m), 0.0)
    p = e / jnp.maximum(jnp.sum(e, axis=-1, keepdims=True), TINY)
    return p.astype(s.dtype)

def split_cols(t):
    offsets = np.cumsum(np.array(IN_SPLITS))[:-1].tolist()
    return jnp.split(t, offsets, axis=-1)

def overlap_matrix(n_cmp, n_slc):
    start = np.arange(n_cmp) * CMP_STRIDE
    sel = np.arange(n_slc) * SLC_BLOCK
    lo = np.maximum(start[:, None], sel[None, :])
    hi = np.minimum(start[:, None] + CMP_BLOCK, sel[None, :] + SLC_BLOCK)
    return (np.clip(hi - lo, 0, None) / CMP_BLOCK).astype(np.float32)

_gather_bg = jax.vmap(jax.vmap(lambda t, i: t[i]))

def nsa_attention(q_flat, kv_cmp, kv_slc, kv_win, gate_logits, cmp_pe, cmp_w1, cmp_w2, pos):
    B, S, _ = q_flat.shape
    G, R, hd = NSA_KV_GROUPS, NSA_HEADS // NSA_KV_GROUPS, NSA_HEAD_DIM
    scale = hd ** -0.5
    q = rope(q_flat.reshape(B, S, G, R, hd).transpose(0, 2, 3, 1, 4), pos)

    def split_kv(kv):
        a = kv.reshape(B, S, 2, G, hd).transpose(2, 0, 3, 1, 4)
        return rope(a[0], pos), a[1]

    k_c, v_c = split_kv(kv_cmp)
    k_s, v_s = split_kv(kv_slc)
    k_w, v_w = split_kv(kv_win)

    n_cmp = (S - CMP_BLOCK) // CMP_STRIDE + 1
    blk_idx = jnp.arange(n_cmp)[:, None] * CMP_STRIDE + jnp.arange(CMP_BLOCK)[None, :]

    def compress(t, j):
        tb = t[:, :, blk_idx] + cmp_pe[j]
        h = jax.nn.silu(tb.reshape(B, G, n_cmp, CMP_BLOCK * hd) @ cmp_w1[j])
        return h @ cmp_w2[j]

    kc = compress(k_c, 0)
    vc = compress(v_c, 1)
    cmp_end = jnp.arange(n_cmp) * CMP_STRIDE + CMP_BLOCK - 1
    cmp_mask = cmp_end[None, :] <= pos[:, None]
    s_cmp = jnp.einsum('bgrsd,bgnd->bgrsn', q, kc) * scale
    p_cmp = masked_softmax(s_cmp, cmp_mask)
    o_cmp = jnp.einsum('bgrsn,bgnd->bgrsd', p_cmp, vc)

    n_slc = S // SLC_BLOCK
    k_top = min(SLC_TOPK, n_slc)
    ov = jnp.asarray(overlap_matrix(n_cmp, n_slc))
    imp = jnp.einsum('bgrsn,nj->bgsj', p_cmp.astype(jnp.float32), ov)
    blk = jnp.arange(n_slc)[None, :]
    cur = (pos // SLC_BLOCK)[:, None]
    causal = blk <= cur
    forced = (blk == 0) | ((cur - blk >= 0) & (cur - blk < N_LOCAL_FORCED))
    score = jnp.where(causal, imp + jnp.where(forced, FORCE_BONUS, 0.0), NEG)
    vals, sel_idx = lax.top_k(score, k_top)
    sel_ok = vals > 0.5 * NEG

    QS = SLC_Q_BLOCK
    nq = S // QS
    qc = jnp.moveaxis(q.reshape(B, G, R, nq, QS, hd), 3, 0)
    ic = jnp.moveaxis(sel_idx.reshape(B, G, nq, QS, k_top), 2, 0)
    okc = jnp.moveaxis(sel_ok.reshape(B, G, nq, QS, k_top), 2, 0)
    pc = pos.reshape(nq, QS)

    def slc_block(args):
        qb, ib, okb, tb = args
        tok = (ib[..., None] * SLC_BLOCK + jnp.arange(SLC_BLOCK)).reshape(
            ib.shape[:-1] + (ib.shape[-1] * SLC_BLOCK,))
        kg = _gather_bg(k_s, tok)
        vg = _gather_bg(v_s, tok)
        mask = jnp.repeat(okb, SLC_BLOCK, axis=-1) & (tok <= tb[:, None])
        s = jnp.einsum('bgrqd,bgqtd->bgrqt', qb, kg) * scale
        p = masked_softmax(s, mask[:, :, None])
        return jnp.einsum('bgrqt,bgqtd->bgrqd', p, vg)

    o_slc = lax.map(slc_block, (qc, ic, okc, pc))
    o_slc = jnp.moveaxis(o_slc, 0, 3).reshape(B, G, R, S, hd)

    nb = S // Q_BLOCK
    pad = ((0, 0), (0, 0), (WINDOW, 0), (0, 0))
    band = jnp.arange(nb)[:, None] * Q_BLOCK + jnp.arange(Q_BLOCK + WINDOW)[None, :]
    kband = jnp.moveaxis(jnp.pad(k_w, pad)[:, :, band], 2, 0)
    vband = jnp.moveaxis(jnp.pad(v_w, pad)[:, :, band], 2, 0)
    kpos = band - WINDOW
    qw = jnp.moveaxis(q.reshape(B, G, R, nb, Q_BLOCK, hd), 3, 0)
    pw = pos.reshape(nb, Q_BLOCK)

    def win_block(args):
        qb, kb, vb, tq, tk = args
        diff = tq[:, None] - tk[None, :]
        mask = (tk[None, :] >= 0) & (diff >= 0) & (diff < WINDOW)
        s = jnp.einsum('bgrqd,bgkd->bgrqk', qb, kb) * scale
        p = masked_softmax(s, mask)
        return jnp.einsum('bgrqk,bgkd->bgrqd', p, vb)

    o_win = lax.map(win_block, (qw, kband, vband, pw, kpos))
    o_win = jnp.moveaxis(o_win, 0, 3).reshape(B, G, R, S, hd)

    g = jax.nn.sigmoid(gate_logits).reshape(B, S, 3, G, R).transpose(2, 0, 3, 4, 1)[..., None]
    o = g[0] * o_cmp + g[1] * o_slc + g[2] * o_win
    return o.transpose(0, 3, 1, 2, 4).reshape(B, S, NSA_HEADS * hd)

def mla_attention(cq, ckv, k_rope_raw, q_norm, kv_norm, w_uq, w_ukv, pos):
    B, S, _ = cq.shape
    H = MLA_HEADS
    dq = MLA_NOPE + MLA_ROPE
    q = (rms_norm(cq, q_norm) @ w_uq).reshape(B, S, H, dq).transpose(0, 2, 1, 3)
    q = jnp.concatenate([q[..., :MLA_NOPE], rope(q[..., MLA_NOPE:], pos)], axis=-1)
    kv = (rms_norm(ckv, kv_norm) @ w_ukv).reshape(B, S, H, MLA_NOPE + MLA_V).transpose(0, 2, 1, 3)
    k_nope, v = kv[..., :MLA_NOPE], kv[..., MLA_NOPE:]
    k_pe = rope(k_rope_raw[:, None], pos)
    k = jnp.concatenate([k_nope, jnp.broadcast_to(k_pe, (B, H, S, MLA_ROPE))], axis=-1)
    scale = dq ** -0.5
    nb = S // Q_BLOCK
    qc = jnp.moveaxis(q.reshape(B, H, nb, Q_BLOCK, dq), 2, 0)
    pc = pos.reshape(nb, Q_BLOCK)

    def blk(args):
        qb, tq = args
        s = jnp.einsum('bhqd,bhkd->bhqk', qb, k) * scale
        p = masked_softmax(s, tq[:, None] >= pos[None, :])
        return jnp.einsum('bhqk,bhkd->bhqd', p, v)

    o = jnp.moveaxis(lax.map(blk, (qc, pc)), 0, 2).reshape(B, H, S, MLA_V)
    return o.transpose(0, 2, 1, 3).reshape(B, S, H * MLA_V)

def setup_inputs(seed: int = 0) -> dict:
    key = jax.random.key(seed)
    ks = jax.random.split(key, 20)
    L = DEPTH
    hd = NSA_HEAD_DIM

    def nrm(k, shape, scale):
        return jax.random.normal(k, shape, jnp.float32) * scale

    def gain(k, shape):
        return 1.0 + nrm(k, shape, 0.02)

    return {
        'x': nrm(ks[0], (BATCH, SEQ, D_MODEL), 1.0),
        'attn_norm': gain(ks[1], (L, D_MODEL)),
        'w_in': nrm(ks[2], (L, D_MODEL, IN_COLS), D_MODEL ** -0.5),
        'cmp_pe': nrm(ks[3], (L, 2, CMP_BLOCK, hd), 0.1),
        'cmp_w1': nrm(ks[4], (L, 2, CMP_BLOCK * hd, CMP_HIDDEN), (CMP_BLOCK * hd) ** -0.5),
        'cmp_w2': nrm(ks[5], (L, 2, CMP_HIDDEN, hd), CMP_HIDDEN ** -0.5),
        'nsa_w_o': nrm(ks[6], (L, NSA_Q_COLS, D_MODEL), NSA_Q_COLS ** -0.5),
        'mla_q_norm': gain(ks[7], (L, MLA_Q_LORA)),
        'mla_kv_norm': gain(ks[8], (L, MLA_KV_LORA)),
        'mla_w_uq': nrm(ks[9], (L, MLA_Q_LORA, MLA_HEADS * (MLA_NOPE + MLA_ROPE)), MLA_Q_LORA ** -0.5),
        'mla_w_ukv': nrm(ks[10], (L, MLA_KV_LORA, MLA_HEADS * (MLA_NOPE + MLA_V)), MLA_KV_LORA ** -0.5),
        'mla_w_o': nrm(ks[11], (L, MLA_HEADS * MLA_V, D_MODEL), (MLA_HEADS * MLA_V) ** -0.5),
        'w_out': nrm(ks[12], (L, D_MODEL, D_MODEL), D_MODEL ** -0.5),
        'mlp_norm': gain(ks[13], (L, D_MODEL)),
        'w_up': nrm(ks[14], (L, D_MODEL, D_FF), D_MODEL ** -0.5),
        'w_down': nrm(ks[15], (L, D_FF, D_MODEL), D_FF ** -0.5),
        'final_norm': gain(ks[16], (D_MODEL,)),
    }

def reference(x, attn_norm, w_in, cmp_pe, cmp_w1, cmp_w2, nsa_w_o, mla_q_norm, mla_kv_norm,
              mla_w_uq, mla_w_ukv, mla_w_o, w_out, mlp_norm, w_up, w_down, final_norm):
    S = x.shape[1]
    pos = jnp.arange(S, dtype=jnp.int32)
    for l in range(DEPTH):
        xn = rms_norm(x, attn_norm[l])
        (nsa_q, kv_c, kv_s, kv_w, nsa_g, cq, ckv, k_rope_raw,
         gate_a, gate_b) = split_cols(xn @ w_in[l])
        o_a = nsa_attention(nsa_q, kv_c, kv_s, kv_w, nsa_g, cmp_pe[l], cmp_w1[l], cmp_w2[l], pos)
        o_b = mla_attention(cq, ckv, k_rope_raw, mla_q_norm[l], mla_kv_norm[l],
                            mla_w_uq[l], mla_w_ukv[l], pos)
        merged = (jax.nn.sigmoid(gate_a) * (o_a @ nsa_w_o[l])
                  + jax.nn.sigmoid(gate_b) * (o_b @ mla_w_o[l]))
        x = x + merged @ w_out[l]
        hn = rms_norm(x, mlp_norm[l])
        x = x + jnp.square(jax.nn.relu(hn @ w_up[l])) @ w_down[l]
    return rms_norm(x, final_norm)


_drawn_inputs = setup_inputs


def setup_inputs(seed=0):
    import zlib

    import numpy as np

    out = dict(_drawn_inputs(seed))
    spreads = {}
    factors = {'attn_norm': 8.0,
     'cmp_pe': 2.711,
     'mla_q_norm': 8.0,
     'mla_kv_norm': 8.0,
     'final_norm': 2.846}
    for name, (base, spread) in spreads.items():
        noise = np.random.default_rng([zlib.crc32(name.encode()), seed]).standard_normal(out[name].shape)
        drawn = base * np.exp(spread * noise) if base else spread * noise
        out[name] = jnp.asarray(drawn.astype(out[name].dtype))
    for name, factor in factors.items():
        out[name] = (out[name] * factor).astype(out[name].dtype)
    return out
```

```python
from contextlib import ExitStack

import concourse.bass as bass
from concourse import mybir

F32 = mybir.dt.float32
R32 = mybir.dt.float32r
BF16 = mybir.dt.bfloat16
ACT = mybir.ActivationFunctionType
ALU = mybir.AluOpType
AX = mybir.AxisListType

P = 128
L = 2
S = 512
D = 1024
KT = D // P
QT = S // P
HD = 64
HEADS = 8
PAIRS = HEADS // 2
N_CMP = 31
NC = 32
EPS = 1e-6
TINY = 1e-30
NSA_SCALE = HD ** -0.5
MLA_SCALE = 96 ** -0.5

U_Q, U_KS, U_KW, U_V, U_KC, U_VC, U_MISC, U_CQ, U_CKV = 0, 4, 5, 6, 8, 9, 10, 11, 13
U_GATE, U_W1, U_W2K, U_W2V, U_MLA, U_WO, U_OUT, U_MLP = 14, 30, 38, 39, 40, 44, 52, 60
QUARTERS = 4
U_QUARTER = 2 * KT
NU = U_MLP + QUARTERS * U_QUARTER
G_Q, G_KS, G_KW, G_KC, G_VC, G_MISC, G_CQ, G_CKV = 0, 4, 5, 6, 7, 8, 9, 11
G_GATE, G_MLA, G_OUT, G_MLP = 12, 28, 44, 52
NG = G_MLP + QUARTERS * U_QUARTER
ROPE_TILES = [0, 1, 2, 3, G_KS, G_KW, G_KC]
WUSED0 = 2
GFREE0 = KT + 2
PR_ATTN, PR_MLP, PR_QN, PR_KVN, PR_PE, NPAR = 0, 8, 16, 18, 19, 51

NSA_JOBS = [(t, e, br, qt) for t in range(PAIRS) for e in range(2) for br in range(2) for qt in range(QT)]
MLA_JOBS = [(t, e, 0, qt) for t in range(PAIRS) for e in range(2) for qt in range(QT)]
NJ = len(NSA_JOBS) + len(MLA_JOBS)
NSA_PASSES = len(NSA_JOBS) // QT
NHP = NJ // QT
PT_STEP = 384
PT_LEN = 3 * PT_STEP + S
LAG_SCALE, LAG_T, LAG_LO, LAG_PV, LAG_OHI, LAG_OLO = 1, 2, 3, 4, 5, 6

AREA = 13312


class Chain:

    def __init__(self, eng, sem):
        self.eng, self.sem, self.n = eng, sem, 0

    def restart(self):
        self.eng.sem_clear(self.sem)
        self.n = 0

    def mark(self, ins):
        ins.then_inc(self.sem, 1)
        self.n += 1

    def wait(self):
        self.eng.wait_ge(self.sem, self.n)


def build(nc, units, params, x_in, tables, cf32, cmasks, gates_dram, out):
    ctx = ExitStack()
    with ctx:
        def sb(name, shape, dt):
            return ctx.enter_context(nc.sbuf_tensor(name, shape, dt))

        def bank(name):
            return ctx.enter_context(nc.psum_tensor(name, [P, 512], F32))

        def sem(name):
            return ctx.enter_context(nc.semaphore(name))

        x = sb("x", [P, KT, S], F32)
        stage = sb("stage", [P, 2, 1024], F32)
        wsplit = sb("wsplit", [P, 2, 2, 1024], R32)
        xg = sb("xg", [P, 2, KT, S], R32)
        area = sb("area", [P, AREA], R32)
        area_b = sb("area_b", [P, 2 * 2 * PT_LEN], R32)
        pcT = sb("pcT", [P, 2, 2, S], R32)
        cn = sb("cn", [P, 2, 3, S], R32)
        vblk = sb("vblk", [P, 2, 4, P], R32)
        F = sb("F", [P, 8, S], F32)
        Y = sb("Y", [P, 2, S], F32)
        rs = sb("rs", [P, S], F32)
        kpe = sb("kpe", [P, S], F32)
        rope = sb("rope", [P, 3, S], F32)
        constf = sb("constf", [P, 2, P], F32)
        constb = sb("constb", [P, 3, P], BF16)
        ones = sb("ones", [P, P], F32)
        par_all = sb("par_all", [P, L * NPAR + KT], F32)
        par = sb("par", [P, NPAR], F32)
        rc = sb("rc", [P, 3, QT], F32)
        gt = sb("gt", [P, QT, 24], F32)
        small = sb("small", [P, 4, 17], F32)
        nmx = sb("nmx", [P, 4], F32)
        sums = sb("sums", [P, 4], F32)
        rsum = sb("rsum", [P, 4], F32)

        QS = area[:, 0:4096].rearrange("p (h n) -> p h n", h=HEADS)
        KN = area[:, 4096:8192].rearrange("p (b g c n) -> p b g c n", b=2, g=2, c=2)
        VN = area[:, 8192:13312].rearrange("p (c b t n) -> p c b t n", c=2, b=2, t=QT)
        MQ = area[:, 0:4096].rearrange("p (s e c n) -> p s e c n", s=2, e=2, c=2)
        MK = area[:, 4096:8192].rearrange("p (s e c n) -> p s e c n", s=2, e=2, c=2)
        MV = area[:, 8192:11264].rearrange("p (s c t n) -> p s c t n", s=2, c=2, t=QT)
        H = area[:, 0:8192].rearrange("p (c m n) -> p c m n", c=2, m=KT)
        PT = area_b[:, :].rearrange("p (s c n) -> p s c n", s=2, c=2)
        TB = area_b[:, 0:4096].rearrange("p (k c j n) -> p k c j n", k=2, c=2, j=16)
        HK = area_b[:, 4096:4352].rearrange("p (c j n) -> p c j n", c=2, j=2)
        kcmp = area_b[:, S + PT_STEP:S + PT_STEP + 4 * NC].rearrange("p (c n) -> p c n", c=2)
        HV = area_b[:, 4352:5376].rearrange("p (c j g n) -> p c j g n", c=2, j=2, g=2)
        ident, mask01 = constf[:, 0, :], constf[:, 1, :].rearrange("p (q n) -> p q n", q=QT)
        identb, causal = constb[:, 0, :], constb[:, 1, :]
        cmask = constb[:, 2, :].rearrange("p (q n) -> p q n", q=QT)
        cosN, sinN, tabM = rope[:, 0, :], rope[:, 1, :], rope[:, 2, :]

        G = [bank("G0"), bank("G1")]
        SB = [bank("S0"), bank("S1")]
        TP = [bank("T0"), bank("T1")]
        O = [bank("O0"), bank("O1")]

        def sems(*names):
            return [sem(n) for n in names]

        eps = small[:, 0, 16:17]
        tbf = F[:, 0:2, :].rearrange("p a n -> p (a n)")
        final = [F[:, 4, :], F[:, 5, :], F[:, 6, :], F[:, 7, :], F[:, 0, :], F[:, 1, :], Y[:, 0, :], Y[:, 1, :]]

        def pt_view(slot, c, qt):
            if qt < 3:
                t = PT[:, slot, c, 0:QT * PT_STEP].rearrange("p (k n) -> p k n", n=PT_STEP)
                return t[:, 0:qt + 1, qt * P:(qt + 1) * P]
            t = PT[:, slot, c, P:P + QT * PT_STEP].rearrange("p (k n) -> p k n", n=PT_STEP)
            return t[:, 0:QT, 2 * P:3 * P]

        def tp_view(i, qt):
            return TP[i][:, 0:(qt + 1) * P].rearrange("p (k n) -> p k n", n=P)

        def pair_ends(n, j):
            return j + 1 == len(n) or n[j + 1][0] != n[j][0]

        s_const, s_init = sems("s_const", "s_init")
        s_w = sems("s_w0", "s_w1")
        s_whi, s_wlo = sems("s_whi", "s_wlo")
        s_wused = sem("s_wused")
        s_gfree = sem("s_gfree")
        s_par = sem("s_par")
        s_sq, s_sqadd = sems("s_sq", "s_sqadd")
        s_ms, s_rms, s_rs = sems("s_ms", "s_rms", "s_rs")
        s_xhi, s_xlo = sems("s_xhi", "s_xlo")
        s_rot, s_roped = sems("s_rot", "s_roped")
        s_rhi, s_rlo, s_kl = sems("s_rhi", "s_rlo", "s_kl")
        s_vz, s_vhi, s_vlo = sems("s_vz", "s_vhi", "s_vlo")
        s_cc, s_tb, s_tbhi, s_tblo = sems("s_cc", "s_tb", "s_tbhi", "s_tblo")
        s_tg, s_gt = sems("s_tg", "s_gt")
        s_pe1, s_swap, s_kpe = sems("s_pe1", "s_swap", "s_kpe")
        s_csq, s_csum, s_cms, s_crms = sems("s_csq", "s_csum", "s_cms", "s_crms")
        s_cf, s_chi, s_clo = sems("s_cf", "s_chi", "s_clo")
        s_ty = sem("s_ty")
        s_gst = sems("s_gst0", "s_gst1")
        s_gld = sems("s_gld0", "s_gld1")
        s_ht, s_hs, s_hT, s_hThi, s_hTlo = sems("s_ht", "s_hs", "s_hT", "s_hThi", "s_hTlo")
        s_kchi, s_kclo = sems("s_kchi", "s_kclo")
        s_cs, s_cmax, s_cexp, s_cw = sems("s_cs", "s_cmax", "s_cexp", "s_cw")
        s_cT, s_cThi, s_cTlo = sems("s_cT", "s_cThi", "s_cTlo")
        s_scores, s_max, s_exp, s_scl = sems("s_scores", "s_max", "s_exp", "s_scl")
        s_trans, s_phi, s_plo = sems("s_trans", "s_phi", "s_plo")
        s_pv = sem("s_pv")
        s_ohi, s_olo = sems("s_ohi", "s_olo")
        s_mready, s_mhi, s_mlo = sems("s_mready", "s_mhi", "s_mlo")
        s_mab, s_mg, s_mghi, s_mglo = sems("s_mab", "s_mg", "s_mghi", "s_mglo")
        s_hsq, s_hhi, s_hlo = sems("s_hsq", "s_hhi", "s_hlo")
        s_fin, s_out = sems("s_fin", "s_out")
        s_stand = sem("s_stand")
        s_dvec = sem("s_dvec")

        block = ctx.enter_context(nc.Block())

        @block.sync
        def _(sp):
            sp.dma_start(stage[:, 0, :], units[0]).then_inc(s_w[0], 16)
            sp.dma_start(stage[:, 1, :], units[1]).then_inc(s_w[1], 16)
            with sp.Fori(1, L * NU // 2 + 1) as i:
                for s in range(2):
                    sp.wait_ge(s_wlo, i * 2 + (s - 1))
                    sp.dma_start(stage[:, s, :], units[bass.ds(i * 2 + s, 1)].rearrange("o p n -> (o p) n"))\
                        .then_inc(s_w[s], 16)
            for m in range(KT):
                sp.wait_ge(s_fin, m + 1)
                sp.dma_start(out[m], final[m]).then_inc(s_out, 16)
            sp.wait_ge(s_w[0], 16 * (L * NU // 2 + 1))
            sp.wait_ge(s_w[1], 16 * (L * NU // 2 + 1))
            sp.wait_ge(s_out, 16 * KT)

        @block.gpsimd
        def _(pool):
            pool.dma_start(x[:, :, :], x_in).then_inc(s_const, 16)
            pool.dma_start(par_all[:, :], params).then_inc(s_const, 16)
            pool.dma_start(rope[:, :, :], tables).then_inc(s_const, 16)
            pool.dma_start(constf[:, :, :], cf32).then_inc(s_const, 16)
            pool.dma_start(F[:, 4, 0:3 * P].rearrange("p (c n) -> p c n", c=3), cmasks).then_inc(s_const, 16)
            pool.memset(ones[:, :], 1.0).then_inc(s_init, 1)
            pool.memset(vblk[:, :, :, :].bitcast(F32), 0.0).then_inc(s_init, 1)
            pool.wait_ge(s_const, 80)
            with pool.Fori(0, L) as l:
                pool.wait_ge(s_par, l + 1)
                pool.sem_inc(s_stand, 1)
                for c in range(2):
                    for br in range(2):
                        zeros = VN[:, c, br, :, :].rearrange("p t (z n) -> p t z n", n=HD)
                        ins = pool.memset(zeros[:, :, 0:5:2, :].bitcast(F32), 0.0)
                ins.then_inc(s_vz, 1)
                for r, g in enumerate(ROPE_TILES):
                    pool.wait_ge(s_gfree, l * NG + (g + 1 + GFREE0))
                    if r >= 2:
                        pool.wait_ge(s_roped, l * 7 + (r - 1))
                    if r == 0:
                        pool.wait_ge(s_vz, l * 2 + 1)
                    elif ROPE_TILES[r - 1] in (G_KS, G_KW):
                        pool.wait_ge(s_kl, l * 2 + (ROPE_TILES[r - 1] - G_KS + 1))
                    for q in range(4):
                        o = q ^ 1
                        ins = pool.tensor_tensor(F[32 * q:32 * q + 32, r % 2, :], Y[32 * o:32 * o + 32, g % 2, :],
                                                 sinN[32 * o:32 * o + 32, :], ALU.mult)
                    ins.then_inc(s_rot, 1)
                    if g in (G_KS, G_KW):
                        br = g - G_KS
                        pool.wait_ge(s_rot, l * 7 + (r + 1))
                        pool.wait_ge(s_rhi, l * 6 + (r + 1))
                        for gr in range(2):
                            src = F[64 * gr:64 * gr + 64, 3 + r % 2, :]
                            for half in range(2):
                                ins = pool.tensor_tensor(KN[64 * half:64 * half + 64, br, gr, 1, :], src,
                                                         KN[64 * gr:64 * gr + 64, br, gr, 0, :], ALU.subtract)
                        ins.then_inc(s_kl, 1)
                for i in range(2 * KT):
                    pool.wait_ge(s_ty, l * 16 + (i + 1))
                    pool.sem_inc(s_stand, 1)
                    pool.dma_start(gates_dram[i], Y[:, i % 2, :]).then_inc(s_gst[i % 2], 16)
                pool.wait_ge(s_rot, l * 7 + 7)
                pool.wait_ge(s_pv, l * NHP + NSA_PASSES)
                pool.sem_inc(s_stand, 1)
                for s in range(2):
                    for c in range(2):
                        ins = pool.memset(MV[:, s, c, :, HD:2 * HD].bitcast(F32), 0.0)
                ins.then_inc(s_vz, 1)
                pool.wait_ge(s_gst[0], l * 128 + 128)
                pool.wait_ge(s_gst[1], l * 128 + 128)
                for m in range(KT):
                    if m < 2:
                        pool.wait_ge(s_plo, l * NJ + NJ)
                    else:
                        pool.wait_ge(s_mab, l * KT + (m - 1))
                    pool.sem_inc(s_stand, 1)
                    pool.dma_start(F[:, m % 2, :], gates_dram[m]).then_inc(s_gld[m % 2], 16)
                    pool.dma_start(F[:, 2 + m % 2, :], gates_dram[KT + m]).then_inc(s_gld[m % 2], 16)
                with pool.Fori(0, QUARTERS) as f:
                    for m in range(KT):
                        pool.wait_ge(s_gfree, l * NG + f * U_QUARTER + (G_MLP + m + 1 + GFREE0))
                        if m >= 2:
                            pool.wait_ge(s_hlo, l * (QUARTERS * KT) + f * KT + (m - 1))
                        pool.tensor_tensor(F[:, m % 2, :], Y[:, m % 2, :], Y[:, m % 2, :], ALU.mult)\
                            .then_inc(s_hsq, 1)

        @block.scalar
        def _(act):
            def split_hi(half, u):
                s = u % 2
                act.wait_ge(s_w[s], half * 16 + (u // 2 + 1) * 16)
                act.wait_ge(s_wused, half * 2 + (u + 1))
                act.activation(wsplit[:, s, 0, :], stage[:, s, :], ACT.Copy).then_inc(s_whi, 1)

            def squares(n, x_ready, gains):
                for m in range(KT):
                    act.wait_ge(s_gfree, x_ready + m)
                    if m >= 2:
                        act.wait_ge(s_sqadd, n * KT + (m - 1))
                    act.activation(F[:, m % 2, :], x[:, m, :], ACT.Square).then_inc(s_sq, 1)
                    if gains is not None:
                        act.activation(xg[:, 0, m, :], x[:, m, :], ACT.Copy, scale=par[:, gains + m:gains + m + 1])\
                            .then_inc(s_xhi, 1)

            def root(n, columns):
                act.wait_ge(s_ms, n + 1)
                if columns:
                    act.activation(rc[:, 2, :], TP[0][:, 0:QT], ACT.Sqrt, scale=1.0 / D, bias=eps)
                act.activation(F[:, 3, :], SB[0][:, :], ACT.Sqrt, scale=1.0 / D, bias=eps).then_inc(s_rms, 1)

            def jobs(l, job0, n, start_pair, hook):
                for i in range(len(n) + LAG_OLO + 1):
                    if i < len(n):
                        hook(i)
                        w = (n[i][3] + 1) * P
                        act.wait_ge(s_max, l * NJ + (job0 + i + 1))
                        act.activation(F[:, i % 3, 0:w], SB[i % 2][:, 0:w], ACT.Exp, bias=nmx[:, i % 4:i % 4 + 1],
                                       accum_out=sums[:, i % 4:i % 4 + 1]).then_inc(s_exp, 1)
                    j = i - LAG_T
                    if 0 <= j < len(n):
                        hp = (job0 + j) // QT
                        act.wait_ge(s_trans, l * NJ + (job0 + j + 1))
                        if hp >= 2:
                            act.wait_ge(s_pv, l * NHP + (hp - 1))
                        act.activation(pt_view(hp % 2, 0, n[j][3]), tp_view(j % 2, n[j][3]), ACT.Copy)\
                            .then_inc(s_phi, 1)
                    j = i - LAG_OHI
                    if 0 <= j < len(n) and pair_ends(n, j):
                        pc = start_pair + n[j][0]
                        act.wait_ge(s_pv, l * NHP + ((job0 + j) // QT + 1))
                        act.activation(xg[:, 0, pc, :], O[pc % 2][:, :], ACT.Copy).then_inc(s_ohi, 1)

            def mla_proj(l, p):
                s, g, hi0 = p % 2, G_MLA + 4 * p, 4 * p + 1
                split_hi(l * (NU // 2), U_MLA + p + 1)
                if p >= 2:
                    act.wait_ge(s_pv, l * NHP + (NSA_PASSES + 2 * (p - 1)))
                for e in range(2):
                    act.wait_ge(s_gfree, l * NG + (g + e + 1 + GFREE0))
                    act.activation(MQ[:, s, e, 0, :], Y[:, e, :], ACT.Copy, scale=MLA_SCALE).then_inc(s_mhi, 1)
                act.wait_ge(s_mready, l * 12 + (3 * p + 3))
                for e in range(2):
                    ins = act.activation(MK[0:64, s, e, 0, :], G[0][64 * e:64 * e + 64, :], ACT.Copy)
                ins.then_inc(s_mhi, 1)
                act.wait_ge(s_wused, l * NU + (U_MLA + p + 1 + WUSED0))
                src = G[1][:, :].rearrange("p (t e n) -> p t e n", t=QT, e=2)
                dst = MV[:, s, 0, :, :].rearrange("p t (z n) -> p t z n", n=HD)
                act.activation(dst[:, :, 0:3:2, :], src, ACT.Copy).then_inc(s_mhi, 1)

            def gate_tanh(l, i):
                act.wait_ge(s_gfree, l * NG + (G_GATE + i + 1 + GFREE0))
                act.activation(Y[:, i % 2, :], Y[:, i % 2, :], ACT.Tanh, scale=0.5).then_inc(s_ty, 1)

            act.wait_ge(s_const, 80)
            act.wait_ge(s_init, 4)
            split_hi(0, 0)
            with act.Fori(0, L) as l:
                half = l * (NU // 2)

                def ahead(u):
                    split_hi(half, u + 1)

                act.wait_ge(s_par, l + 1)
                squares(l * 2, l * NG + (GFREE0 - KT + 1), PR_ATTN)
                ahead(0)
                root(l * 2, True)
                for r in range(4):
                    if r > 0:
                        ahead(r)
                    act.wait_ge(s_roped, l * 7 + (r + 1))
                    q = F[:, 3 + r % 2, :]
                    act.activation(QS[0:64, 2 * r, :], q[0:64], ACT.Copy, scale=NSA_SCALE)
                    act.activation(QS[64:128, 2 * r + 1, :], q[64:128], ACT.Copy, scale=NSA_SCALE).then_inc(s_rhi, 1)
                for br in range(2):
                    ahead(U_KS + br)
                    act.wait_ge(s_roped, l * 7 + (5 + br))
                    for gr in range(2):
                        k = F[64 * gr:64 * gr + 64, 3 + br, :]
                        for hf in range(2):
                            ins = act.activation(KN[64 * hf:64 * hf + 64, br, gr, 0, :], k, ACT.Copy)
                    ins.then_inc(s_rhi, 1)
                ahead(U_V)
                ahead(U_V + 1)
                act.wait_ge(s_rs, l * 2 + 1)
                act.wait_ge(s_wused, l * NU + (U_V + 2 + WUSED0))
                for tt in range(QT):
                    src = SB[tt // 2][:, 256 * (tt % 2):256 * (tt % 2) + 256].rearrange("p (b g n) -> p b g n", b=2, g=2)
                    for br in range(2):
                        dst = VN[:, 0, br, tt, :].rearrange("p (z n) -> p z n", n=HD)
                        ins = act.activation(dst[:, 1:4:2, :], src[:, br], ACT.Copy, scale=rc[:, 0, tt:tt + 1])
                ins.then_inc(s_vhi, 1)
                for kind in range(2):
                    if kind == 0:
                        ahead(U_KC)
                        act.wait_ge(s_roped, l * 7 + 7)
                        src = F[:, 3, :]
                    else:
                        act.wait_ge(s_gfree, l * NG + (G_VC + 1 + GFREE0))
                        act.wait_ge(s_tb, l * 2 + 1)
                        src = Y[:, 1, :]
                    for gr in range(2):
                        act.activation(F[0:64, 5 + gr, :], src[64 * gr:64 * gr + 64, :], ACT.Copy)
                        ins = act.activation(F[64:128, 5 + gr, 0:S - 1], src[64 * gr:64 * gr + 64, 1:S], ACT.Copy)
                    ins.then_inc(s_cc, 1)
                    if kind == 0:
                        ahead(U_VC)
                    act.wait_ge(s_tb, l * 2 + (kind + 1))
                    act.activation(TB[:, kind, 0, :, :].rearrange("p j n -> p (j n)"), tbf, ACT.Copy)\
                        .then_inc(s_tbhi, 1)
                ahead(U_MISC)
                act.wait_ge(s_wused, l * NU + (U_MISC + 1 + WUSED0))
                for tt in range(QT):
                    ins = act.activation(gt[:, tt, :], TP[1][:, 24 * tt:24 * tt + 24], ACT.Tanh,
                                         scale=rc[:, 1, tt:tt + 1])
                ins.then_inc(s_tg, 1)
                act.wait_ge(s_pe1, l + 1)
                act.activation(F[64:96, 4, :], kpe[96:128, :], ACT.Copy)
                act.activation(F[96:128, 4, :], kpe[64:96, :], ACT.Copy).then_inc(s_swap, 1)
                ahead(U_CQ)
                ahead(U_CQ + 1)
                ahead(U_CKV)
                for i in range(2 * KT):
                    ahead(U_GATE + i)
                    if i == 1:
                        act.wait_ge(s_gfree, l * NG + (G_CKV + 1 + GFREE0))
                        act.wait_ge(s_tblo, l * 2 + 2)
                        for c in range(3):
                            act.activation(F[:, 3 + c, :], F[:, c, :], ACT.Square).then_inc(s_csq, 1)
                    if i == 3:
                        act.wait_ge(s_cms, l + 1)
                        act.activation(F[:, 6, :], SB[0][:, :], ACT.Sqrt, scale=1.0 / 256, bias=eps)
                        act.activation(F[:, 7, :], SB[1][:, :], ACT.Sqrt, scale=1.0 / 128, bias=eps)\
                            .then_inc(s_crms, 1)
                    gate_tanh(l, i)
                    if i == 9:
                        for c in range(3):
                            act.wait_ge(s_cf, l * 3 + (c + 1))
                            act.activation(cn[:, 0, c, :], F[:, 3 + c, :], ACT.Copy).then_inc(s_chi, 1)
                for kind in range(2):
                    for i in range(4):
                        ahead(U_W1 + 4 * kind + i)
                    act.wait_ge(s_wused, l * NU + (U_W1 + 4 * kind + 4 + WUSED0))
                    act.activation(F[0:64, kind, 0:256], O[kind][0:64, 0:256], ACT.Tanh, scale=0.5).then_inc(s_ht, 1)
                    act.wait_ge(s_hT, l * 2 + (kind + 1))
                    hT = TP[kind][:, 0:128]
                    if kind == 0:
                        act.activation(HK[:, 0, :, :].rearrange("p j n -> p (j n)"), hT, ACT.Copy, scale=0.5)\
                            .then_inc(s_hThi, 1)
                    else:
                        dst = HV[:, 0, :, :, :].rearrange("p j g (r n) -> p (j g) r n", n=NC)
                        src = hT.rearrange("p (a n) -> p a n", n=NC).unsqueeze(2).broadcast_to([P, 4, 4, NC])
                        act.activation(dst, src, ACT.Copy, scale=0.5).then_inc(s_hThi, 1)
                ahead(U_W2K)
                act.wait_ge(s_wused, l * NU + (U_W2K + 1 + WUSED0))
                act.activation(kcmp[:, 0, :], SB[0][:, 0:64], ACT.Copy).then_inc(s_kchi, 1)
                ahead(U_W2V)
                act.wait_ge(s_wused, l * NU + (U_W2V + 1 + WUSED0))
                for gr in range(2):
                    for b in range(4):
                        ins = act.activation(vblk[32 * b:32 * b + 32, 0, 2 * gr + b // 2, 64 * (b % 2):64 * (b % 2) + 64],
                                             SB[1][32 * b:32 * b + 32, 64 * gr:64 * gr + 64], ACT.Copy)
                ins.then_inc(s_kchi, 1)
                for i in range(2):
                    act.wait_ge(s_cmax, l * 2 + (i + 1))
                    act.activation(F[:, 6 + i, :], F[:, 4 + i, :], ACT.Exp).then_inc(s_cexp, 1)
                for gr in range(2):
                    act.wait_ge(s_cT, l * 2 + (gr + 1))
                    act.activation(pcT[:, gr, 0, :], TP[gr][:, :], ACT.Copy).then_inc(s_cThi, 1)
                jobs(l, 0, NSA_JOBS, 0, lambda i: None)
                for s in range(2):
                    for e in range(2):
                        ins = act.activation(MK[64:128, s, e, 0, :], kpe[64:128, :], ACT.Copy)
                ins.then_inc(s_mhi, 1)
                mla_proj(l, 0)
                jobs(l, len(NSA_JOBS), MLA_JOBS, PAIRS,
                     lambda i: mla_proj(l, i // 8 + 1) if i % 8 == 5 and i < 24 else None)
                for m in range(KT):
                    ahead(U_WO + m)
                    act.wait_ge(s_mg, l * KT + (m + 1))
                    act.activation(H[:, 0, m, :], F[:, 6 + m % 2, :], ACT.Copy, scale=0.5).then_inc(s_mghi, 1)
                for m in range(KT):
                    ahead(U_OUT + m)
                squares(l * 2 + 1, l * NG + (G_OUT + 1 + GFREE0), PR_MLP)
                root(l * 2 + 1, False)
                with act.Fori(0, QUARTERS) as f:
                    half_f = l * (NU // 2) + f * KT
                    for m in range(2 * KT):
                        split_hi(half_f, U_MLP + m + 1)
                        if m < KT:
                            act.wait_ge(s_gfree, l * NG + f * U_QUARTER + (G_MLP + m + 1 + GFREE0))
                            act.activation(H[:, 0, m, :], Y[:, m % 2, :], ACT.Square).then_inc(s_hhi, 1)
            squares(L * 2, L * NG + (GFREE0 - KT + 1), None)
            root(L * 2, False)

        @block.vector
        def _(dve):
            chain = Chain(dve, s_dvec)

            def split_lo(half, u):
                s = u % 2
                dve.wait_ge(s_whi, half * 2 + (u + 1))
                dve.tensor_tensor(wsplit[:, s, 1, :], stage[:, s, :], wsplit[:, s, 0, :], ALU.subtract)\
                    .then_inc(s_wlo, 1)

            def rest(out_ap, full, scale, hi):
                return dve.scalar_tensor_tensor(out_ap, full, scale, hi, ALU.mult, ALU.subtract)

            def norm_sum(n, gains):
                for m in range(KT):
                    dve.wait_ge(s_sq, n * KT + (m + 1))
                    if m == 0:
                        dve.tensor_copy(F[:, 2, :], F[:, 0, :]).then_inc(s_sqadd, 1)
                    else:
                        dve.wait_ge(s_sqadd, n * KT + m)
                        dve.tensor_tensor(F[:, 2, :], F[:, 2, :], F[:, m % 2, :], ALU.add).then_inc(s_sqadd, 1)
                    if gains is not None:
                        dve.wait_ge(s_xhi, n * KT + (m + 1))
                        rest(xg[:, 1, m, :], x[:, m, :], par[:, gains + m:gains + m + 1], xg[:, 0, m, :])\
                            .then_inc(s_xlo, 1)

            def norm_end(n, columns):
                dve.wait_ge(s_rms, n + 1)
                if columns:
                    chain.mark(dve.reciprocal(rc[:, 0, :], rc[:, 2, :]))
                    chain.wait()
                    dve.tensor_scalar(rc[:, 1, :], rc[:, 0, :], 0.5, None, ALU.mult)
                dve.reciprocal(rs[:, :], F[:, 3, :]).then_inc(s_rs, 1)
                dve.wait_ge(s_const, 80)
                dve.wait_ge(s_rs, n + 1)

            def jobs(l, job0, n, start_pair, gated, hook):
                for i in range(len(n) + LAG_OLO + 1):
                    if i < len(n):
                        hook(i)
                        w = (n[i][3] + 1) * P
                        dve.wait_ge(s_scores, l * NJ + (job0 + i + 1))
                        dve.tensor_reduce(nmx[:, i % 4:i % 4 + 1], SB[i % 2][:, 0:w], AX.X, ALU.max, negate=True)\
                            .then_inc(s_max, 1)
                    j = i - LAG_SCALE
                    if 0 <= j < len(n):
                        t, e, br, qt = n[j]
                        w = (qt + 1) * P
                        dve.wait_ge(s_exp, l * NJ + (job0 + j + 1))
                        chain.mark(dve.reciprocal(rsum[:, j % 4:j % 4 + 1], sums[:, j % 4:j % 4 + 1]))
                        chain.wait()
                        col = (1 + br) * HEADS + 2 * t + e
                        dve.tensor_scalar(F[:, j % 3, 0:w], F[:, j % 3, 0:w], rsum[:, j % 4:j % 4 + 1],
                                          gt[:, qt, col:col + 1] if gated else None,
                                          ALU.mult, ALU.mult if gated else ALU.bypass).then_inc(s_scl, 1)
                    j = i - LAG_LO
                    if 0 <= j < len(n):
                        hp = (job0 + j) // QT
                        dve.wait_ge(s_phi, l * NJ + (job0 + j + 1))
                        dve.tensor_tensor(pt_view(hp % 2, 1, n[j][3]), tp_view(j % 2, n[j][3]),
                                          pt_view(hp % 2, 0, n[j][3]), ALU.subtract).then_inc(s_plo, 1)
                    j = i - LAG_OLO
                    if 0 <= j < len(n) and pair_ends(n, j):
                        pc = start_pair + n[j][0]
                        dve.wait_ge(s_ohi, l * 8 + (pc + 1))
                        dve.tensor_tensor(xg[:, 1, pc, :], O[pc % 2][:, :], xg[:, 0, pc, :], ALU.subtract)\
                            .then_inc(s_olo, 1)

            def mla_proj(l, p):
                s, g, hi0 = p % 2, G_MLA + 4 * p, 4 * p + 1
                split_lo(l * (NU // 2), U_MLA + p + 1)
                for e in range(2):
                    dve.wait_ge(s_mready, l * 12 + (3 * p + e + 1))
                    dve.tensor_tensor(Y[:, e, :], G[e][:, :], tabM, ALU.mult).then_inc(s_gfree, 1)
                for e in range(2):
                    dve.wait_ge(s_mhi, l * 17 + (hi0 + e + 1))
                    rest(MQ[:, s, e, 1, :], Y[:, e, :], MLA_SCALE, MQ[:, s, e, 0, :]).then_inc(s_mlo, 1)
                dve.wait_ge(s_mhi, l * 17 + (hi0 + 3))
                for e in range(2):
                    ins = dve.tensor_tensor(MK[0:64, s, e, 1, :], G[0][64 * e:64 * e + 64, :], MK[0:64, s, e, 0, :],
                                            ALU.subtract)
                ins.then_inc(s_gfree, 1)
                dve.wait_ge(s_mhi, l * 17 + (hi0 + 4))
                src = G[1][:, :].rearrange("p (t e n) -> p t e n", t=QT, e=2)
                hi = MV[:, s, 0, :, :].rearrange("p t (z n) -> p t z n", n=HD)
                lo = MV[:, s, 1, :, :].rearrange("p t (z n) -> p t z n", n=HD)
                dve.tensor_tensor(lo[:, :, 0:3:2, :], src, hi[:, :, 0:3:2, :], ALU.subtract).then_inc(s_gfree, 1)

            dve.sem_inc(s_gfree, GFREE0)
            dve.memset(eps, EPS).then_inc(s_init, 1)
            dve.wait_ge(s_const, 80)
            dve.tensor_copy(constb[:, :, :].rearrange("p c n -> p (c n)"), F[:, 4, 0:3 * P]).then_inc(s_init, 1)
            split_lo(0, 0)
            with dve.Fori(0, L) as l:
                half = l * (NU // 2)

                def ahead(u):
                    split_lo(half, u + 1)

                def evac(g, u, dst):
                    dve.wait_ge(s_wused, l * NU + (u + 1 + WUSED0))
                    dve.tensor_tensor(dst, G[g % 2][:, :], rs[:, :], ALU.mult).then_inc(s_gfree, 1)

                def own(g):
                    dve.wait_ge(s_gfree, l * NG + (g + 1 + GFREE0))

                def q_lo(r):
                    dve.wait_ge(s_rhi, l * 6 + (r + 1))
                    q = F[:, 3 + r % 2, :]
                    rest(QS[64:128, 2 * r, :], q[0:64], NSA_SCALE, QS[0:64, 2 * r, :])
                    rest(QS[0:64, 2 * r + 1, :], q[64:128], NSA_SCALE, QS[64:128, 2 * r + 1, :]).then_inc(s_rlo, 1)

                def rotate(r, g, u, between=None):
                    evac(g, u, Y[:, g % 2, :])
                    own(g)
                    chain.mark(dve.tensor_tensor(F[:, 2, :], Y[:, g % 2, :], cosN, ALU.mult))
                    if between is not None:
                        between()
                    dve.wait_ge(s_rot, l * 7 + (r + 1))
                    chain.wait()
                    dve.tensor_tensor(F[:, 3 + r % 2, :], F[:, 2, :], F[:, r % 2, :], ALU.add).then_inc(s_roped, 1)

                chain.restart()
                dve.tensor_copy(par[:, :], par_all[:, bass.ds(l * NPAR, NPAR)]).then_inc(s_par, 1)
                dve.wait_ge(s_par, l + 1)
                norm_sum(l * 2, PR_ATTN)
                ahead(0)
                norm_end(l * 2, True)
                for r in range(4):
                    if r > 0:
                        ahead(r)
                    rotate(r, r, r, (lambda: q_lo(r - 1)) if r else None)
                for br in range(2):
                    ahead(U_KS + br)
                    rotate(4 + br, G_KS + br, U_KS + br, (lambda: q_lo(3)) if br == 0 else None)
                ahead(U_V)
                ahead(U_V + 1)
                dve.wait_ge(s_vhi, l + 1)
                for tt in range(QT):
                    src = SB[tt // 2][:, 256 * (tt % 2):256 * (tt % 2) + 256].rearrange("p (b g n) -> p b g n", b=2, g=2)
                    for br in range(2):
                        hi = VN[:, 0, br, tt, :].rearrange("p (z n) -> p z n", n=HD)[:, 1:4:2, :]
                        lo = VN[:, 1, br, tt, :].rearrange("p (z n) -> p z n", n=HD)[:, 1:4:2, :]
                        ins = rest(lo, src[:, br], rc[:, 0, tt:tt + 1], hi)
                ins.then_inc(s_vlo, 1)
                ahead(U_KC)
                rotate(6, G_KC, U_KC, lambda: dve.wait_ge(s_kl, l * 2 + 1))
                for kind in range(2):
                    dve.wait_ge(s_cc, l * 2 + (kind + 1))
                    if kind == 1:
                        dve.wait_ge(s_tblo, l * 2 + 1)
                    tb = tbf.rearrange("p (j g n) -> p j g n", j=16, g=2)
                    dve.memset(tb[:, :, :, N_CMP:NC], 0.0)
                    tok = F[:, 5:7, :].rearrange("p g (n r) -> p r g n", r=16)[:, 0:16:2]
                    for hf in range(2):
                        pe = par[:, PR_PE + 16 * kind + 8 * hf:PR_PE + 16 * kind + 8 * hf + 8]
                        pe = pe.unsqueeze(2).unsqueeze(3).broadcast_to([P, 8, 2, N_CMP])
                        ins = dve.tensor_tensor(tb[:, 8 * hf:8 * hf + 8, :, 0:N_CMP], tok[:, :, :, hf:hf + N_CMP], pe,
                                                ALU.add)
                    ins.then_inc(s_tb, 1)
                    if kind == 0:
                        ahead(U_VC)
                    dve.wait_ge(s_tbhi, l * 2 + (kind + 1))
                    dve.tensor_tensor(TB[:, kind, 1, :, :].rearrange("p j n -> p (j n)"), tbf,
                                      TB[:, kind, 0, :, :].rearrange("p j n -> p (j n)"), ALU.subtract)\
                        .then_inc(s_tblo, 1)
                    if kind == 0:
                        evac(G_VC, U_VC, Y[:, 1, :])
                ahead(U_MISC)
                evac(G_MISC, U_MISC, Y[:, 0, :])
                own(G_MISC)
                dve.tensor_tensor(kpe[64:128, :], Y[64:128, 0, :], tabM[64:128, :], ALU.mult).then_inc(s_pe1, 1)
                dve.wait_ge(s_tg, l + 1)
                dve.tensor_scalar(gt[:, :, :], gt[:, :, :], 0.5, 0.5, ALU.mult, ALU.add).then_inc(s_gt, 1)
                dve.wait_ge(s_swap, l + 1)
                dve.tensor_tensor(kpe[64:128, :], kpe[64:128, :], F[64:128, 4, :], ALU.add).then_inc(s_kpe, 1)
                for c in range(3):
                    ahead(U_CQ + c)
                    evac(G_CQ + c, U_CQ + c, F[:, c, :])
                for i in range(2 * KT):
                    ahead(U_GATE + i)
                    if i >= 2:
                        dve.wait_ge(s_gst[i % 2], l * 128 + 16 * (i // 2))
                    evac(G_GATE + i, U_GATE + i, Y[:, i % 2, :])
                    if i == 1:
                        dve.wait_ge(s_csq, l * 3 + 2)
                        dve.tensor_tensor(F[:, 3, :], F[:, 3, :], F[:, 4, :], ALU.add).then_inc(s_csum, 1)
                    if i == 4:
                        dve.wait_ge(s_crms, l + 1)
                        chain.mark(dve.reciprocal(F[:, 6, :], F[:, 6, :]))
                    if i == 6:
                        chain.mark(dve.reciprocal(F[:, 7, :], F[:, 7, :]))
                    if i == 8:
                        chain.wait()
                        for c in range(3):
                            gain = par[:, PR_QN + c:PR_QN + c + 1]
                            dve.scalar_tensor_tensor(F[:, 3 + c, :], F[:, c, :], gain, F[:, 6 + c // 2, :],
                                                     ALU.mult, ALU.mult).then_inc(s_cf, 1)
                    if i == 10:
                        for c in range(3):
                            dve.wait_ge(s_chi, l * 3 + (c + 1))
                            dve.tensor_tensor(cn[:, 1, c, :], F[:, 3 + c, :], cn[:, 0, c, :], ALU.subtract)\
                                .then_inc(s_clo, 1)
                for kind in range(2):
                    for i in range(4):
                        ahead(U_W1 + 4 * kind + i)
                    dve.wait_ge(s_ht, l * 2 + (kind + 1))
                    dve.scalar_tensor_tensor(F[0:64, 2 + kind, 0:256], F[0:64, kind, 0:256], 1.0, O[kind][0:64, 0:256],
                                             ALU.add, ALU.mult).then_inc(s_hs, 1)
                    dve.wait_ge(s_hThi, l * 2 + (kind + 1))
                    hT = TP[kind][:, 0:128]
                    if kind == 0:
                        rest(HK[:, 1, :, :].rearrange("p j n -> p (j n)"), hT, 0.5,
                             HK[:, 0, :, :].rearrange("p j n -> p (j n)")).then_inc(s_hTlo, 1)
                    else:
                        hi = HV[:, 0, :, :, :].rearrange("p j g (r n) -> p (j g) r n", n=NC)
                        lo = HV[:, 1, :, :, :].rearrange("p j g (r n) -> p (j g) r n", n=NC)
                        for r in range(4):
                            ins = rest(lo[:, :, r, :], hT.rearrange("p (a n) -> p a n", n=NC), 0.5, hi[:, :, r, :])
                        ins.then_inc(s_hTlo, 1)
                ahead(U_W2K)
                dve.wait_ge(s_kchi, l * 2 + 1)
                dve.tensor_tensor(kcmp[:, 1, :], SB[0][:, 0:64], kcmp[:, 0, :], ALU.subtract).then_inc(s_kclo, 1)
                ahead(U_W2V)
                dve.wait_ge(s_kchi, l * 2 + 2)
                for gr in range(2):
                    for b in range(4):
                        rows, cols = slice(32 * b, 32 * b + 32), slice(64 * (b % 2), 64 * (b % 2) + 64)
                        ins = dve.tensor_tensor(vblk[rows, 1, 2 * gr + b // 2, cols], SB[1][rows, 64 * gr:64 * gr + 64],
                                                vblk[rows, 0, 2 * gr + b // 2, cols], ALU.subtract)
                ins.then_inc(s_kclo, 1)
                for i in range(2):
                    dve.wait_ge(s_cs, l * 2 + (i + 1))
                    sc = O[i][:, :].rearrange("p (a n) -> p a n", n=NC)
                    chain.mark(dve.tensor_reduce(small[:, i, 0:16], sc, AX.X, ALU.max, negate=True))
                    chain.wait()
                    dve.tensor_tensor(F[:, 4 + i, :].rearrange("p (a n) -> p a n", n=NC), sc,
                                      small[:, i, 0:16].unsqueeze(2).broadcast_to([P, 16, NC]), ALU.add).then_inc(s_cmax, 1)
                dve.wait_ge(s_gt, l + 1)
                for i in range(2):
                    dve.wait_ge(s_cexp, l * 2 + (i + 1))
                    e4 = F[:, 6 + i, :].rearrange("p (q h n) -> p q h n", q=2, h=HEADS)
                    e3 = F[:, 6 + i, :].rearrange("p (a n) -> p a n", n=NC)
                    m4 = mask01[:, 2 * i:2 * i + 2, :].unsqueeze(2).broadcast_to([P, 2, HEADS, NC])
                    tot = small[:, 2 + i, 0:16]
                    chain.mark(dve.tensor_tensor(e4, e4, m4, ALU.mult))
                    chain.wait()
                    chain.mark(dve.tensor_reduce(tot, e3, AX.X, ALU.add))
                    chain.wait()
                    chain.mark(dve.tensor_scalar(tot, tot, TINY, None, ALU.max))
                    chain.wait()
                    chain.mark(dve.reciprocal(tot, tot))
                    chain.wait()
                    chain.mark(dve.tensor_tensor(tot.rearrange("p (q h) -> p q h", q=2),
                                                 tot.rearrange("p (q h) -> p q h", q=2),
                                                 gt[:, 2 * i:2 * i + 2, 0:HEADS], ALU.mult))
                    chain.wait()
                    dve.tensor_tensor(e3, e3, tot.unsqueeze(2).broadcast_to([P, 16, NC]), ALU.mult).then_inc(s_cw, 1)
                for gr in range(2):
                    dve.wait_ge(s_cThi, l * 2 + (gr + 1))
                    dve.tensor_tensor(pcT[:, gr, 1, :], TP[gr][:, :], pcT[:, gr, 0, :], ALU.subtract).then_inc(s_cTlo, 1)
                jobs(l, 0, NSA_JOBS, 0, True, lambda i: None)
                dve.wait_ge(s_mhi, l * 17 + 1)
                for s in range(2):
                    for e in range(2):
                        ins = dve.tensor_tensor(MK[64:128, s, e, 1, :], kpe[64:128, :], MK[64:128, s, e, 0, :],
                                                ALU.subtract)
                ins.then_inc(s_mlo, 1)
                dve.wait_ge(s_gst[0], l * 128 + 128)
                dve.wait_ge(s_gst[1], l * 128 + 128)
                mla_proj(l, 0)
                jobs(l, len(NSA_JOBS), MLA_JOBS, PAIRS, False,
                     lambda i: mla_proj(l, i // 8 + 1) if i % 8 == 5 and i < 24 else None)

                def merged_lo(m):
                    dve.wait_ge(s_mghi, l * KT + (m + 1))
                    rest(H[:, 1, m, :], F[:, 6 + m % 2, :], 0.5, H[:, 0, m, :]).then_inc(s_mglo, 1)

                for m in range(KT):
                    ahead(U_WO + m)
                    dve.wait_ge(s_wused, l * NU + (U_WO + m + 1 + WUSED0))
                    dve.wait_ge(s_gld[m % 2], l * 128 + 32 * (m // 2 + 1))
                    dve.scalar_tensor_tensor(F[:, 4 + m % 2, :], F[:, m % 2, :], 1.0, SB[m % 2][:, :], ALU.add, ALU.mult)
                    dve.scalar_tensor_tensor(F[:, 6 + m % 2, :], F[:, 2 + m % 2, :], 1.0, TP[m % 2][:, :], ALU.add,
                                             ALU.mult).then_inc(s_mab, 1)
                    if m > 0:
                        merged_lo(m - 1)
                    dve.wait_ge(s_mab, l * KT + (m + 1))
                    dve.tensor_tensor(F[:, 6 + m % 2, :], F[:, 6 + m % 2, :], F[:, 4 + m % 2, :], ALU.add)\
                        .then_inc(s_mg, 1)
                merged_lo(KT - 1)
                for m in range(KT):
                    ahead(U_OUT + m)
                    dve.wait_ge(s_wused, l * NU + (U_OUT + m + 1 + WUSED0))
                    dve.tensor_tensor(x[:, m, :], x[:, m, :], G[(G_OUT + m) % 2][:, :], ALU.add).then_inc(s_gfree, 1)
                norm_sum(l * 2 + 1, PR_MLP)
                norm_end(l * 2 + 1, False)
                with dve.Fori(0, QUARTERS) as f:
                    half_f = l * (NU // 2) + f * KT
                    for m in range(2 * KT):
                        split_lo(half_f, U_MLP + m + 1)
                        dve.wait_ge(s_wused, half_f * 2 + (U_MLP + m + 1 + WUSED0))
                        if m < KT:
                            dve.scalar_tensor_tensor(Y[:, m % 2, :], G[m % 2][:, :], 0.0, rs[:, :], ALU.max, ALU.mult)\
                                .then_inc(s_gfree, 1)
                        else:
                            k = m - KT
                            dve.tensor_tensor(x[:, k, :], x[:, k, :], G[m % 2][:, :], ALU.add).then_inc(s_gfree, 1)
                        if m < KT:
                            dve.wait_ge(s_hhi, l * (QUARTERS * KT) + f * KT + (m + 1))
                            dve.wait_ge(s_hsq, l * (QUARTERS * KT) + f * KT + (m + 1))
                            dve.tensor_tensor(H[:, 1, m, :], F[:, m % 2, :], H[:, 0, m, :], ALU.subtract)\
                                .then_inc(s_hlo, 1)
            dve.wait_ge(s_gfree, L * NG + GFREE0)
            norm_sum(L * 2, None)
            norm_end(L * 2, False)
            for m in range(KT):
                dve.scalar_tensor_tensor(final[m], x[:, m, :], par_all[:, L * NPAR + m:L * NPAR + m + 1], rs[:, :],
                                         ALU.mult, ALU.mult).then_inc(s_fin, 1)

        @block.tensor
        def _(pe):
            def three(dst, a, b, first, last, check=False):
                pe.matmul(dst, a(0), b(0), start=first, stop=False, skip_group_check=check)
                pe.matmul(dst, a(0), b(1), start=False, stop=False, skip_group_check=check)
                return pe.matmul(dst, a(1), b(0), start=False, stop=last, skip_group_check=check)

            def wtile(u, k, width=P):
                return lambda c: wsplit[:, u % 2, c, k * width:(k + 1) * width]

            def rows(t, k):
                return lambda c: t[:, c, k, :]

            def tile(dst, u, t, first=None):
                for k in range(KT):
                    if first is not None:
                        first(k)
                    ins = three(dst, wtile(u, k), rows(t, k), k == 0, k == KT - 1)
                ins.then_inc(s_wused, 1)

            def mean_square(n, columns):
                pe.wait_ge(s_sqadd, n * KT + KT)
                if columns:
                    for tt in range(QT):
                        pe.matmul(TP[0][:, tt:tt + 1], F[:, 2, tt * P:(tt + 1) * P], ones[:, 0:1], start=True, stop=True)
                pe.matmul(SB[0][:, :], ones[:, :], F[:, 2, :], start=True, stop=True).then_inc(s_ms, 1)

            pe.sem_inc(s_wused, WUSED0)
            pe.wait_ge(s_init, 4)
            pe.wait_ge(s_const, 80)
            with pe.Fori(0, L) as l:
                def unit(u):
                    pe.wait_ge(s_wlo, l * NU + (u + 1))

                def free(g):
                    pe.wait_ge(s_gfree, l * NG + (g + 1 + GFREE0 - 2))

                def project(g, u, first=None):
                    unit(u)
                    free(g)
                    tile(G[g % 2][:, :], u, xg, first)

                project(0, 0, lambda k: pe.wait_ge(s_xlo, l * 16 + (k + 1)))
                mean_square(l * 2, True)
                for g in range(1, 6):
                    project(g, g)
                pe.wait_ge(s_rms, l * 2 + 1)
                for hf in range(2):
                    unit(U_V + hf)
                    for tt in range(QT):
                        dst = SB[tt // 2][:, 256 * (tt % 2):256 * (tt % 2) + 256]
                        for k in range(4):
                            ins = three(dst, lambda c: xg[:, c, 4 * hf + k, tt * P:(tt + 1) * P], wtile(U_V + hf, k, 256),
                                        hf == 0 and k == 0 and tt % 2 == 0, hf == 1 and k == 3, True)
                    ins.then_inc(s_wused, 1)
                project(G_KC, U_KC)
                project(G_VC, U_VC)
                unit(U_MISC)
                for tt in range(QT):
                    for k in range(KT):
                        three(TP[1][:, 24 * tt:24 * tt + 24], lambda c: xg[:, c, k, tt * P:(tt + 1) * P],
                              lambda c: wsplit[:, U_MISC % 2, c, k * P:k * P + 24], k == 0, k == KT - 1)
                project(G_MISC, U_MISC)
                for c in range(3):
                    project(G_CQ + c, U_CQ + c)
                for i in range(2 * KT):
                    project(G_GATE + i, U_GATE + i)
                    if i == 2:
                        pe.wait_ge(s_csum, l + 1)
                        pe.wait_ge(s_csq, l * 3 + 3)
                        pe.wait_ge(s_vlo, l + 1)
                        pe.matmul(SB[0][:, :], ones[:, :], F[:, 3, :], start=True, stop=True)
                        pe.matmul(SB[1][:, :], ones[:, :], F[:, 5, :], start=True, stop=True).then_inc(s_cms, 1)

                def hidden_T(kind):
                    pe.wait_ge(s_const, 80)
                    pe.wait_ge(s_hs, l * 2 + (kind + 1))
                    for c in range(2):
                        ins = pe.transpose(TP[kind][:, 64 * c:64 * c + 64], F[0:64, 2 + kind, P * c:P * c + P],
                                           ident[0:64, 0:64])
                    ins.then_inc(s_hT, 1)

                for kind in range(2):
                    pe.wait_ge(s_tblo, l * 2 + (kind + 1))
                    for i in range(4):
                        u = U_W1 + 4 * kind + i
                        unit(u)
                        for c in range(4):
                            j = 4 * i + c
                            ins = three(O[kind][0:64, 0:256], lambda b: TB[:, kind, b, j, :], wtile(u, c, 256),
                                        j == 0, j == 15)
                        ins.then_inc(s_wused, 1)
                        if kind == 1 and i == 0:
                            hidden_T(0)
                unit(U_W2K)
                pe.wait_ge(s_hTlo, l * 2 + 1)
                for c in range(2):
                    ins = three(SB[0][:, 0:64], wtile(U_W2K, c), lambda b: HK[:, b, c, :], c == 0, c == 1)
                ins.then_inc(s_wused, 1)
                hidden_T(1)
                unit(U_W2V)
                pe.wait_ge(s_hTlo, l * 2 + 2)
                for gr in range(2):
                    for c in range(2):
                        ins = three(SB[1][:, 64 * gr:64 * gr + 64], lambda b: HV[:, b, c, gr, :],
                                    wtile(U_W2V, c, 64), c == 0, c == 1)
                ins.then_inc(s_wused, 1)
                pe.wait_ge(s_kclo, l * 2 + 2)
                pe.wait_ge(s_rlo, l * 4 + 4)
                for i in range(2):
                    for q2 in range(2):
                        qt = 2 * i + q2
                        for h in range(HEADS):
                            for c in range(2):
                                pe.matmul(O[i][:, q2 * 256 + h * NC:q2 * 256 + (h + 1) * NC],
                                          QS[:, h, qt * P:(qt + 1) * P], kcmp[:, c, (h // 4) * NC:(h // 4 + 1) * NC],
                                          start=(q2 == 0 and h == 0 and c == 0), stop=False, skip_group_check=True)
                        ins = pe.matmul(O[i][:, q2 * 256:(q2 + 1) * 256], identb,
                                        cmask[:, qt, :].unsqueeze(1).broadcast_to([P, HEADS, NC]),
                                        start=False, stop=(q2 == 1), skip_group_check=True)
                    ins.then_inc(s_cs, 1)
                pe.wait_ge(s_cw, l * 2 + 2)
                for gr in range(2):
                    for qt in range(QT):
                        ins = pe.transpose(TP[gr][:, qt * P:(qt + 1) * P],
                                           F[:, 6 + qt // 2, (qt % 2) * 256 + gr * P:(qt % 2) * 256 + (gr + 1) * P], ident)
                    ins.then_inc(s_cT, 1)

                def nsa_scores(i):
                    t, e, br, qt = NSA_JOBS[i]
                    w = (qt + 1) * P
                    for c in range(2):
                        pe.matmul(SB[i % 2][:, 0:w], QS[:, 2 * t + e, qt * P:w], KN[:, br, t // 2, c, 0:w],
                                  start=(c == 0), stop=False)

                def mla_scores(i):
                    t, e, _, qt = MLA_JOBS[i]
                    w = (qt + 1) * P
                    if qt == 0:
                        pe.wait_ge(s_mlo, l * 9 + (2 + 2 * t + e))
                        pe.wait_ge(s_gfree, l * NG + (G_MLA + 4 * t + 4 + GFREE0))
                    three(SB[i % 2][:, 0:w], lambda c: MQ[:, t % 2, e, c, qt * P:w], lambda c: MK[:, t % 2, e, c, 0:w],
                          True, False)

                def nsa_values(hp):
                    t, e, br, _ = NSA_JOBS[hp * QT]
                    dst = O[t % 2]
                    if e == 0 and br == 0:
                        if t >= 2:
                            pe.wait_ge(s_olo, l * 8 + (t - 1))
                        three(dst[:, :], lambda c: vblk[:, c, t, :], lambda c: pcT[:, t // 2, c, :], True, False)
                    col = 128 * (t // 2) + (64 if e == 0 else 0)
                    return dst, lambda kt: (lambda c: VN[:, c, br, kt, col:col + P]), False, e == 1 and br == 1

                def mla_values(hp):
                    t, e, _, _ = MLA_JOBS[hp * QT]
                    if e == 0:
                        pe.wait_ge(s_olo, l * 8 + (PAIRS + t - 1))
                    return O[t % 2], lambda kt: (lambda c: MV[:, t % 2, c, kt, 64 * e:64 * e + P]), e == 0, e == 1

                def jobs(job0, n, scores, values, hook):
                    for i in range(len(n) + LAG_PV + 1):
                        if i < len(n):
                            hook(i)
                            qt = n[i][3]
                            if job0 + i >= 2:
                                pe.wait_ge(s_exp, l * NJ + (job0 + i - 1))
                            scores(i)
                            pe.matmul(SB[i % 2][:, qt * P:(qt + 1) * P], identb, causal, start=False, stop=True)\
                                .then_inc(s_scores, 1)
                        j = i - LAG_T
                        if 0 <= j < len(n):
                            pe.wait_ge(s_scl, l * NJ + (job0 + j + 1))
                            if job0 + j >= 2:
                                pe.wait_ge(s_plo, l * NJ + (job0 + j - 1))
                            for kt in range(n[j][3] + 1):
                                ins = pe.transpose(TP[j % 2][:, kt * P:(kt + 1) * P], F[:, j % 3, kt * P:(kt + 1) * P],
                                                   ident)
                            ins.then_inc(s_trans, 1)
                        j = i - LAG_PV
                        if j >= 0 and j % QT == QT - 1:
                            hp = j // QT
                            pe.wait_ge(s_plo, l * NJ + (job0 + j + 1))
                            dst, v, first, last = values(hp)
                            slot = (job0 // QT + hp) % 2
                            for kt in range(QT):
                                ins = three(dst[:, kt * P:S], v(kt), lambda c: PT[:, slot, c, kt * S:(kt + 1) * S - kt * P],
                                            first and kt == 0, last and kt == QT - 1)
                            ins.then_inc(s_pv, 1)

                def mla_proj(p):
                    u, g = U_MLA + p, G_MLA + 4 * p
                    unit(u)
                    for e in range(2):
                        free(g + e)
                        for k in range(2):
                            ins = three(G[e][:, :], wtile(u, 2 * k + e), rows(cn, k), k == 0, k == 1)
                        ins.then_inc(s_mready, 1)
                    free(g + 2)
                    three(G[0][:, :], wtile(u, 4), rows(cn, 2), True, True).then_inc(s_mready, 1)
                    free(g + 3)
                    for tt in range(QT):
                        ins = three(G[1][:, tt * P:(tt + 1) * P], lambda c: cn[:, c, 2, tt * P:(tt + 1) * P],
                                    wtile(u, 5), True, True)
                    ins.then_inc(s_wused, 1)

                pe.wait_ge(s_vlo, l + 1)
                pe.wait_ge(s_vz, l * 2 + 1)
                pe.wait_ge(s_kl, l * 2 + 2)
                pe.wait_ge(s_cTlo, l * 2 + 2)
                jobs(0, NSA_JOBS, nsa_scores, nsa_values, lambda i: None)
                pe.wait_ge(s_clo, l * 3 + 3)
                pe.wait_ge(s_vz, l * 2 + 2)
                mla_proj(0)
                jobs(len(NSA_JOBS), MLA_JOBS, mla_scores, mla_values,
                     lambda i: mla_proj(i // 8 + 1) if i % 8 == 5 and i < 24 else None)
                pe.wait_ge(s_olo, l * 8 + 8)
                for m in range(KT):
                    unit(U_WO + m)
                    if m >= 2:
                        pe.wait_ge(s_mab, l * KT + (m - 1))
                    for k in range(KT):
                        dst = (SB if k < 4 else TP)[m % 2][:, :]
                        ins = three(dst, wtile(U_WO + m, k), rows(xg, k), k % 4 == 0, k % 4 == 3)
                    ins.then_inc(s_wused, 1)
                for m in range(KT):
                    unit(U_OUT + m)
                    free(G_OUT + m)
                    tile(G[m % 2][:, :], U_OUT + m, H,
                         (lambda k: pe.wait_ge(s_mglo, l * KT + (k + 1))) if m == 0 else None)
                mean_square(l * 2 + 1, False)
                with pe.Fori(0, QUARTERS) as f:
                    for m in range(2 * KT):
                        u = U_MLP + m
                        pe.wait_ge(s_wlo, l * NU + f * U_QUARTER + (u + 1))
                        pe.wait_ge(s_gfree, l * NG + f * U_QUARTER + (G_MLP + m + 1 + GFREE0 - 2))
                        if m < KT:
                            tile(G[m % 2][:, :], u, xg, (lambda k: pe.wait_ge(s_xlo, l * 16 + (8 + k + 1))) if m == 0 else None)
                        else:
                            tile(G[m % 2][:, :], u, H,
                                 (lambda k: pe.wait_ge(s_hlo, l * (QUARTERS * KT) + f * KT + (k + 1)))
                                 if m == KT else None)
            mean_square(L * 2, False)


def _columns(w, cols):
    import numpy as np
    w = w[:, cols]
    return np.ascontiguousarray(w.reshape(-1, P, w.shape[1]).transpose(1, 0, 2)).reshape(P, -1)


def _units(w):
    import numpy as np
    r = np.arange
    slabs = np.zeros((L * NU + 2, P, 1024), np.float32)
    for l in range(L):
        n = l * NU
        wi, w1, w2 = w["w_in"][l], w["cmp_w1"][l], w["cmp_w2"][l]

        def put(u, slab):
            slabs[n + u, :, :slab.shape[1]] = slab

        for t in range(4):
            put(U_Q + t, _columns(wi, r(128 * t, 128 * t + 128)))
        put(U_KS, _columns(wi, r(768, 896)))
        put(U_KW, _columns(wi, r(1024, 1152)))
        v = _columns(wi, np.concatenate([r(896, 1024), r(1152, 1280)]))
        put(U_V, v[:, 0:1024])
        put(U_V + 1, v[:, 1024:2048])
        put(U_KC, _columns(wi, r(512, 640)))
        put(U_VC, _columns(wi, r(640, 768)))
        put(U_MISC, _columns(wi, np.concatenate([r(1280, 1304), r(1264, 1304), r(1688, 1720), r(1704, 1720), r(1688, 1704)])))
        for t in range(2):
            put(U_CQ + t, _columns(wi, r(1304 + 128 * t, 1432 + 128 * t)))
        put(U_CKV, _columns(wi, r(1560, 1688)))
        for i in range(2 * KT):
            put(U_GATE + i, _columns(wi, r(1720 + 128 * i, 1848 + 128 * i)))
        for kind in range(2):
            slab = _columns(w1[kind], r(256))
            for i in range(4):
                put(U_W1 + 4 * kind + i, slab[:, 1024 * i:1024 * i + 1024])
        put(U_W2K, _columns(w2[0], np.concatenate([r(64), r(64)])))
        put(U_W2V, _columns(w2[1], r(64)))
        for p in range(PAIRS):
            head = np.concatenate([r(96), r(80, 96), r(64, 80)])
            uq = _columns(w["mla_w_uq"][l], np.concatenate([192 * p + head, 192 * p + 96 + head]))
            kv = [256 * p + 128 * e + o + r(64) for o in (0, 64) for e in range(2)]
            put(U_MLA + p, np.concatenate([uq, _columns(w["mla_w_ukv"][l], np.concatenate(kv))], axis=1))
        for m in range(KT):
            c = r(128 * m, 128 * m + 128)
            put(U_WO + m, np.concatenate([_columns(w["nsa_w_o"][l], c), _columns(w["mla_w_o"][l], c)], axis=1))
            put(U_OUT + m, _columns(w["w_out"][l], c))
            for f in range(QUARTERS):
                put(U_MLP + f * U_QUARTER + m, _columns(w["w_up"][l], D * f + c))
                put(U_MLP + f * U_QUARTER + KT + m, _columns(w["w_down"][l][D * f:D * f + D], c))
    return slabs


def _params(w):
    import numpy as np
    cols = []
    for l in range(L):
        for name in ("attn_norm", "mlp_norm", "mla_q_norm", "mla_kv_norm"):
            cols.append(w[name][l].reshape(-1, P).T)
        for kind in range(2):
            cols.append(w["cmp_pe"][l, kind].reshape(16, P).T)
    cols.append(w["final_norm"].reshape(-1, P).T)
    return np.ascontiguousarray(np.concatenate(cols, axis=1))


def _constants():
    import numpy as np

    def angles(d):
        inv = np.float32(10000.0) ** (-np.arange(0, d, 2, dtype=np.float32) / np.float32(d))
        a = np.arange(S, dtype=np.float32)[None, :] * inv.astype(np.float32)[:, None]
        return np.cos(a).astype(np.float32), np.sin(a).astype(np.float32)

    c, s = angles(64)
    cm, sm = angles(32)
    tables = np.stack([np.concatenate([c, c, c, c]), np.concatenate([s, -s, s, -s]),
                       np.concatenate([np.ones((64, S), np.float32), cm, cm, -sm, sm])], axis=1)
    q = np.arange(P)
    seen = (16 * np.arange(NC) + 31)[None, None, :] <= (P * np.arange(QT)[None, :, None] + q[:, None, None])
    seen &= (np.arange(NC) < N_CMP)[None, None, :]
    eye = np.eye(P, dtype=np.float32)
    cf = np.stack([eye, seen.reshape(P, P).astype(np.float32)], axis=1)
    neg = np.float32(-1e30)
    cb = np.stack([eye, np.where(q[None, :] <= q[:, None], 0, neg), np.where(seen.reshape(P, P), 0, neg)], axis=1)
    return np.ascontiguousarray(tables.astype(np.float32)), cf, np.ascontiguousarray(cb.astype(np.float32))


def kernel(**inputs):
    import numpy as np
    import concourse.bacc as bacc
    from concourse import mybir as mb
    from concourse.bass_utils import run_bass_kernel_spmd as run

    w = {k: np.asarray(v) for k, v in inputs.items()}
    tables, cf, cb = _constants()
    arrays = {
        "units": _units(w), "params": _params(w), "tables": tables, "cf32": cf, "cmasks": cb,
        "x_in": np.ascontiguousarray(w["x"][0].T.reshape(KT, P, S).transpose(1, 0, 2)),
    }
    nc = bacc.Bacc("TRN2", target_bir_lowering=False, num_devices=1)
    ins = {k: nc.dram_tensor(k, v.shape, mb.dt.from_np(v.dtype), kind="ExternalInput").ap() for k, v in arrays.items()}
    gates = nc.dram_tensor("gates", (2 * KT, P, S), mb.dt.float32, kind="Internal").ap()
    out = nc.dram_tensor("out", (KT, P, S), mb.dt.float32, kind="ExternalOutput").ap()
    build(nc, ins["units"], ins["params"], ins["x_in"], ins["tables"], ins["cf32"], ins["cmasks"], gates, out)
    r = run(nc, [arrays], core_ids=[0])
    return np.ascontiguousarray(r.results[0]["out"].reshape(D, S).T).reshape(1, S, D)
```

```python
from contextlib import ExitStack

import concourse.bass as bass
from concourse import mybir

F32 = mybir.dt.float32
R32 = mybir.dt.float32r
BF16 = mybir.dt.bfloat16
ACT = mybir.ActivationFunctionType
ALU = mybir.AluOpType
AX = mybir.AxisListType

P = 128
L = 2
S = 512
D = 1024
KT = D // P
QT = S // P
HD = 64
HEADS = 8
PAIRS = HEADS // 2
N_CMP = 31
NC = 32
EPS = 1e-6
TINY = 1e-30
NSA_SCALE = HD ** -0.5
MLA_SCALE = 96 ** -0.5

PREFIX = [("Q", 0), ("GATE", 0), ("Q", 1), ("GATE", 1), ("Q", 2), ("GATE", 2), ("Q", 3), ("GATE", 3), ("KS", 0), ("GATE", 4),
          ("KW", 0), ("GATE", 5), ("KC", 0), ("GATE", 6), ("VC", 0), ("GATE", 7), ("V", 0), ("V", 1), ("MISC", 0),
          ("CQ", 0), ("CQ", 1), ("CQ", 2), ("W1", 0), ("W1", 1), ("W1", 2), ("W1", 3), ("GATE", 8),
          ("W1", 4), ("W1", 5), ("W1", 6), ("W1", 7), ("GATE", 9), ("GATE", 10), ("W2K", 0), ("GATE", 11),
          ("W2V", 0), ("GATE", 12), ("GATE", 13), ("GATE", 14), ("GATE", 15)]
UNIT = {item: u for u, item in enumerate(PREFIX)}
U_MLA = len(PREFIX)
U_WO = U_MLA + PAIRS
U_OUT = U_WO + KT
U_MLP = U_OUT + KT
QUARTERS = 4
U_QUARTER = 2 * KT
NU = U_MLP + QUARTERS * U_QUARTER
TILE = {item: g for g, item in enumerate(p for p in PREFIX if p[0] in ("Q", "GATE", "KS", "KW", "KC", "VC", "MISC", "CQ"))}
G_MLA = len(TILE)
G_OUT = G_MLA + 4 * PAIRS
G_MLP = G_OUT + KT
NG = G_MLP + QUARTERS * U_QUARTER
ROPED = [("Q", 0), ("Q", 1), ("Q", 2), ("Q", 3), ("KS", 0), ("KW", 0), ("KC", 0)]
NGATE = 2 * KT
WUSED0 = 2
GFREE0 = KT + 2
PR_ATTN, PR_MLP, PR_QN, PR_KVN, PR_PE, NPAR = 0, 8, 16, 18, 19, 51

NSA_JOBS = [(t, e, br, qt) for t in range(PAIRS) for e in range(2) for br in range(2) for qt in range(QT)]
MLA_JOBS = [(t, e, 0, qt) for t in range(PAIRS) for e in range(2) for qt in range(QT)]
JOBS = NSA_JOBS + MLA_JOBS
NJ, NSA_NJ = len(JOBS), len(NSA_JOBS)
NSA_PASSES = NSA_NJ // QT
NHP = NJ // QT
PT_STEP = 384
PT_LEN = 3 * PT_STEP + S
LAG_SUM, LAG_T, LAG_SPLIT, LAG_PV, LAG_O = 1, 3, 4, 8, 9
STEPS = NJ + LAG_O
FR = 4
QK_STEP = {NSA_NJ // 2 + 10: 0, NSA_NJ + 3: 1, NSA_NJ + 11: 2, NSA_NJ + 19: 3}
V_STEP = {NSA_NJ // 2 + 14: 0, NSA_NJ + 9: 1, NSA_NJ + 17: 2, NSA_NJ + 25: 3}
QK_AFTER = [NSA_NJ // 2, NSA_NJ, NSA_NJ + 8, NSA_NJ + 16]
V_AFTER = [5, NSA_PASSES, NSA_PASSES + 2, NSA_PASSES + 4]
MHI0, MLO0 = [0, 5, 10, 14], [0, 3, 6, 8]
NMHI, NMLO = 18, 10
NOUT = PAIRS + HEADS

AREA = 13312


class Chain:

    def __init__(self, eng, sem):
        self.eng, self.sem, self.n = eng, sem, 0

    def restart(self):
        self.eng.sem_clear(self.sem)
        self.n = 0

    def mark(self, ins):
        ins.then_inc(self.sem, 1)
        self.n += 1

    def wait(self):
        self.eng.wait_ge(self.sem, self.n)


def build(nc, units, params, x_in, tables, cf32, cmasks, gates_dram, out):
    ctx = ExitStack()
    with ctx:
        def sb(name, shape, dt):
            return ctx.enter_context(nc.sbuf_tensor(name, shape, dt))

        def bank(name):
            return ctx.enter_context(nc.psum_tensor(name, [P, 512], F32))

        def sem(name):
            return ctx.enter_context(nc.semaphore(name))

        x = sb("x", [P, KT, S], F32)
        stage = sb("stage", [P, 2, 1024], F32)
        wsplit = sb("wsplit", [P, 2, 2, 1024], R32)
        xg = sb("xg", [P, 2, KT, S], R32)
        area = sb("area", [P, AREA], R32)
        area_b = sb("area_b", [P, 2 * 2 * PT_LEN], R32)
        pcT = sb("pcT", [P, 2, 2, S], R32)
        cn = sb("cn", [P, 2, 3, S], R32)
        vblk = sb("vblk", [P, 2, 4, P], R32)
        F = sb("F", [P, 8, S], F32)
        Y = sb("Y", [P, 2, S], F32)
        rs = sb("rs", [P, S], F32)
        kpe = sb("kpe", [P, S], F32)
        rope = sb("rope", [P, 3, S], F32)
        constf = sb("constf", [P, 2, P], F32)
        constb = sb("constb", [P, 3, P], BF16)
        ones = sb("ones", [P, P], F32)
        par_all = sb("par_all", [P, L * NPAR + KT], F32)
        par = sb("par", [P, NPAR], F32)
        rc = sb("rc", [P, 3, QT], F32)
        gt = sb("gt", [P, QT, 24], F32)
        small = sb("small", [P, 4, 17], F32)
        nmx = sb("nmx", [P, 4], F32)
        sums = sb("sums", [P, 4], F32)
        rsum = sb("rsum", [P, 4], F32)

        QS = area[:, 0:4096].rearrange("p (h n) -> p h n", h=HEADS)
        KN = area[:, 4096:8192].rearrange("p (g b c n) -> p b g c n", b=2, g=2, c=2)
        VN = area[:, 8192:13312].rearrange("p (c b t n) -> p c b t n", c=2, b=2, t=QT)
        MQ = area[:, 0:4096].rearrange("p (s e c n) -> p s e c n", s=2, e=2, c=2)
        MK = area[:, 4096:8192].rearrange("p (s e c n) -> p s e c n", s=2, e=2, c=2)
        MV = [pcT[:, 0, :, :], area[:, 8192:9216].rearrange("p (c n) -> p c n", c=2)]
        H = area[:, 0:8192].rearrange("p (c m n) -> p c m n", c=2, m=KT)
        PT = area_b[:, :].rearrange("p (s c n) -> p s c n", s=2, c=2)
        TB = area_b[:, 0:4096].rearrange("p (k c j n) -> p k c j n", k=2, c=2, j=16)
        HK = area_b[:, 4096:4352].rearrange("p (c j n) -> p c j n", c=2, j=2)
        kcmp = area_b[:, S + PT_STEP:S + PT_STEP + 4 * NC].rearrange("p (c n) -> p c n", c=2)
        HV = area_b[:, 4352:5376].rearrange("p (c j g n) -> p c j g n", c=2, j=2, g=2)
        ident, mask01 = constf[:, 0, :], constf[:, 1, :].rearrange("p (q n) -> p q n", q=QT)
        identb, causal = constb[:, 0, :], constb[:, 1, :]
        cmask = constb[:, 2, :].rearrange("p (q n) -> p q n", q=QT)
        cosN, sinN, tabM = rope[:, 0, :], rope[:, 1, :], rope[:, 2, :]

        G = [bank("G0"), bank("G1")]
        SB = [bank("S0"), bank("S1")]
        TP = [bank("T0"), bank("T1")]
        O = [bank("O0"), bank("O1")]

        def sems(*names):
            return [sem(n) for n in names]

        eps = small[:, 0, 16:17]
        tbf = F[:, 0:2, :].rearrange("p a n -> p (a n)")
        final = [F[:, 4, :], F[:, 5, :], F[:, 6, :], F[:, 7, :], F[:, 0, :], F[:, 1, :], Y[:, 0, :], Y[:, 1, :]]

        def pt_view(slot, c, qt):
            if qt < 3:
                t = PT[:, slot, c, 0:QT * PT_STEP].rearrange("p (k n) -> p k n", n=PT_STEP)
                return t[:, 0:qt + 1, qt * P:(qt + 1) * P]
            t = PT[:, slot, c, P:P + QT * PT_STEP].rearrange("p (k n) -> p k n", n=PT_STEP)
            return t[:, 0:QT, 2 * P:3 * P]

        def tp_view(i, qt):
            return TP[i][:, 0:(qt + 1) * P].rearrange("p (k n) -> p k n", n=P)

        def output_of(j):
            t, e, br, qt = JOBS[j]
            if j < NSA_NJ:
                return t, (e, br, qt) == (1, 1, QT - 1), slice(0, P), slice(0, P), t
            return PAIRS + 2 * t + e, qt == QT - 1, slice(0, HD), slice(HD * e, HD * e + HD), PAIRS + t

        def prob(j, w):
            return F[:, j % FR, 0:w]

        s_const, s_init = sems("s_const", "s_init")
        s_w = sems("s_w0", "s_w1")
        s_whi, s_wlo = sems("s_whi", "s_wlo")
        s_wused = sem("s_wused")
        s_gfree = sem("s_gfree")
        s_par = sem("s_par")
        s_sq, s_sqadd = sems("s_sq", "s_sqadd")
        s_ms, s_rms, s_rs = sems("s_ms", "s_rms", "s_rs")
        s_xhi, s_xlo = sems("s_xhi", "s_xlo")
        s_rot, s_roped = sems("s_rot", "s_roped")
        s_rhi, s_rlo, s_kl = sems("s_rhi", "s_rlo", "s_kl")
        s_vz, s_vhi, s_vlo = sems("s_vz", "s_vhi", "s_vlo")
        s_cc, s_tb, s_tbhi, s_tblo = sems("s_cc", "s_tb", "s_tbhi", "s_tblo")
        s_tgT, s_tg, s_gt = sems("s_tgT", "s_tg", "s_gt")
        s_pe1, s_swap, s_kpe = sems("s_pe1", "s_swap", "s_kpe")
        s_csq, s_csum, s_cms, s_crms = sems("s_csq", "s_csum", "s_cms", "s_crms")
        s_cf, s_chi, s_clo = sems("s_cf", "s_chi", "s_clo")
        s_ty = sem("s_ty")
        s_gst = sem("s_gst")
        s_gld = sems("s_gld0", "s_gld1")
        s_ht, s_hs, s_hT, s_hThi, s_hTlo = sems("s_ht", "s_hs", "s_hT", "s_hThi", "s_hTlo")
        s_kchi, s_kclo = sems("s_kchi", "s_kclo")
        s_cs, s_cmax, s_cexp, s_cw = sems("s_cs", "s_cmax", "s_cexp", "s_cw")
        s_cT, s_cThi, s_cTlo = sems("s_cT", "s_cThi", "s_cTlo")
        s_scores, s_max, s_exp, s_rsum, s_scl = sems("s_scores", "s_max", "s_exp", "s_rsum", "s_scl")
        s_trans, s_phi, s_plo = sems("s_trans", "s_phi", "s_plo")
        s_pv = sem("s_pv")
        s_ohi, s_olo = sems("s_ohi", "s_olo")
        s_mready, s_mhi, s_mlo = sems("s_mready", "s_mhi", "s_mlo")
        s_mab, s_mg, s_mghi, s_mglo = sems("s_mab", "s_mg", "s_mghi", "s_mglo")
        s_hsq, s_hhi, s_hlo = sems("s_hsq", "s_hhi", "s_hlo")
        s_fin, s_out = sems("s_fin", "s_out")
        s_stand = sem("s_stand")
        s_carry = sem("s_carry")
        s_dvec = sem("s_dvec")

        block = ctx.enter_context(nc.Block())

        @block.sync
        def _(sp):
            sp.dma_start(stage[:, 0, :], units[0]).then_inc(s_w[0], 16)
            sp.dma_start(stage[:, 1, :], units[1]).then_inc(s_w[1], 16)
            with sp.Fori(1, L * NU // 2 + 1) as i:
                for s in range(2):
                    sp.wait_ge(s_wlo, i * 2 + (s - 1))
                    sp.dma_start(stage[:, s, :], units[bass.ds(i * 2 + s, 1)].rearrange("o p n -> (o p) n"))\
                        .then_inc(s_w[s], 16)
            for m in range(KT):
                sp.wait_ge(s_fin, m + 1)
                sp.dma_start(out[m], final[m]).then_inc(s_out, 16)
            sp.wait_ge(s_w[0], 16 * (L * NU // 2 + 1))
            sp.wait_ge(s_w[1], 16 * (L * NU // 2 + 1))
            sp.wait_ge(s_out, 16 * KT)

        @block.gpsimd
        def _(pool):
            pool.dma_start(x[:, :, :], x_in).then_inc(s_const, 16)
            pool.dma_start(par_all[:, :], params).then_inc(s_const, 16)
            pool.dma_start(rope[:, :, :], tables).then_inc(s_const, 16)
            pool.dma_start(constf[:, :, :], cf32).then_inc(s_const, 16)
            pool.dma_start(F[:, 4, 0:3 * P].rearrange("p (c n) -> p c n", c=3), cmasks).then_inc(s_const, 16)
            pool.memset(ones[:, :], 1.0).then_inc(s_init, 1)
            pool.memset(vblk[:, :, :, :].bitcast(F32), 0.0).then_inc(s_init, 1)
            pool.wait_ge(s_const, 80)
            with pool.Fori(0, L) as l:
                pool.wait_ge(s_par, l + 1)
                pool.sem_inc(s_stand, 1)
                for c in range(2):
                    for br in range(2):
                        zeros = VN[:, c, br, :, :].rearrange("p t (z n) -> p t z n", n=HD)
                        ins = pool.memset(zeros[:, :, 0:5:2, :].bitcast(F32), 0.0)
                ins.then_inc(s_vz, 1)
                for item in PREFIX:
                    if item in ROPED:
                        r = ROPED.index(item)
                        pool.wait_ge(s_gfree, l * NG + (TILE[item] + 1 + GFREE0))
                        if r >= 2:
                            pool.wait_ge(s_roped, l * 7 + (r - 1))
                        if r == 0:
                            pool.wait_ge(s_vz, l + 1)
                        elif r >= 5:
                            pool.wait_ge(s_kl, l * 2 + (r - 4))
                        for q in range(4):
                            o = q ^ 1
                            ins = pool.tensor_tensor(F[32 * q:32 * q + 32, r % 2, :], Y[32 * o:32 * o + 32, 0, :],
                                                     sinN[32 * o:32 * o + 32, :], ALU.mult)
                        ins.then_inc(s_rot, 1)
                    if item[0] == "GATE":
                        i = item[1]
                        pool.wait_ge(s_ty, l * NGATE + (i + 1))
                        pool.sem_inc(s_stand, 1)
                        pool.dma_start(gates_dram[i], Y[:, 1, :]).then_inc(s_gst, 16)
                    if item in (("GATE", 4), ("GATE", 5)):
                        r = item[1]
                        pool.wait_ge(s_rot, l * 7 + (r + 1))
                        pool.wait_ge(s_rhi, l * 6 + (r + 1))
                        for gr in range(2):
                            src = F[64 * gr:64 * gr + 64, 3 + r % 2, :]
                            for half in range(2):
                                ins = pool.tensor_tensor(KN[64 * half:64 * half + 64, r - 4, gr, 1, :], src,
                                                         KN[64 * gr:64 * gr + 64, r - 4, gr, 0, :], ALU.subtract)
                        ins.then_inc(s_kl, 1)
                pool.wait_ge(s_rot, l * 7 + 7)
                for j, (t, e, br, qt) in enumerate(JOBS):
                    pool.wait_ge(s_rsum, l * NJ + (j + 1))
                    pool.sem_inc(s_stand, 1)
                    p, col = prob(j, (qt + 1) * P), (1 + br) * HEADS + 2 * t + e
                    gated = j < NSA_NJ
                    pool.tensor_scalar(p, p, rsum[:, j % 4:j % 4 + 1], gt[:, qt, col:col + 1] if gated else None,
                                       ALU.mult, ALU.mult if gated else ALU.bypass).then_inc(s_scl, 1)
                pool.wait_ge(s_gst, (l + 1) * (16 * NGATE))
                for m in range(KT):
                    if m < 2:
                        pool.wait_ge(s_plo, l * NJ + NJ)
                    else:
                        pool.wait_ge(s_mab, l * KT + (m - 1))
                    pool.sem_inc(s_stand, 1)
                    pool.dma_start(F[:, m % 2, :], gates_dram[m]).then_inc(s_gld[m % 2], 16)
                    pool.dma_start(F[:, 2 + m % 2, :], gates_dram[KT + m]).then_inc(s_gld[m % 2], 16)
                with pool.Fori(0, QUARTERS) as f:
                    for m in range(KT):
                        pool.wait_ge(s_gfree, l * NG + f * U_QUARTER + (G_MLP + m + 1 + GFREE0))
                        if m >= 2:
                            pool.wait_ge(s_hlo, l * (QUARTERS * KT) + f * KT + (m - 1))
                        pool.tensor_tensor(F[:, m % 2, :], Y[:, m % 2, :], Y[:, m % 2, :], ALU.mult)\
                            .then_inc(s_hsq, 1)

        @block.scalar
        def _(act):
            def split_hi(half, u):
                s = u % 2
                act.wait_ge(s_w[s], half * 16 + (u // 2 + 1) * 16)
                act.wait_ge(s_wused, half * 2 + (u + 1))
                act.activation(wsplit[:, s, 0, :], stage[:, s, :], ACT.Copy).then_inc(s_whi, 1)

            def squares(n, x_ready, gains):
                for m in range(KT):
                    act.wait_ge(s_gfree, x_ready + m)
                    if m >= 2:
                        act.wait_ge(s_sqadd, n * KT + (m - 1))
                    act.activation(F[:, m % 2, :], x[:, m, :], ACT.Square).then_inc(s_sq, 1)
                    if gains is not None:
                        act.activation(xg[:, 0, m, :], x[:, m, :], ACT.Copy, scale=par[:, gains + m:gains + m + 1])\
                            .then_inc(s_xhi, 1)

            def root(n, columns):
                act.wait_ge(s_ms, n + 1)
                if columns:
                    act.activation(rc[:, 2, :], TP[0][:, 0:QT], ACT.Sqrt, scale=1.0 / D, bias=eps)
                act.activation(F[:, 3, :], SB[0][:, :], ACT.Sqrt, scale=1.0 / D, bias=eps).then_inc(s_rms, 1)

            def jobs(l):
                for i in range(STEPS):
                    if i in QK_STEP:
                        mla_qk(l, QK_STEP[i])
                    if i in V_STEP:
                        mla_v(l, V_STEP[i])
                    j = i - LAG_SPLIT
                    if 0 <= j < NJ:
                        hp, qt = j // QT, JOBS[j][3]
                        act.wait_ge(s_trans, l * NJ + (j + 1))
                        if hp >= 2:
                            act.wait_ge(s_pv, l * NHP + (hp - 1))
                        act.activation(pt_view(hp % 2, 0, qt), tp_view(j % 2, qt), ACT.Copy).then_inc(s_phi, 1)
                    if i < NJ:
                        w = (JOBS[i][3] + 1) * P
                        act.wait_ge(s_max, l * NJ + (i + 1))
                        act.activation(prob(i, w), SB[i % 2][:, 0:w], ACT.Exp, bias=nmx[:, i % 4:i % 4 + 1],
                                       accum_out=sums[:, i % 4:i % 4 + 1]).then_inc(s_exp, 1)
                    j = i - LAG_O
                    if j >= 0:
                        n, last, src, dst, tile = output_of(j)
                        if last:
                            act.wait_ge(s_pv, l * NHP + (j // QT + 1))
                            act.activation(xg[dst, 0, tile, :], O[n % 2][src, :], ACT.Copy).then_inc(s_ohi, 1)

            def mla_qk(l, p):
                s, g, hi0 = p % 2, G_MLA + 4 * p, MHI0[p]
                split_hi(l * (NU // 2), U_MLA + p + 1)
                act.wait_ge(s_scores, l * NJ + QK_AFTER[p])
                if p < 2:
                    for e in range(2):
                        ins = act.activation(MK[64:128, s, e, 0, :], kpe[64:128, :], ACT.Copy)
                    ins.then_inc(s_mhi, 1)
                for e in range(2):
                    act.wait_ge(s_gfree, l * NG + (g + e + 1 + GFREE0))
                    act.activation(MQ[:, s, e, 0, :], Y[:, e, :], ACT.Copy, scale=MLA_SCALE).then_inc(s_mhi, 1)
                act.wait_ge(s_mready, l * 12 + (3 * p + 3))
                for e in range(2):
                    ins = act.activation(MK[0:64, s, e, 0, :], G[0][64 * e:64 * e + 64, :], ACT.Copy)
                ins.then_inc(s_mhi, 1)

            def mla_v(l, p):
                act.wait_ge(s_pv, l * NHP + V_AFTER[p])
                act.wait_ge(s_wused, l * NU + (U_MLA + p + 1 + WUSED0))
                act.activation(MV[p % 2][:, 0, :], G[1][:, :], ACT.Copy).then_inc(s_mhi, 1)

            def gate_tanh(l, i):
                act.wait_ge(s_gfree, l * NG + (TILE["GATE", i] + 1 + GFREE0))
                act.activation(Y[:, 1, :], Y[:, 1, :], ACT.Tanh, scale=0.5).then_inc(s_ty, 1)

            act.wait_ge(s_const, 80)
            act.wait_ge(s_init, 4)
            split_hi(0, 0)
            with act.Fori(0, L) as l:
                half = l * (NU // 2)

                def ahead(u):
                    split_hi(half, u + 1)

                def q_hi(r):
                    act.wait_ge(s_roped, l * 7 + (r + 1))
                    q = F[:, 3 + r % 2, :]
                    act.activation(QS[0:64, 2 * r, :], q[0:64], ACT.Copy, scale=NSA_SCALE)
                    act.activation(QS[64:128, 2 * r + 1, :], q[64:128], ACT.Copy, scale=NSA_SCALE).then_inc(s_rhi, 1)

                def k_hi(br):
                    act.wait_ge(s_roped, l * 7 + (5 + br))
                    for gr in range(2):
                        k = F[64 * gr:64 * gr + 64, 3 + br, :]
                        for hf in range(2):
                            ins = act.activation(KN[64 * hf:64 * hf + 64, br, gr, 0, :], k, ACT.Copy)
                    ins.then_inc(s_rhi, 1)

                def v_hi():
                    act.wait_ge(s_rs, l * 2 + 1)
                    act.wait_ge(s_wused, l * NU + (UNIT["V", 1] + 1 + WUSED0))
                    for tt in range(QT):
                        src = SB[tt // 2][:, 256 * (tt % 2):256 * (tt % 2) + 256]
                        src = src.rearrange("p (b g n) -> p b g n", b=2, g=2)
                        for br in range(2):
                            dst = VN[:, 0, br, tt, :].rearrange("p (z n) -> p z n", n=HD)
                            ins = act.activation(dst[:, 1:4:2, :], src[:, br], ACT.Copy, scale=rc[:, 0, tt:tt + 1])
                    ins.then_inc(s_vhi, 1)

                def copies(kind):
                    if kind == 0:
                        act.wait_ge(s_roped, l * 7 + 7)
                        src = F[:, 3, :]
                    else:
                        act.wait_ge(s_gfree, l * NG + (TILE["VC", 0] + 1 + GFREE0))
                        act.wait_ge(s_tb, l * 2 + 1)
                        src = Y[:, 0, :]
                    for gr in range(2):
                        act.activation(F[0:64, 5 + gr, :], src[64 * gr:64 * gr + 64, :], ACT.Copy)
                        ins = act.activation(F[64:128, 5 + gr, 0:S - 1], src[64 * gr:64 * gr + 64, 1:S], ACT.Copy)
                    ins.then_inc(s_cc, 1)

                def blocks_hi(kind):
                    act.wait_ge(s_tb, l * 2 + (kind + 1))
                    act.activation(TB[:, kind, 0, :, :].rearrange("p j n -> p (j n)"), tbf, ACT.Copy)\
                        .then_inc(s_tbhi, 1)

                def nsa_gates():
                    act.wait_ge(s_tgT, l + 1)
                    act.activation(gt[:, :, :], TP[1][:, 0:QT * 24].rearrange("p (q n) -> p q n", q=QT), ACT.Tanh,
                                   scale=0.5).then_inc(s_tg, 1)

                def swap_key():
                    act.wait_ge(s_pe1, l + 1)
                    act.activation(F[64:96, 4, :], kpe[96:128, :], ACT.Copy)
                    act.activation(F[96:128, 4, :], kpe[64:96, :], ACT.Copy).then_inc(s_swap, 1)

                def c_squares():
                    act.wait_ge(s_gfree, l * NG + (TILE["CQ", 2] + 1 + GFREE0))
                    act.wait_ge(s_kpe, l + 1)
                    for c in range(3):
                        act.activation(F[:, 3 + c, :], F[:, c, :], ACT.Square).then_inc(s_csq, 1)

                def c_roots():
                    act.wait_ge(s_cms, l + 1)
                    act.activation(F[:, 3, :], SB[0][:, :], ACT.Sqrt, scale=1.0 / 256, bias=eps)
                    act.activation(F[:, 4, :], SB[1][:, :], ACT.Sqrt, scale=1.0 / 128, bias=eps).then_inc(s_crms, 1)

                def c_hi():
                    for c in range(3):
                        act.wait_ge(s_cf, l * 3 + (c + 1))
                        act.activation(cn[:, 0, c, :], F[:, c, :], ACT.Copy).then_inc(s_chi, 1)

                def hidden(kind):
                    act.wait_ge(s_wused, l * NU + (UNIT["W1", 4 * kind + 3] + 1 + WUSED0))
                    act.activation(F[0:64, 7, 256 * kind:256 * kind + 256], O[kind][0:64, 0:256], ACT.Tanh, scale=0.5)\
                        .then_inc(s_ht, 1)

                def hidden_hi(kind):
                    act.wait_ge(s_hT, l * 2 + (kind + 1))
                    hT = TP[kind][:, 0:128]
                    if kind == 0:
                        act.activation(HK[:, 0, :, :].rearrange("p j n -> p (j n)"), hT, ACT.Copy, scale=0.5)\
                            .then_inc(s_hThi, 1)
                    else:
                        dst = HV[:, 0, :, :, :].rearrange("p j g (r n) -> p (j g) r n", n=NC)
                        src = hT.rearrange("p (a n) -> p a n", n=NC).unsqueeze(2).broadcast_to([P, 4, 4, NC])
                        act.activation(dst, src, ACT.Copy, scale=0.5).then_inc(s_hThi, 1)

                def kc_hi():
                    act.wait_ge(s_wused, l * NU + (UNIT["W2K", 0] + 1 + WUSED0))
                    act.activation(kcmp[:, 0, :], SB[0][:, 0:64], ACT.Copy).then_inc(s_kchi, 1)

                def vc_hi():
                    act.wait_ge(s_wused, l * NU + (UNIT["W2V", 0] + 1 + WUSED0))
                    for gr in range(2):
                        for b in range(4):
                            dst = vblk[32 * b:32 * b + 32, 0, 2 * gr + b // 2, 64 * (b % 2):64 * (b % 2) + 64]
                            ins = act.activation(dst, SB[1][32 * b:32 * b + 32, 64 * gr:64 * gr + 64], ACT.Copy)
                    ins.then_inc(s_kchi, 1)

                act.wait_ge(s_par, l + 1)
                squares(l * 2, l * NG + (GFREE0 - KT + 1), PR_ATTN)
                for u, (name, i) in enumerate(PREFIX):
                    ahead(u)
                    if u == 0:
                        root(l * 2, True)
                    if (name, i) == ("GATE", 7):
                        blocks_hi(0)
                    if (name, i) == ("V", 0):
                        copies(1)
                    if (name, i) == ("MISC", 0):
                        v_hi()
                        blocks_hi(1)
                    if (name, i) == ("CQ", 1):
                        nsa_gates()
                        swap_key()
                    if (name, i) == ("W1", 0):
                        c_squares()
                    if (name, i) == ("GATE", 8):
                        hidden(0)
                    if (name, i) == ("W1", 5):
                        hidden_hi(0)
                    if (name, i) == ("GATE", 9):
                        hidden(1)
                        c_roots()
                    if (name, i) == ("GATE", 10):
                        hidden_hi(1)
                    if (name, i) == ("GATE", 11):
                        kc_hi()
                    if (name, i) == ("GATE", 12):
                        vc_hi()
                        c_hi()
                    if name == "GATE":
                        gate_tanh(l, i)
                        if i < 4:
                            q_hi(i)
                        elif i < 6:
                            k_hi(i - 4)
                        elif i == 6:
                            copies(0)
                for i in range(2):
                    act.wait_ge(s_cmax, l * 2 + (i + 1))
                    act.activation(F[:, 6 + i, :], F[:, 4 + i, :], ACT.Exp).then_inc(s_cexp, 1)
                for gr in range(2):
                    act.wait_ge(s_cT, l * 2 + (gr + 1))
                    act.activation(pcT[:, gr, 0, :], TP[gr][:, :], ACT.Copy).then_inc(s_cThi, 1)
                jobs(l)
                for m in range(KT):
                    ahead(U_WO + m)
                    act.wait_ge(s_mg, l * KT + (m + 1))
                    act.activation(H[:, 0, m, :], F[:, 6 + m % 2, :], ACT.Copy, scale=0.5).then_inc(s_mghi, 1)
                for m in range(KT):
                    ahead(U_OUT + m)
                squares(l * 2 + 1, l * NG + (G_OUT + 1 + GFREE0), PR_MLP)
                root(l * 2 + 1, False)
                with act.Fori(0, QUARTERS) as f:
                    half_f = l * (NU // 2) + f * KT
                    for m in range(2 * KT):
                        split_hi(half_f, U_MLP + m + 1)
                        if m < KT:
                            act.wait_ge(s_gfree, l * NG + f * U_QUARTER + (G_MLP + m + 1 + GFREE0))
                            act.activation(H[:, 0, m, :], Y[:, m % 2, :], ACT.Square).then_inc(s_hhi, 1)
            squares(L * 2, L * NG + (GFREE0 - KT + 1), None)
            root(L * 2, False)

        @block.vector
        def _(dve):
            chain = Chain(dve, s_dvec)

            def split_lo(half, u):
                s = u % 2
                dve.wait_ge(s_whi, half * 2 + (u + 1))
                dve.tensor_tensor(wsplit[:, s, 1, :], stage[:, s, :], wsplit[:, s, 0, :], ALU.subtract)\
                    .then_inc(s_wlo, 1)

            def rest(out_ap, full, scale, hi):
                return dve.scalar_tensor_tensor(out_ap, full, scale, hi, ALU.mult, ALU.subtract)

            def norm_sum(n, gains):
                for m in range(KT):
                    dve.wait_ge(s_sq, n * KT + (m + 1))
                    if m == 0:
                        dve.tensor_copy(F[:, 2, :], F[:, 0, :]).then_inc(s_sqadd, 1)
                    else:
                        dve.wait_ge(s_sqadd, n * KT + m)
                        dve.tensor_tensor(F[:, 2, :], F[:, 2, :], F[:, m % 2, :], ALU.add).then_inc(s_sqadd, 1)
                    if gains is not None:
                        dve.wait_ge(s_xhi, n * KT + (m + 1))
                        rest(xg[:, 1, m, :], x[:, m, :], par[:, gains + m:gains + m + 1], xg[:, 0, m, :])\
                            .then_inc(s_xlo, 1)

            def norm_end(n, columns):
                dve.wait_ge(s_rms, n + 1)
                if columns:
                    chain.mark(dve.reciprocal(rc[:, 0, :], rc[:, 2, :]))
                    chain.wait()
                    dve.tensor_scalar(rc[:, 1, :], rc[:, 0, :], 0.5, None, ALU.mult)
                dve.reciprocal(rs[:, :], F[:, 3, :]).then_inc(s_rs, 1)
                dve.wait_ge(s_const, 80)
                dve.wait_ge(s_rs, n + 1)

            def jobs(l):
                for i in range(STEPS):
                    if i in QK_STEP:
                        mla_qk(l, QK_STEP[i])
                    if i in V_STEP:
                        mla_v(l, V_STEP[i])
                    j = i - LAG_SUM
                    if 0 <= j < NJ:
                        dve.wait_ge(s_exp, l * NJ + (j + 1))
                        dve.reciprocal(rsum[:, j % 4:j % 4 + 1], sums[:, j % 4:j % 4 + 1]).then_inc(s_rsum, 1)
                    if i < NJ:
                        w = (JOBS[i][3] + 1) * P
                        dve.wait_ge(s_scores, l * NJ + (i + 1))
                        dve.tensor_reduce(nmx[:, i % 4:i % 4 + 1], SB[i % 2][:, 0:w], AX.X, ALU.max, negate=True)\
                            .then_inc(s_max, 1)
                    j = i - LAG_SPLIT
                    if 0 <= j < NJ:
                        slot, qt = (j // QT) % 2, JOBS[j][3]
                        dve.wait_ge(s_phi, l * NJ + (j + 1))
                        dve.tensor_tensor(pt_view(slot, 1, qt), tp_view(j % 2, qt), pt_view(slot, 0, qt), ALU.subtract)\
                            .then_inc(s_plo, 1)
                    j = i - LAG_O
                    if j >= 0:
                        n, last, src, dst, tile = output_of(j)
                        if last:
                            dve.wait_ge(s_ohi, l * NOUT + (n + 1))
                            dve.tensor_tensor(xg[dst, 1, tile, :], O[n % 2][src, :], xg[dst, 0, tile, :], ALU.subtract)\
                                .then_inc(s_olo, 1)

            def mla_qk(l, p):
                s, hi0 = p % 2, MHI0[p]
                split_lo(l * (NU // 2), U_MLA + p + 1)
                if p < 2:
                    dve.wait_ge(s_mhi, l * NMHI + (hi0 + 1))
                    for e in range(2):
                        ins = dve.tensor_tensor(MK[64:128, s, e, 1, :], kpe[64:128, :], MK[64:128, s, e, 0, :],
                                                ALU.subtract)
                    ins.then_inc(s_mlo, 1)
                    hi0 += 1
                for e in range(2):
                    dve.wait_ge(s_mready, l * 12 + (3 * p + e + 1))
                    dve.tensor_tensor(Y[:, e, :], G[e][:, :], tabM, ALU.mult).then_inc(s_gfree, 1)
                for e in range(2):
                    dve.wait_ge(s_mhi, l * NMHI + (hi0 + e + 1))
                    rest(MQ[:, s, e, 1, :], Y[:, e, :], MLA_SCALE, MQ[:, s, e, 0, :]).then_inc(s_mlo, 1)
                dve.wait_ge(s_mhi, l * NMHI + (hi0 + 3))
                for e in range(2):
                    ins = dve.tensor_tensor(MK[0:64, s, e, 1, :], G[0][64 * e:64 * e + 64, :], MK[0:64, s, e, 0, :],
                                            ALU.subtract)
                ins.then_inc(s_gfree, 1)

            def mla_v(l, p):
                dve.wait_ge(s_mhi, l * NMHI + (MHI0[p] + (5 if p < 2 else 4)))
                dve.tensor_tensor(MV[p % 2][:, 1, :], G[1][:, :], MV[p % 2][:, 0, :], ALU.subtract).then_inc(s_gfree, 1)

            dve.sem_inc(s_gfree, GFREE0)
            dve.memset(eps, EPS).then_inc(s_init, 1)
            dve.wait_ge(s_const, 80)
            dve.tensor_copy(constb[:, :, :].rearrange("p c n -> p (c n)"), F[:, 4, 0:3 * P]).then_inc(s_init, 1)
            split_lo(0, 0)
            with dve.Fori(0, L) as l:
                half = l * (NU // 2)

                def ahead(u):
                    split_lo(half, u + 1)

                def evac(item, dst):
                    dve.wait_ge(s_wused, l * NU + (UNIT[item] + 1 + WUSED0))
                    dve.tensor_tensor(dst, G[TILE[item] % 2][:, :], rs[:, :], ALU.mult).then_inc(s_gfree, 1)

                def own(item):
                    dve.wait_ge(s_gfree, l * NG + (TILE[item] + 1 + GFREE0))

                def q_lo(r):
                    dve.wait_ge(s_rhi, l * 6 + (r + 1))
                    q = F[:, 3 + r % 2, :]
                    rest(QS[64:128, 2 * r, :], q[0:64], NSA_SCALE, QS[0:64, 2 * r, :])
                    rest(QS[0:64, 2 * r + 1, :], q[64:128], NSA_SCALE, QS[64:128, 2 * r + 1, :]).then_inc(s_rlo, 1)

                def rotated(r):
                    dve.wait_ge(s_rot, l * 7 + (r + 1))
                    if r == 6:
                        dve.wait_ge(s_kl, l * 2 + 1)
                    chain.wait()
                    dve.tensor_tensor(F[:, 3 + r % 2, :], F[:, 2, :], F[:, r % 2, :], ALU.add).then_inc(s_roped, 1)

                def v_lo():
                    dve.wait_ge(s_vhi, l + 1)
                    for tt in range(QT):
                        src = SB[tt // 2][:, 256 * (tt % 2):256 * (tt % 2) + 256]
                        src = src.rearrange("p (b g n) -> p b g n", b=2, g=2)
                        for br in range(2):
                            hi = VN[:, 0, br, tt, :].rearrange("p (z n) -> p z n", n=HD)[:, 1:4:2, :]
                            lo = VN[:, 1, br, tt, :].rearrange("p (z n) -> p z n", n=HD)[:, 1:4:2, :]
                            ins = rest(lo, src[:, br], rc[:, 0, tt:tt + 1], hi)
                    ins.then_inc(s_vlo, 1)

                def blocks(kind):
                    dve.wait_ge(s_cc, l * 2 + (kind + 1))
                    if kind == 1:
                        dve.wait_ge(s_tblo, l * 2 + 1)
                    tb = tbf.rearrange("p (j g n) -> p j g n", j=16, g=2)
                    dve.memset(tb[:, :, :, N_CMP:NC], 0.0)
                    tok = F[:, 5:7, :].rearrange("p g (n r) -> p r g n", r=16)[:, 0:16:2]
                    for hf in range(2):
                        pe = par[:, PR_PE + 16 * kind + 8 * hf:PR_PE + 16 * kind + 8 * hf + 8]
                        pe = pe.unsqueeze(2).unsqueeze(3).broadcast_to([P, 8, 2, N_CMP])
                        ins = dve.tensor_tensor(tb[:, 8 * hf:8 * hf + 8, :, 0:N_CMP], tok[:, :, :, hf:hf + N_CMP], pe,
                                                ALU.add)
                    ins.then_inc(s_tb, 1)

                def blocks_lo(kind):
                    dve.wait_ge(s_tbhi, l * 2 + (kind + 1))
                    dve.tensor_tensor(TB[:, kind, 1, :, :].rearrange("p j n -> p (j n)"), tbf,
                                      TB[:, kind, 0, :, :].rearrange("p j n -> p (j n)"), ALU.subtract)\
                        .then_inc(s_tblo, 1)

                def key_products():
                    own(("MISC", 0))
                    dve.wait_ge(s_kl, l * 2 + 2)
                    dve.tensor_tensor(kpe[64:128, :], Y[64:128, 0, :], tabM[64:128, :], ALU.mult).then_inc(s_pe1, 1)

                def key_sum():
                    dve.wait_ge(s_swap, l + 1)
                    dve.tensor_tensor(kpe[64:128, :], kpe[64:128, :], F[64:128, 4, :], ALU.add).then_inc(s_kpe, 1)

                def nsa_gates():
                    dve.wait_ge(s_tg, l + 1)
                    dve.tensor_scalar(gt[:, :, :], gt[:, :, :], 0.5, 0.5, ALU.mult, ALU.add).then_inc(s_gt, 1)

                def c_norm():
                    dve.wait_ge(s_crms, l + 1)
                    chain.wait()
                    for c in range(3):
                        gain = par[:, PR_QN + c:PR_QN + c + 1]
                        dve.scalar_tensor_tensor(F[:, c, :], F[:, c, :], gain, F[:, 3 + c // 2, :],
                                                 ALU.mult, ALU.mult).then_inc(s_cf, 1)

                def c_lo():
                    for c in range(3):
                        dve.wait_ge(s_chi, l * 3 + (c + 1))
                        dve.tensor_tensor(cn[:, 1, c, :], F[:, c, :], cn[:, 0, c, :], ALU.subtract).then_inc(s_clo, 1)

                def hidden(kind):
                    h = F[0:64, 7, 256 * kind:256 * kind + 256]
                    dve.wait_ge(s_ht, l * 2 + (kind + 1))
                    dve.scalar_tensor_tensor(h, h, 1.0, O[kind][0:64, 0:256], ALU.add, ALU.mult).then_inc(s_hs, 1)

                def hidden_lo(kind):
                    dve.wait_ge(s_hThi, l * 2 + (kind + 1))
                    hT = TP[kind][:, 0:128]
                    if kind == 0:
                        rest(HK[:, 1, :, :].rearrange("p j n -> p (j n)"), hT, 0.5,
                             HK[:, 0, :, :].rearrange("p j n -> p (j n)")).then_inc(s_hTlo, 1)
                    else:
                        hi = HV[:, 0, :, :, :].rearrange("p j g (r n) -> p (j g) r n", n=NC)
                        lo = HV[:, 1, :, :, :].rearrange("p j g (r n) -> p (j g) r n", n=NC)
                        for r in range(4):
                            ins = rest(lo[:, :, r, :], hT.rearrange("p (a n) -> p a n", n=NC), 0.5, hi[:, :, r, :])
                        ins.then_inc(s_hTlo, 1)

                def kc_lo():
                    dve.wait_ge(s_kchi, l * 2 + 1)
                    dve.tensor_tensor(kcmp[:, 1, :], SB[0][:, 0:64], kcmp[:, 0, :], ALU.subtract).then_inc(s_kclo, 1)

                def vc_lo():
                    dve.wait_ge(s_kchi, l * 2 + 2)
                    for gr in range(2):
                        for b in range(4):
                            rows, cols = slice(32 * b, 32 * b + 32), slice(64 * (b % 2), 64 * (b % 2) + 64)
                            ins = dve.tensor_tensor(vblk[rows, 1, 2 * gr + b // 2, cols],
                                                    SB[1][rows, 64 * gr:64 * gr + 64],
                                                    vblk[rows, 0, 2 * gr + b // 2, cols], ALU.subtract)
                    ins.then_inc(s_kclo, 1)

                chain.restart()
                dve.tensor_copy(par[:, :], par_all[:, bass.ds(l * NPAR, NPAR)]).then_inc(s_par, 1)
                dve.wait_ge(s_par, l + 1)
                norm_sum(l * 2, PR_ATTN)
                for u, item in enumerate(PREFIX):
                    name, i = item
                    ahead(u)
                    if u == 0:
                        norm_end(l * 2, True)
                    if item in ROPED:
                        r = ROPED.index(item)
                        evac(item, Y[:, 0, :])
                        own(item)
                        chain.mark(dve.tensor_tensor(F[:, 2, :], Y[:, 0, :], cosN, ALU.mult))
                        if 1 <= r <= 4:
                            q_lo(r - 1)
                    if name == "GATE":
                        if i == 8:
                            hidden(0)
                        if i == 9:
                            hidden(1)
                        if i == 10:
                            hidden_lo(1)
                        if i == 11:
                            kc_lo()
                        if i == 12:
                            vc_lo()
                            c_lo()
                        if i > 0:
                            dve.wait_ge(s_gst, l * (16 * NGATE) + 16 * i)
                        evac(item, Y[:, 1, :])
                        if i < 7:
                            rotated(i)
                        if i == 6:
                            blocks(0)
                        if i == 7:
                            blocks_lo(0)
                        if i == 9:
                            dve.wait_ge(s_crms, l + 1)
                            chain.mark(dve.reciprocal(F[:, 3, :], F[:, 3, :]))
                        if i == 10:
                            chain.mark(dve.reciprocal(F[:, 4, :], F[:, 4, :]))
                        if i == 11:
                            c_norm()
                    if name == "VC":
                        evac(item, Y[:, 0, :])
                    if item == ("V", 1):
                        blocks(1)
                    if name == "MISC":
                        v_lo()
                        blocks_lo(1)
                        evac(item, Y[:, 0, :])
                        key_products()
                    if name == "CQ":
                        evac(item, F[:, i, :])
                        if i == 1:
                            nsa_gates()
                            key_sum()
                    if item == ("W1", 1):
                        dve.wait_ge(s_csq, l * 3 + 2)
                        dve.tensor_tensor(F[:, 3, :], F[:, 3, :], F[:, 4, :], ALU.add).then_inc(s_csum, 1)
                    if item == ("W1", 5):
                        hidden_lo(0)
                for i in range(2):
                    dve.wait_ge(s_cs, l * 2 + (i + 1))
                    sc = O[i][:, :].rearrange("p (a n) -> p a n", n=NC)
                    chain.mark(dve.tensor_reduce(small[:, i, 0:16], sc, AX.X, ALU.max, negate=True))
                    chain.wait()
                    dve.tensor_tensor(F[:, 4 + i, :].rearrange("p (a n) -> p a n", n=NC), sc,
                                      small[:, i, 0:16].unsqueeze(2).broadcast_to([P, 16, NC]), ALU.add).then_inc(s_cmax, 1)
                dve.wait_ge(s_gt, l + 1)
                for i in range(2):
                    dve.wait_ge(s_cexp, l * 2 + (i + 1))
                    e4 = F[:, 6 + i, :].rearrange("p (q h n) -> p q h n", q=2, h=HEADS)
                    e3 = F[:, 6 + i, :].rearrange("p (a n) -> p a n", n=NC)
                    m4 = mask01[:, 2 * i:2 * i + 2, :].unsqueeze(2).broadcast_to([P, 2, HEADS, NC])
                    tot = small[:, 2 + i, 0:16]
                    chain.mark(dve.tensor_tensor(e4, e4, m4, ALU.mult))
                    chain.wait()
                    chain.mark(dve.tensor_reduce(tot, e3, AX.X, ALU.add))
                    chain.wait()
                    chain.mark(dve.tensor_scalar(tot, tot, TINY, None, ALU.max))
                    chain.wait()
                    chain.mark(dve.reciprocal(tot, tot))
                    chain.wait()
                    chain.mark(dve.tensor_tensor(tot.rearrange("p (q h) -> p q h", q=2),
                                                 tot.rearrange("p (q h) -> p q h", q=2),
                                                 gt[:, 2 * i:2 * i + 2, 0:HEADS], ALU.mult))
                    chain.wait()
                    dve.tensor_tensor(e3, e3, tot.unsqueeze(2).broadcast_to([P, 16, NC]), ALU.mult).then_inc(s_cw, 1)
                for gr in range(2):
                    dve.wait_ge(s_cThi, l * 2 + (gr + 1))
                    dve.tensor_tensor(pcT[:, gr, 1, :], TP[gr][:, :], pcT[:, gr, 0, :], ALU.subtract).then_inc(s_cTlo, 1)
                dve.wait_ge(s_gst, (l + 1) * (16 * NGATE))
                jobs(l)

                def merged_lo(m):
                    dve.wait_ge(s_mghi, l * KT + (m + 1))
                    rest(H[:, 1, m, :], F[:, 6 + m % 2, :], 0.5, H[:, 0, m, :]).then_inc(s_mglo, 1)

                for m in range(KT):
                    ahead(U_WO + m)
                    dve.wait_ge(s_wused, l * NU + (U_WO + m + 1 + WUSED0))
                    dve.wait_ge(s_gld[m % 2], l * 128 + 32 * (m // 2 + 1))
                    dve.scalar_tensor_tensor(F[:, 4 + m % 2, :], F[:, m % 2, :], 1.0, SB[m % 2][:, :], ALU.add, ALU.mult)
                    dve.scalar_tensor_tensor(F[:, 6 + m % 2, :], F[:, 2 + m % 2, :], 1.0, TP[m % 2][:, :], ALU.add,
                                             ALU.mult).then_inc(s_mab, 1)
                    if m > 0:
                        merged_lo(m - 1)
                    dve.wait_ge(s_mab, l * KT + (m + 1))
                    dve.tensor_tensor(F[:, 6 + m % 2, :], F[:, 6 + m % 2, :], F[:, 4 + m % 2, :], ALU.add)\
                        .then_inc(s_mg, 1)
                merged_lo(KT - 1)
                for m in range(KT):
                    ahead(U_OUT + m)
                    dve.wait_ge(s_wused, l * NU + (U_OUT + m + 1 + WUSED0))
                    dve.tensor_tensor(x[:, m, :], x[:, m, :], G[(G_OUT + m) % 2][:, :], ALU.add).then_inc(s_gfree, 1)
                norm_sum(l * 2 + 1, PR_MLP)
                norm_end(l * 2 + 1, False)
                with dve.Fori(0, QUARTERS) as f:
                    half_f = l * (NU // 2) + f * KT
                    for m in range(2 * KT):
                        split_lo(half_f, U_MLP + m + 1)
                        dve.wait_ge(s_wused, half_f * 2 + (U_MLP + m + 1 + WUSED0))
                        if m < KT:
                            dve.scalar_tensor_tensor(Y[:, m % 2, :], G[m % 2][:, :], 0.0, rs[:, :], ALU.max, ALU.mult)\
                                .then_inc(s_gfree, 1)
                        else:
                            k = m - KT
                            dve.tensor_tensor(x[:, k, :], x[:, k, :], G[m % 2][:, :], ALU.add).then_inc(s_gfree, 1)
                        if m < KT:
                            dve.wait_ge(s_hhi, l * (QUARTERS * KT) + f * KT + (m + 1))
                            dve.wait_ge(s_hsq, l * (QUARTERS * KT) + f * KT + (m + 1))
                            dve.tensor_tensor(H[:, 1, m, :], F[:, m % 2, :], H[:, 0, m, :], ALU.subtract)\
                                .then_inc(s_hlo, 1)
            dve.wait_ge(s_gfree, L * NG + GFREE0)
            norm_sum(L * 2, None)
            norm_end(L * 2, False)
            for m in range(KT):
                dve.scalar_tensor_tensor(final[m], x[:, m, :], par_all[:, L * NPAR + m:L * NPAR + m + 1], rs[:, :],
                                         ALU.mult, ALU.mult).then_inc(s_fin, 1)

        @block.tensor
        def _(pe):
            def three(dst, a, b, first, last, check=False):
                pe.matmul(dst, a(0), b(0), start=first, stop=False, skip_group_check=check)
                pe.matmul(dst, a(0), b(1), start=False, stop=False, skip_group_check=check)
                return pe.matmul(dst, a(1), b(0), start=False, stop=last, skip_group_check=check)

            def wtile(u, k, width=P):
                return lambda c: wsplit[:, u % 2, c, k * width:(k + 1) * width]

            def rows(t, k):
                return lambda c: t[:, c, k, :]

            def tile(dst, u, t, first=None):
                for k in range(KT):
                    if first is not None:
                        first(k)
                    ins = three(dst, wtile(u, k), rows(t, k), k == 0, k == KT - 1)
                ins.then_inc(s_wused, 1)

            def mean_square(n, columns):
                pe.wait_ge(s_sqadd, n * KT + KT)
                if columns:
                    for tt in range(QT):
                        pe.matmul(TP[0][:, tt:tt + 1], F[:, 2, tt * P:(tt + 1) * P], ones[:, 0:1], start=True, stop=True)
                pe.matmul(SB[0][:, :], ones[:, :], F[:, 2, :], start=True, stop=True).then_inc(s_ms, 1)

            pe.sem_inc(s_wused, WUSED0)
            pe.wait_ge(s_init, 4)
            pe.wait_ge(s_const, 80)
            with pe.Fori(0, L) as l:
                def unit(u):
                    pe.wait_ge(s_wlo, l * NU + (u + 1))

                def free(g):
                    pe.wait_ge(s_gfree, l * NG + (g + 1 + GFREE0 - 2))

                def project(g, u, first=None):
                    unit(u)
                    free(g)
                    tile(G[g % 2][:, :], u, xg, first)

                def values_of(hf):
                    unit(UNIT["V", hf])
                    for tt in range(QT):
                        dst = SB[tt // 2][:, 256 * (tt % 2):256 * (tt % 2) + 256]
                        for k in range(4):
                            ins = three(dst, lambda c: xg[:, c, 4 * hf + k, tt * P:(tt + 1) * P],
                                        wtile(UNIT["V", hf], k, 256),
                                        hf == 0 and k == 0 and tt % 2 == 0, hf == 1 and k == 3, True)
                    ins.then_inc(s_wused, 1)

                def gates_T():
                    pe.wait_ge(s_pe1, l + 1)
                    pe.sem_inc(s_carry, 1)
                    for tt in range(QT):
                        ins = pe.transpose(TP[1][:, 24 * tt:24 * tt + 24], Y[0:24, 0, tt * P:(tt + 1) * P],
                                           ident[0:24, 0:24])
                    ins.then_inc(s_tgT, 1)

                def c_mean_squares():
                    pe.wait_ge(s_csum, l + 1)
                    pe.wait_ge(s_csq, l * 3 + 3)
                    pe.matmul(SB[0][:, :], ones[:, :], F[:, 3, :], start=True, stop=True)
                    pe.matmul(SB[1][:, :], ones[:, :], F[:, 5, :], start=True, stop=True).then_inc(s_cms, 1)

                def hidden_T(kind):
                    pe.wait_ge(s_hs, l * 2 + (kind + 1))
                    pe.sem_inc(s_carry, 1)
                    for c in range(2):
                        ins = pe.transpose(TP[kind][:, 64 * c:64 * c + 64],
                                           F[0:64, 7, 256 * kind + P * c:256 * kind + P * c + P], ident[0:64, 0:64])
                    ins.then_inc(s_hT, 1)

                def hidden(i):
                    kind = i // 4
                    if i % 4 == 0:
                        pe.wait_ge(s_tblo, l * 2 + (kind + 1))
                    unit(UNIT["W1", i])
                    for c in range(4):
                        j = 4 * (i % 4) + c
                        ins = three(O[kind][0:64, 0:256], lambda b: TB[:, kind, b, j, :], wtile(UNIT["W1", i], c, 256),
                                    j == 0, j == 15)
                    ins.then_inc(s_wused, 1)

                def compressed_keys():
                    unit(UNIT["W2K", 0])
                    pe.wait_ge(s_hTlo, l * 2 + 1)
                    pe.wait_ge(s_crms, l + 1)
                    for c in range(2):
                        ins = three(SB[0][:, 0:64], wtile(UNIT["W2K", 0], c), lambda b: HK[:, b, c, :], c == 0, c == 1)
                    ins.then_inc(s_wused, 1)

                def compressed_values():
                    unit(UNIT["W2V", 0])
                    pe.wait_ge(s_hTlo, l * 2 + 2)
                    for gr in range(2):
                        for c in range(2):
                            ins = three(SB[1][:, 64 * gr:64 * gr + 64], lambda b: HV[:, b, c, gr, :],
                                        wtile(UNIT["W2V", 0], c, 64), c == 0, c == 1)
                    ins.then_inc(s_wused, 1)

                def compressed_scores():
                    pe.wait_ge(s_kclo, l * 2 + 2)
                    pe.wait_ge(s_rlo, l * 4 + 4)
                    for i in range(2):
                        for q2 in range(2):
                            qt = 2 * i + q2
                            for h in range(HEADS):
                                for c in range(2):
                                    pe.matmul(O[i][:, q2 * 256 + h * NC:q2 * 256 + (h + 1) * NC],
                                              QS[:, h, qt * P:(qt + 1) * P], kcmp[:, c, (h // 4) * NC:(h // 4 + 1) * NC],
                                              start=(q2 == 0 and h == 0 and c == 0), stop=False, skip_group_check=True)
                            ins = pe.matmul(O[i][:, q2 * 256:(q2 + 1) * 256], identb,
                                            cmask[:, qt, :].unsqueeze(1).broadcast_to([P, HEADS, NC]),
                                            start=False, stop=(q2 == 1), skip_group_check=True)
                        ins.then_inc(s_cs, 1)

                def weights_T():
                    pe.wait_ge(s_cw, l * 2 + 2)
                    for gr in range(2):
                        for qt in range(QT):
                            cols = (qt % 2) * 256 + gr * P
                            ins = pe.transpose(TP[gr][:, qt * P:(qt + 1) * P], F[:, 6 + qt // 2, cols:cols + P], ident)
                        ins.then_inc(s_cT, 1)

                for item in PREFIX:
                    name, i = item
                    if name == "V":
                        values_of(i)
                    elif name == "W1":
                        hidden(i)
                    elif name == "W2K":
                        compressed_keys()
                    elif name == "W2V":
                        compressed_values()
                    else:
                        project(TILE[item], UNIT[item],
                                (lambda k: pe.wait_ge(s_xlo, l * 16 + (k + 1))) if item == ("Q", 0) else None)
                    if item == ("Q", 0):
                        mean_square(l * 2, True)
                    if item == ("CQ", 0):
                        gates_T()
                    if item == ("GATE", 8):
                        hidden_T(0)
                        c_mean_squares()
                    if item == ("GATE", 9):
                        hidden_T(1)
                    if item == ("GATE", 12):
                        compressed_scores()
                weights_T()
                def scores(i):
                    t, e, br, qt = JOBS[i]
                    w = (qt + 1) * P
                    dst = SB[i % 2]
                    if i >= 2:
                        pe.wait_ge(s_exp, l * NJ + (i - 1))
                    if i < NSA_NJ:
                        for c in range(2):
                            pe.matmul(dst[:, 0:w], QS[:, 2 * t + e, qt * P:w], KN[:, br, t // 2, c, 0:w],
                                      start=(c == 0), stop=False)
                    else:
                        if qt == 0:
                            pe.wait_ge(s_mlo, l * NMLO + (MLO0[t] + (1 if t < 2 else 0) + e + 1))
                            pe.wait_ge(s_gfree, l * NG + (G_MLA + 4 * t + 3 + GFREE0))
                        three(dst[:, 0:w], lambda c: MQ[:, t % 2, e, c, qt * P:w], lambda c: MK[:, t % 2, e, c, 0:w],
                              True, False)
                    pe.matmul(dst[:, qt * P:w], identb, causal, start=False, stop=True).then_inc(s_scores, 1)

                def turn(j):
                    pe.wait_ge(s_scl, l * NJ + (j + 1))
                    if j >= 2:
                        pe.wait_ge(s_plo, l * NJ + (j - 1))
                    for kt in range(JOBS[j][3] + 1):
                        ins = pe.transpose(TP[j % 2][:, kt * P:(kt + 1) * P], F[:, j % FR, kt * P:(kt + 1) * P], ident)
                    ins.then_inc(s_trans, 1)

                def values(hp, kt):
                    t, e, br, _ = JOBS[hp * QT]
                    nsa, n = hp < NSA_PASSES, output_of(hp * QT)[0]
                    dst = O[n % 2]
                    opens = kt == 0 and (not nsa or (e == 0 and br == 0))
                    if kt == 0:
                        pe.wait_ge(s_plo, l * NJ + (hp * QT + QT))
                        if opens and n >= 2:
                            pe.wait_ge(s_olo, l * NOUT + (n - 1))
                        if opens and not nsa:
                            pe.wait_ge(s_const, 80)
                            pe.wait_ge(s_gfree, l * NG + (G_MLA + 4 * t + 4 + GFREE0))
                        if opens and nsa:
                            three(dst[:, :], lambda c: vblk[:, c, t, :], lambda c: pcT[:, t // 2, c, :], True, False)
                    w = lambda c: PT[:, hp % 2, c, kt * S:(kt + 1) * S - kt * P]
                    if nsa:
                        col = 128 * (t // 2) + (64 if e == 0 else 0)
                        ins = three(dst[:, kt * P:S], lambda c: VN[:, c, br, kt, col:col + P], w, False,
                                    e == 1 and br == 1 and kt == QT - 1)
                    else:
                        col = P * kt + HD * e
                        ins = three(dst[0:HD, kt * P:S], lambda c: MV[t % 2][:, c, col:col + HD], w,
                                    kt == 0, kt == QT - 1, True)
                    if kt == QT - 1:
                        ins.then_inc(s_pv, 1)

                def mla_qk(p):
                    u, g = U_MLA + p, G_MLA + 4 * p
                    unit(u)
                    for e in range(2):
                        free(g + e)
                        for k in range(2):
                            ins = three(G[e][:, :], wtile(u, 2 * k + e), rows(cn, k), k == 0, k == 1)
                        ins.then_inc(s_mready, 1)
                    free(g + 2)
                    three(G[0][:, :], wtile(u, 4), rows(cn, 2), True, True).then_inc(s_mready, 1)

                def mla_v(p):
                    u, g = U_MLA + p, G_MLA + 4 * p
                    free(g + 3)
                    for tt in range(QT):
                        ins = three(G[1][:, tt * P:(tt + 1) * P], lambda c: cn[:, c, 2, tt * P:(tt + 1) * P],
                                    wtile(u, 5), True, True)
                    ins.then_inc(s_wused, 1)

                pe.wait_ge(s_vlo, l + 1)
                pe.wait_ge(s_vz, l + 1)
                pe.wait_ge(s_kl, l * 2 + 2)
                pe.wait_ge(s_cTlo, l * 2 + 2)
                pe.wait_ge(s_clo, l * 3 + 3)
                for i in range(STEPS):
                    if i in QK_STEP:
                        mla_qk(QK_STEP[i])
                    if i in V_STEP:
                        mla_v(V_STEP[i])
                    if i < NJ:
                        scores(i)
                    if i >= LAG_PV and i - LAG_PV < NJ:
                        values((i - LAG_PV) // QT, (i - LAG_PV) % QT)
                    if 0 <= i - LAG_T < NJ:
                        turn(i - LAG_T)
                pe.wait_ge(s_olo, l * NOUT + NOUT)
                for m in range(KT):
                    unit(U_WO + m)
                    if m >= 2:
                        pe.wait_ge(s_mab, l * KT + (m - 1))
                    for k in range(KT):
                        dst = (SB if k < 4 else TP)[m % 2][:, :]
                        ins = three(dst, wtile(U_WO + m, k), rows(xg, k), k % 4 == 0, k % 4 == 3)
                    ins.then_inc(s_wused, 1)
                for m in range(KT):
                    unit(U_OUT + m)
                    free(G_OUT + m)
                    tile(G[m % 2][:, :], U_OUT + m, H,
                         (lambda k: pe.wait_ge(s_mglo, l * KT + (k + 1))) if m == 0 else None)
                mean_square(l * 2 + 1, False)
                with pe.Fori(0, QUARTERS) as f:
                    for m in range(2 * KT):
                        u = U_MLP + m
                        pe.wait_ge(s_wlo, l * NU + f * U_QUARTER + (u + 1))
                        pe.wait_ge(s_gfree, l * NG + f * U_QUARTER + (G_MLP + m + 1 + GFREE0 - 2))
                        if m < KT:
                            tile(G[m % 2][:, :], u, xg, (lambda k: pe.wait_ge(s_xlo, l * 16 + (8 + k + 1))) if m == 0 else None)
                        else:
                            tile(G[m % 2][:, :], u, H,
                                 (lambda k: pe.wait_ge(s_hlo, l * (QUARTERS * KT) + f * KT + (k + 1)))
                                 if m == KT else None)
            mean_square(L * 2, False)


def _columns(w, cols):
    import numpy as np
    w = w[:, cols]
    return np.ascontiguousarray(w.reshape(-1, P, w.shape[1]).transpose(1, 0, 2)).reshape(P, -1)


def _units(w):
    import numpy as np
    r = np.arange
    slabs = np.zeros((L * NU + 2, P, 1024), np.float32)
    for l in range(L):
        n = l * NU
        wi, w1, w2 = w["w_in"][l], w["cmp_w1"][l], w["cmp_w2"][l]

        def put(u, slab):
            slabs[n + u, :, :slab.shape[1]] = slab

        for t in range(4):
            put(UNIT["Q", t], _columns(wi, r(128 * t, 128 * t + 128)))
        put(UNIT["KS", 0], _columns(wi, r(768, 896)))
        put(UNIT["KW", 0], _columns(wi, r(1024, 1152)))
        v = _columns(wi, np.concatenate([r(896, 1024), r(1152, 1280)]))
        put(UNIT["V", 0], v[:, 0:1024])
        put(UNIT["V", 1], v[:, 1024:2048])
        put(UNIT["KC", 0], _columns(wi, r(512, 640)))
        put(UNIT["VC", 0], _columns(wi, r(640, 768)))
        put(UNIT["MISC", 0], _columns(wi, np.concatenate([r(1280, 1304), r(1264, 1304), r(1688, 1720), r(1704, 1720), r(1688, 1704)])))
        for t in range(2):
            put(UNIT["CQ", t], _columns(wi, r(1304 + 128 * t, 1432 + 128 * t)))
        put(UNIT["CQ", 2], _columns(wi, r(1560, 1688)))
        for i in range(2 * KT):
            put(UNIT["GATE", i], _columns(wi, r(1720 + 128 * i, 1848 + 128 * i)))
        for kind in range(2):
            slab = _columns(w1[kind], r(256))
            for i in range(4):
                put(UNIT["W1", 4 * kind + i], slab[:, 1024 * i:1024 * i + 1024])
        put(UNIT["W2K", 0], _columns(w2[0], np.concatenate([r(64), r(64)])))
        put(UNIT["W2V", 0], _columns(w2[1], r(64)))
        for p in range(PAIRS):
            head = np.concatenate([r(96), r(80, 96), r(64, 80)])
            uq = _columns(w["mla_w_uq"][l], np.concatenate([192 * p + head, 192 * p + 96 + head]))
            kv = [256 * p + 128 * e + o + r(64) for o in (0, 64) for e in range(2)]
            put(U_MLA + p, np.concatenate([uq, _columns(w["mla_w_ukv"][l], np.concatenate(kv))], axis=1))
        for m in range(KT):
            c = r(128 * m, 128 * m + 128)
            put(U_WO + m, np.concatenate([_columns(w["nsa_w_o"][l], c), _columns(w["mla_w_o"][l], c)], axis=1))
            put(U_OUT + m, _columns(w["w_out"][l], c))
            for f in range(QUARTERS):
                put(U_MLP + f * U_QUARTER + m, _columns(w["w_up"][l], D * f + c))
                put(U_MLP + f * U_QUARTER + KT + m, _columns(w["w_down"][l][D * f:D * f + D], c))
    return slabs


def _params(w):
    import numpy as np
    cols = []
    for l in range(L):
        for name in ("attn_norm", "mlp_norm", "mla_q_norm", "mla_kv_norm"):
            cols.append(w[name][l].reshape(-1, P).T)
        for kind in range(2):
            cols.append(w["cmp_pe"][l, kind].reshape(16, P).T)
    cols.append(w["final_norm"].reshape(-1, P).T)
    return np.ascontiguousarray(np.concatenate(cols, axis=1))


def _constants():
    import numpy as np

    def angles(d):
        inv = np.float32(10000.0) ** (-np.arange(0, d, 2, dtype=np.float32) / np.float32(d))
        a = np.arange(S, dtype=np.float32)[None, :] * inv.astype(np.float32)[:, None]
        return np.cos(a).astype(np.float32), np.sin(a).astype(np.float32)

    c, s = angles(64)
    cm, sm = angles(32)
    tables = np.stack([np.concatenate([c, c, c, c]), np.concatenate([s, -s, s, -s]),
                       np.concatenate([np.ones((64, S), np.float32), cm, cm, -sm, sm])], axis=1)
    q = np.arange(P)
    seen = (16 * np.arange(NC) + 31)[None, None, :] <= (P * np.arange(QT)[None, :, None] + q[:, None, None])
    seen &= (np.arange(NC) < N_CMP)[None, None, :]
    eye = np.eye(P, dtype=np.float32)
    cf = np.stack([eye, seen.reshape(P, P).astype(np.float32)], axis=1)
    neg = np.float32(-1e30)
    cb = np.stack([eye, np.where(q[None, :] <= q[:, None], 0, neg), np.where(seen.reshape(P, P), 0, neg)], axis=1)
    return np.ascontiguousarray(tables.astype(np.float32)), cf, np.ascontiguousarray(cb.astype(np.float32))


def kernel(**inputs):
    import numpy as np
    import concourse.bacc as bacc
    from concourse import mybir as mb
    from concourse.bass_utils import run_bass_kernel_spmd as run

    w = {k: np.asarray(v) for k, v in inputs.items()}
    tables, cf, cb = _constants()
    arrays = {
        "units": _units(w), "params": _params(w), "tables": tables, "cf32": cf, "cmasks": cb,
        "x_in": np.ascontiguousarray(w["x"][0].T.reshape(KT, P, S).transpose(1, 0, 2)),
    }
    nc = bacc.Bacc("TRN2", target_bir_lowering=False, num_devices=1)
    ins = {k: nc.dram_tensor(k, v.shape, mb.dt.from_np(v.dtype), kind="ExternalInput").ap() for k, v in arrays.items()}
    gates = nc.dram_tensor("gates", (2 * KT, P, S), mb.dt.float32, kind="Internal").ap()
    out = nc.dram_tensor("out", (KT, P, S), mb.dt.float32, kind="ExternalOutput").ap()
    build(nc, ins["units"], ins["params"], ins["x_in"], ins["tables"], ins["cf32"], ins["cmasks"], gates, out)
    r = run(nc, [arrays], core_ids=[0])
    return np.ascontiguousarray(r.results[0]["out"].reshape(D, S).T).reshape(1, S, D)
```

```python
from contextlib import ExitStack

import concourse.bass as bass
from concourse import mybir

F32 = mybir.dt.float32
R32 = mybir.dt.float32r
BF16 = mybir.dt.bfloat16
ACT = mybir.ActivationFunctionType
ALU = mybir.AluOpType
AX = mybir.AxisListType

P = 128
L = 2
S = 512
D = 1024
KT = D // P
QT = S // P
HD = 64
HEADS = 8
PAIRS = HEADS // 2
N_CMP = (S - 32) // 16 + 1
NC = 32
EPS = 1e-6
TINY = 1e-30
NSA_SCALE = HD ** -0.5
MLA_SCALE = 96 ** -0.5

PREFIX = [("Q", 0), ("GATE", 0), ("Q", 1), ("GATE", 1), ("Q", 2), ("GATE", 2), ("Q", 3), ("GATE", 3),
          ("KS", 0), ("GATE", 4), ("KW", 0), ("GATE", 5), ("KC", 0), ("GATE", 6), ("VC", 0), ("GATE", 7), ("V", 0), ("W1", 0), ("V", 1), ("W1", 1),
          ("MISC", 0), ("W1", 2), ("CQ", 0), ("W1", 3), ("CQ", 1), ("W1", 4), ("CQ", 2), ("W1", 5), ("GATE", 8),
          ("W1", 6), ("GATE", 9), ("W1", 7), ("GATE", 10), ("W2K", 0), ("GATE", 11), ("W2V", 0), ("GATE", 12),
          ("GATE", 13), ("GATE", 14), ("GATE", 15)]
UNIT = {item: u for u, item in enumerate(PREFIX)}
U_MLA = len(PREFIX)
U_WO = U_MLA + PAIRS
U_OUT = U_WO + KT
U_MLP = U_OUT + KT
QUARTERS = 4
U_QUARTER = 2 * KT
NU = U_MLP + QUARTERS * U_QUARTER
TILE = {item: g for g, item in enumerate(p for p in PREFIX if p[0] in ("Q", "GATE", "KS", "KW", "KC", "VC", "MISC", "CQ"))}
G_MLA = len(TILE)
G_OUT = G_MLA + 4 * PAIRS
G_MLP = G_OUT + KT
NG = G_MLP + QUARTERS * U_QUARTER
ROPED = [("Q", 0), ("Q", 1), ("Q", 2), ("Q", 3), ("KS", 0), ("KW", 0), ("KC", 0)]
NGATE = 2 * KT
GATE_Y = [1 if i < 8 else i % 2 for i in range(NGATE)]
GATE_N = [GATE_Y[:i].count(GATE_Y[i]) for i in range(NGATE)]
STORES = [GATE_Y.count(0), GATE_Y.count(1)]
BIG = [u for u, item in enumerate(PREFIX) if item[0] not in ("W1", "W2K", "W2V")]
SLOT = {u: BIG.index(u) % 2 if u in BIG else 2 for u in range(U_MLA)}
PREV = {u: max([v for v in range(-2, u) if SLOT.get(v, v % 2) == SLOT[u]], default=-1) for u in range(U_MLA)}
WUSED0 = 2
GFREE0 = KT + 2
PR_ATTN, PR_MLP, PR_QN, PR_KVN, PR_PE, NPAR = 0, 8, 16, 18, 19, 51

NSA_JOBS = [(t, e, br, qt) for t in range(PAIRS) for e in range(2) for br in range(2) for qt in reversed(range(QT))]
MLA_JOBS = [(t, e, 0, qt) for t in range(PAIRS) for e in range(2) for qt in reversed(range(QT))]
JOBS = NSA_JOBS + MLA_JOBS
NJ, NSA_NJ = len(JOBS), len(NSA_JOBS)
NSA_PASSES = NSA_NJ // QT
NHP = NJ // QT
PT_STEP = 384
PT_LEN = 3 * PT_STEP + S
LAG_SUM, LAG_T, LAG_SPLIT, LAG_PV, LAG_O = 1, 3, 4, 6, 7
STEPS = NJ + LAG_O
FR = 4
QK_STEP = {NSA_NJ // 2 + 10: 0, NSA_NJ + 1: 1, NSA_NJ + 9: 2, NSA_NJ + 17: 3}
V_STEP = {NSA_NJ // 2 + 18: 0, NSA_NJ + 7: 1, NSA_NJ + 15: 2, NSA_NJ + 23: 3}
QK_AFTER = [NSA_NJ // 2, NSA_NJ, NSA_NJ + 8, NSA_NJ + 16]
V_AFTER = [5, NSA_PASSES, NSA_PASSES + 2, NSA_PASSES + 4]
MHI0, MLO0 = [0, 5, 10, 14], [0, 3, 6, 8]
NMHI, NMLO = 18, 10
NOUT = PAIRS + HEADS

AREA = 13312


class Chain:

    def __init__(self, eng, sem):
        self.eng, self.sem, self.n = eng, sem, 0

    def restart(self):
        self.eng.sem_clear(self.sem)
        self.n = 0

    def mark(self, ins):
        ins.then_inc(self.sem, 1)
        self.n += 1

    def wait(self):
        self.eng.wait_ge(self.sem, self.n)


def build(nc, units, params, x_in, tables, cf32, cmasks, gates_dram, out):
    ctx = ExitStack()
    with ctx:
        def sb(name, shape, dt):
            return ctx.enter_context(nc.sbuf_tensor(name, shape, dt))

        def bank(name):
            return ctx.enter_context(nc.psum_tensor(name, [P, 512], F32))

        def sem(name):
            return ctx.enter_context(nc.semaphore(name))

        x = sb("x", [P, KT, S], F32)
        stage = sb("stage", [P, 2, 1024], F32)
        wsplit = sb("wsplit", [P, 2, 2, 1024], R32)
        xg = sb("xg", [P, 2, KT, S], R32)
        area = sb("area", [P, AREA], R32)
        area_b = sb("area_b", [P, 2 * 2 * PT_LEN], R32)
        pcT = sb("pcT", [P, 2, 2, S], R32)
        cn = sb("cn", [P, 2, 3, S], R32)
        vblk = sb("vblk", [P, 2, 4, P], R32)
        F = sb("F", [P, 8, S], F32)
        Y = sb("Y", [P, 2, S], F32)
        rs = sb("rs", [P, S], F32)
        kpe = sb("kpe", [P, S], F32)
        rope = sb("rope", [P, 3, S], F32)
        constf = sb("constf", [P, 2, P], F32)
        constb = sb("constb", [P, 3, P], BF16)
        ones = sb("ones", [P, P], F32)
        par_all = sb("par_all", [P, L * NPAR + KT], F32)
        par = sb("par", [P, NPAR], F32)
        nextgain = sb("nextgain", [P, KT], F32)
        rc = sb("rc", [P, 2, QT], F32)
        gt = sb("gt", [P, QT, 24], F32)
        small = sb("small", [P, 4, 17], F32)
        nmx = sb("nmx", [P, 4], F32)
        sums = sb("sums", [P, 4], F32)
        rsum = sb("rsum", [P, 8], F32)

        QS = area[:, 0:4096].rearrange("p (h n) -> p h n", h=HEADS)
        KN = area[:, 4096:8192].rearrange("p (g b c n) -> p b g c n", b=2, g=2, c=2)
        VN = area[:, 8192:13312].rearrange("p (c b t n) -> p c b t n", c=2, b=2, t=QT)
        MQ = area[:, 0:4096].rearrange("p (s e c n) -> p s e c n", s=2, e=2, c=2)
        MK = area[:, 4096:8192].rearrange("p (s e c n) -> p s e c n", s=2, e=2, c=2)
        MV = [pcT[:, 0, :, :], area[:, 8192:9216].rearrange("p (c n) -> p c n", c=2)]
        H = area[:, 0:8192].rearrange("p (c m n) -> p c m n", c=2, m=KT)
        PT = area_b[:, :].rearrange("p (s c n) -> p s c n", s=2, c=2)
        TB = area_b[:, 0:4096].rearrange("p (k c j n) -> p k c j n", k=2, c=2, j=16)
        HK = area_b[:, 4096:4352].rearrange("p (c j n) -> p c j n", c=2, j=2)
        kcmp = area_b[:, S + PT_STEP:S + PT_STEP + 4 * NC].rearrange("p (c n) -> p c n", c=2)
        HV = area_b[:, 4352:5376].rearrange("p (c j g n) -> p c j g n", c=2, j=2, g=2)
        ident, mask01 = constf[:, 0, :], constf[:, 1, :].rearrange("p (q n) -> p q n", q=QT)
        identb, causal = constb[:, 0, :], constb[:, 1, :]
        cmask = constb[:, 2, :].rearrange("p (q n) -> p q n", q=QT)
        cosN, sinN, tabM = rope[:, 0, :], rope[:, 1, :], rope[:, 2, :]

        G = [bank("G0"), bank("G1")]
        SB = [bank("S0"), bank("S1")]
        TP = [bank("T0"), bank("T1")]
        O = [bank("O0"), bank("O1")]

        def sems(*names):
            return [sem(n) for n in names]

        eps = small[:, 0, 16:17]
        tbf = F[:, 0:2, :].rearrange("p a n -> p (a n)")
        final = [F[:, 4, :], F[:, 5, :], F[:, 6, :], F[:, 7, :], F[:, 0, :], F[:, 1, :], Y[:, 0, :], Y[:, 1, :]]

        wslots = [wsplit[:, 0], wsplit[:, 1], pcT[:, :, :, :].rearrange("p g c n -> p g (c n)")]

        def wslot(u):
            return wslots[SLOT.get(u, u % 2)]

        def splits(u):
            if u not in BIG:
                return []
            return [u + 1] if u + 1 not in SLOT or u + 1 in BIG else [u + 1, u + 2]

        def pt_view(slot, c, qt):
            if qt < 3:
                t = PT[:, slot, c, 0:QT * PT_STEP].rearrange("p (k n) -> p k n", n=PT_STEP)
                return t[:, 0:qt + 1, qt * P:(qt + 1) * P]
            t = PT[:, slot, c, P:P + QT * PT_STEP].rearrange("p (k n) -> p k n", n=PT_STEP)
            return t[:, 0:QT, 2 * P:3 * P]

        def tp_view(i, qt):
            return TP[i][:, 0:(qt + 1) * P].rearrange("p (k n) -> p k n", n=P)

        def output_of(j):
            t, e, br, qt = JOBS[j]
            if j < NSA_NJ:
                return t, (e, br, qt) == (1, 1, 0), slice(0, P), slice(0, P), t
            return PAIRS + 2 * t + e, qt == 0, slice(0, HD), slice(HD * e, HD * e + HD), PAIRS + t

        def prob(j, w):
            return F[:, j % FR, 0:w]

        s_const, s_init = sems("s_const", "s_init")
        s_params = sem("s_params")
        s_x = sems("s_x0", "s_x1", "s_x2", "s_x3")
        s_w = sems("s_w0", "s_w1")
        s_whi, s_wlo = sems("s_whi", "s_wlo")
        s_wused = sem("s_wused")
        s_gfree = sem("s_gfree")
        s_par = sem("s_par")
        s_sq, s_sqadd = sems("s_sq", "s_sqadd")
        s_ms, s_rms, s_rs = sems("s_ms", "s_rms", "s_rs")
        s_xhi, s_xlo = sems("s_xhi", "s_xlo")
        s_rot, s_roped = sems("s_rot", "s_roped")
        s_rhi, s_rlo, s_kl = sems("s_rhi", "s_rlo", "s_kl")
        s_vz, s_vhi, s_vlo = sems("s_vz", "s_vhi", "s_vlo")
        s_cc, s_tb, s_tbhi, s_tblo = sems("s_cc", "s_tb", "s_tbhi", "s_tblo")
        s_tgT, s_tg, s_gt = sems("s_tgT", "s_tg", "s_gt")
        s_pe1, s_swap, s_kpe = sems("s_pe1", "s_swap", "s_kpe")
        s_csq, s_csum, s_cms, s_crms = sems("s_csq", "s_csum", "s_cms", "s_crms")
        s_cf, s_chi, s_clo = sems("s_cf", "s_chi", "s_clo")
        s_ty = sem("s_ty")
        s_gst = sems("s_gst0", "s_gst1")
        s_gld = sems("s_gld0", "s_gld1")
        s_ht, s_hs, s_hT, s_hThi, s_hTlo = sems("s_ht", "s_hs", "s_hT", "s_hThi", "s_hTlo")
        s_kchi, s_kclo = sems("s_kchi", "s_kclo")
        s_cs, s_cmax, s_cexp, s_cw = sems("s_cs", "s_cmax", "s_cexp", "s_cw")
        s_cT, s_cThi, s_cTlo = sems("s_cT", "s_cThi", "s_cTlo")
        s_scores, s_max, s_exp, s_rsum, s_scl = sems("s_scores", "s_max", "s_exp", "s_rsum", "s_scl")
        s_trans, s_phi, s_plo = sems("s_trans", "s_phi", "s_plo")
        s_pv = sem("s_pv")
        s_ohi, s_olo = sems("s_ohi", "s_olo")
        s_mready, s_mhi, s_mlo = sems("s_mready", "s_mhi", "s_mlo")
        s_mab, s_mg, s_mghi, s_mglo = sems("s_mab", "s_mg", "s_mghi", "s_mglo")
        s_hsq, s_hhi, s_hlo = sems("s_hsq", "s_hhi", "s_hlo")
        s_fin, s_out = sems("s_fin", "s_out")
        s_stand = sem("s_stand")
        s_carry = sem("s_carry")
        s_dvec = sem("s_dvec")

        block = ctx.enter_context(nc.Block())

        @block.sync
        def _(sp):
            sp.dma_start(stage[:, 0, :], units[0]).then_inc(s_w[0], 16)
            sp.dma_start(stage[:, 1, :], units[1]).then_inc(s_w[1], 16)
            with sp.Fori(1, L * NU // 2 + 1) as i:
                for s in range(2):
                    sp.wait_ge(s_wlo, i * 2 + (s - 1))
                    sp.dma_start(stage[:, s, :], units[bass.ds(i * 2 + s, 1)].rearrange("o p n -> (o p) n"))\
                        .then_inc(s_w[s], 16)
            for m in range(KT):
                sp.wait_ge(s_fin, m + 1)
                sp.dma_start(out[m], final[m]).then_inc(s_out, 16)
            sp.wait_ge(s_w[0], 16 * (L * NU // 2 + 1))
            sp.wait_ge(s_w[1], 16 * (L * NU // 2 + 1))
            sp.wait_ge(s_out, 16 * KT)

        @block.gpsimd
        def _(pool):
            pool.dma_start(par_all[:, :], params).then_inc(s_params, 16)
            pool.dma_start(rope[:, :, :], tables).then_inc(s_const, 16)
            pool.dma_start(constf[:, :, :], cf32).then_inc(s_const, 16)
            pool.dma_start(F[:, 4, 0:3 * P].rearrange("p (c n) -> p c n", c=3), cmasks).then_inc(s_const, 16)
            pool.memset(ones[:, :], 1.0).then_inc(s_init, 1)
            pool.memset(vblk[:, :, :, :].bitcast(F32), 0.0).then_inc(s_init, 1)
            pool.wait_ge(s_const, 48)
            with pool.Fori(0, L) as l:
                pool.wait_ge(s_par, l + 1)
                pool.sem_inc(s_stand, 1)
                for c in range(2):
                    for br in range(2):
                        zeros = VN[:, c, br, :, :].rearrange("p t (z n) -> p t z n", n=HD)
                        ins = pool.memset(zeros[:, :, 0:5:2, :].bitcast(F32), 0.0)
                ins.then_inc(s_vz, 1)
                for item in PREFIX:
                    if item in ROPED:
                        r = ROPED.index(item)
                        pool.wait_ge(s_gfree, l * NG + (TILE[item] + 1 + GFREE0))
                        if r >= 2:
                            pool.wait_ge(s_roped, l * 7 + (r - 1))
                        if r == 0:
                            pool.wait_ge(s_vz, l + 1)
                        elif r == 6:
                            pool.wait_ge(s_kl, l * 2 + 1)
                        for q in range(4):
                            o = q ^ 1
                            ins = pool.tensor_tensor(F[32 * q:32 * q + 32, r % 2, :], Y[32 * o:32 * o + 32, 0, :],
                                                     sinN[32 * o:32 * o + 32, :], ALU.mult)
                        ins.then_inc(s_rot, 1)
                    if item[0] == "GATE":
                        i = item[1]
                        pool.wait_ge(s_ty, l * NGATE + (i + 1))
                        pool.sem_inc(s_stand, 1)
                        pool.dma_start(gates_dram[i], Y[:, GATE_Y[i], :]).then_inc(s_gst[GATE_Y[i]], 16)
                    if item in (("GATE", 5), ("GATE", 6)):
                        r = item[1] - 1
                        pool.wait_ge(s_rot, l * 7 + (r + 2))
                        pool.wait_ge(s_rhi, l * 6 + (r + 1))
                        for gr in range(2):
                            src = F[64 * gr:64 * gr + 64, 3 + r % 2, :]
                            for half in range(2):
                                ins = pool.tensor_tensor(KN[64 * half:64 * half + 64, r - 4, gr, 1, :], src,
                                                         KN[64 * gr:64 * gr + 64, r - 4, gr, 0, :], ALU.subtract)
                        ins.then_inc(s_kl, 1)
                pool.wait_ge(s_rot, l * 7 + 7)
                for j, (t, e, br, qt) in enumerate(JOBS):
                    pool.wait_ge(s_rsum, l * NJ + (j + 1))
                    pool.sem_inc(s_stand, 1)
                    p, col = prob(j, (qt + 1) * P), (1 + br) * HEADS + 2 * t + e
                    gated = j < NSA_NJ
                    pool.tensor_scalar(p, p, rsum[:, j % 8:j % 8 + 1], gt[:, qt, col:col + 1] if gated else None,
                                       ALU.mult, ALU.mult if gated else ALU.bypass).then_inc(s_scl, 1)
                for y in range(2):
                    pool.wait_ge(s_gst[y], (l + 1) * (16 * STORES[y]))
                for m in range(KT):
                    if m < 2:
                        pool.wait_ge(s_plo, l * NJ + NJ)
                    else:
                        pool.wait_ge(s_mab, l * KT + (m - 1))
                    pool.sem_inc(s_stand, 1)
                    pool.dma_start(F[:, m % 2, :], gates_dram[m]).then_inc(s_gld[m % 2], 16)
                    pool.dma_start(F[:, 2 + m % 2, :], gates_dram[KT + m]).then_inc(s_gld[m % 2], 16)
                with pool.Fori(0, QUARTERS) as f:
                    for m in range(KT):
                        pool.wait_ge(s_gfree, l * NG + f * U_QUARTER + (G_MLP + m + 1 + GFREE0))
                        if m >= 2:
                            pool.wait_ge(s_hlo, l * (QUARTERS * KT) + f * KT + (m - 1))
                        pool.tensor_tensor(F[:, m % 2, :], Y[:, m % 2, :], Y[:, m % 2, :], ALU.mult)\
                            .then_inc(s_hsq, 1)

        @block.scalar
        def _(act):
            def split_hi(half, u):
                s = u % 2
                act.wait_ge(s_w[s], half * 16 + (u // 2 + 1) * 16)
                act.wait_ge(s_wused, half * 2 + (PREV.get(u, u - 2) + 1 + WUSED0))
                act.activation(wslot(u)[:, 0, :], stage[:, s, :], ACT.Copy).then_inc(s_whi, 1)

            def square(n, m, x_ready, gain):
                act.wait_ge(s_gfree, x_ready)
                if m >= 2:
                    act.wait_ge(s_sqadd, n * KT + (m - 1))
                act.activation(F[:, m % 2, :], x[:, m, :], ACT.Square).then_inc(s_sq, 1)
                act.activation(xg[:, 0, m, :], x[:, m, :], ACT.Copy, scale=gain).then_inc(s_xhi, 1)

            def root(n, columns):
                act.wait_ge(s_ms, n + 1)
                if columns:
                    act.activation(rc[:, 1, :], TP[0][:, 0:QT], ACT.Sqrt, scale=1.0 / D, bias=eps)
                act.activation(F[:, 3, :], SB[0][:, :], ACT.Sqrt, scale=1.0 / D, bias=eps).then_inc(s_rms, 1)

            def jobs(l):
                for i in range(STEPS):
                    if i in QK_STEP:
                        mla_begin(l, QK_STEP[i])
                    for e in range(2):
                        if i - 2 - e in QK_STEP:
                            mla_q(l, QK_STEP[i - 2 - e], e)
                    if i - 4 in QK_STEP:
                        mla_k(l, QK_STEP[i - 4])
                    if i in V_STEP:
                        mla_v(l, V_STEP[i])
                    j = i - LAG_SPLIT
                    if 0 <= j < NJ:
                        hp, qt = j // QT, JOBS[j][3]
                        act.wait_ge(s_trans, l * NJ + (j + 1))
                        if hp >= 2:
                            act.wait_ge(s_pv, l * NHP + (hp - 1))
                        act.activation(pt_view(hp % 2, 0, qt), tp_view(j % 2, qt), ACT.Copy).then_inc(s_phi, 1)
                    if i < NJ:
                        w = (JOBS[i][3] + 1) * P
                        act.wait_ge(s_max, l * NJ + (i + 1))
                        act.activation(prob(i, w), SB[i % 2][:, 0:w], ACT.Exp, bias=nmx[:, i % 4:i % 4 + 1],
                                       accum_out=sums[:, i % 4:i % 4 + 1]).then_inc(s_exp, 1)
                    if i < 2:
                        act.wait_ge(s_cT, l * 2 + (i + 1))
                        act.activation(pcT[:, i, 0, :], TP[i][:, :], ACT.Copy).then_inc(s_cThi, 1)
                    j = i - LAG_O
                    if j >= 0:
                        n, last, src, dst, tile = output_of(j)
                        if last:
                            act.wait_ge(s_pv, l * NHP + (j // QT + 1))
                            act.activation(xg[dst, 0, tile, :], O[n % 2][src, :], ACT.Copy).then_inc(s_ohi, 1)

            def mla_begin(l, p):
                s = p % 2
                split_hi(l * (NU // 2), U_MLA + p + 1)
                act.wait_ge(s_scores, l * NJ + QK_AFTER[p])
                if p < 2:
                    for e in range(2):
                        ins = act.activation(MK[64:128, s, e, 0, :], kpe[64:128, :], ACT.Copy)
                    ins.then_inc(s_mhi, 1)

            def mla_q(l, p, e):
                act.wait_ge(s_gfree, l * NG + (G_MLA + 4 * p + e + 1 + GFREE0))
                act.activation(MQ[:, p % 2, e, 0, :], Y[:, e, :], ACT.Copy, scale=MLA_SCALE).then_inc(s_mhi, 1)

            def mla_k(l, p):
                act.wait_ge(s_mready, l * 12 + (3 * p + 3))
                for e in range(2):
                    ins = act.activation(MK[0:64, p % 2, e, 0, :], G[0][64 * e:64 * e + 64, :], ACT.Copy)
                ins.then_inc(s_mhi, 1)

            def mla_v(l, p):
                act.wait_ge(s_pv, l * NHP + V_AFTER[p])
                act.wait_ge(s_wused, l * NU + (U_MLA + p + 1 + WUSED0))
                act.activation(MV[p % 2][:, 0, :], G[1][:, :], ACT.Copy).then_inc(s_mhi, 1)

            def gate_tanh(l, i):
                act.wait_ge(s_gfree, l * NG + (TILE["GATE", i] + 1 + GFREE0))
                y = Y[:, GATE_Y[i], :]
                act.activation(y, y, ACT.Tanh, scale=0.5).then_inc(s_ty, 1)

            for i in range(4):
                act.dma_start(x[:, 2 * i:2 * i + 2, :], x_in[:, 2 * i:2 * i + 2, :]).then_inc(s_x[i], 16)
            act.wait_ge(s_params, 16)
            split_hi(0, 0)
            for m in range(KT):
                act.wait_ge(s_x[m // 2], 16)
                square(0, m, GFREE0 - KT + (m + 1), par_all[:, PR_ATTN + m:PR_ATTN + m + 1])
            with act.Fori(0, L) as l:
                half = l * (NU // 2)

                def ahead(u):
                    split_hi(half, u + 1)

                def q_hi(r):
                    act.wait_ge(s_roped, l * 7 + (r + 1))
                    q = F[:, 3 + r % 2, :]
                    act.activation(QS[0:64, 2 * r, :], q[0:64], ACT.Copy, scale=NSA_SCALE)
                    act.activation(QS[64:128, 2 * r + 1, :], q[64:128], ACT.Copy, scale=NSA_SCALE).then_inc(s_rhi, 1)

                def k_hi(br):
                    act.wait_ge(s_roped, l * 7 + (5 + br))
                    for gr in range(2):
                        k = F[64 * gr:64 * gr + 64, 3 + br, :]
                        for hf in range(2):
                            ins = act.activation(KN[64 * hf:64 * hf + 64, br, gr, 0, :], k, ACT.Copy)
                    ins.then_inc(s_rhi, 1)

                def v_hi():
                    act.wait_ge(s_rs, l * 2 + 1)
                    act.wait_ge(s_wused, l * NU + (UNIT["V", 1] + 1 + WUSED0))
                    for tt in range(QT):
                        src = SB[tt // 2][:, 256 * (tt % 2):256 * (tt % 2) + 256]
                        src = src.rearrange("p (b g n) -> p b g n", b=2, g=2)
                        for br in range(2):
                            dst = VN[:, 0, br, tt, :].rearrange("p (z n) -> p z n", n=HD)
                            ins = act.activation(dst[:, 1:4:2, :], src[:, br], ACT.Copy, scale=rc[:, 0, tt:tt + 1])
                    ins.then_inc(s_vhi, 1)

                def copies(kind):
                    if kind == 0:
                        act.wait_ge(s_roped, l * 7 + 7)
                        src = F[:, 3, :]
                    else:
                        act.wait_ge(s_gfree, l * NG + (TILE["VC", 0] + 1 + GFREE0))
                        act.wait_ge(s_tb, l * 2 + 1)
                        src = Y[:, 0, :]
                    for gr in range(2):
                        act.activation(F[0:64, 5 + gr, :], src[64 * gr:64 * gr + 64, :], ACT.Copy)
                        ins = act.activation(F[64:128, 5 + gr, 0:S - 1], src[64 * gr:64 * gr + 64, 1:S], ACT.Copy)
                    ins.then_inc(s_cc, 1)

                def blocks_hi(kind):
                    act.wait_ge(s_tb, l * 2 + (kind + 1))
                    act.activation(TB[:, kind, 0, :, :].rearrange("p j n -> p (j n)"), tbf, ACT.Copy)\
                        .then_inc(s_tbhi, 1)

                def nsa_gates():
                    act.wait_ge(s_tgT, l + 1)
                    act.activation(gt[:, :, :], TP[1][:, 0:QT * 24].rearrange("p (q n) -> p q n", q=QT), ACT.Tanh,
                                   scale=0.5).then_inc(s_tg, 1)

                def swap_key():
                    act.wait_ge(s_pe1, l + 1)
                    act.activation(F[64:96, 4, :], kpe[96:128, :], ACT.Copy)
                    act.activation(F[96:128, 4, :], kpe[64:96, :], ACT.Copy).then_inc(s_swap, 1)

                def c_squares():
                    act.wait_ge(s_gfree, l * NG + (TILE["CQ", 2] + 1 + GFREE0))
                    act.wait_ge(s_kpe, l + 1)
                    for c in range(3):
                        act.activation(F[:, 3 + c, :], F[:, c, :], ACT.Square).then_inc(s_csq, 1)

                def c_roots():
                    act.wait_ge(s_cms, l + 1)
                    act.activation(F[:, 3, :], SB[0][:, :], ACT.Sqrt, scale=1.0 / 256, bias=eps)
                    act.activation(F[:, 6, :], SB[1][:, :], ACT.Sqrt, scale=1.0 / 128, bias=eps).then_inc(s_crms, 1)

                def c_hi():
                    for c in range(3):
                        act.wait_ge(s_cf, l * 3 + (c + 1))
                        act.activation(cn[:, 0, c, :], F[:, c, :], ACT.Copy).then_inc(s_chi, 1)

                def hidden(kind):
                    act.wait_ge(s_wused, l * NU + (UNIT["W1", 4 * kind + 3] + 1 + WUSED0))
                    act.activation(F[0:64, 7, 256 * kind:256 * kind + 256], O[kind][0:64, 0:256], ACT.Tanh, scale=0.5)\
                        .then_inc(s_ht, 1)

                def hidden_hi(kind):
                    act.wait_ge(s_hT, l * 2 + (kind + 1))
                    hT = TP[kind][:, 0:128]
                    if kind == 0:
                        act.activation(HK[:, 0, :, :].rearrange("p j n -> p (j n)"), hT, ACT.Copy, scale=0.5)\
                            .then_inc(s_hThi, 1)
                    else:
                        dst = HV[:, 0, :, :, :].rearrange("p j g (r n) -> p (j g) r n", n=NC)
                        src = hT.rearrange("p (a n) -> p a n", n=NC).unsqueeze(2).broadcast_to([P, 4, 4, NC])
                        act.activation(dst, src, ACT.Copy, scale=0.5).then_inc(s_hThi, 1)

                def kc_hi():
                    act.wait_ge(s_wused, l * NU + (UNIT["W2K", 0] + 1 + WUSED0))
                    act.activation(kcmp[:, 0, :], SB[0][:, 0:64], ACT.Copy).then_inc(s_kchi, 1)

                def vc_hi():
                    act.wait_ge(s_wused, l * NU + (UNIT["W2V", 0] + 1 + WUSED0))
                    for gr in range(2):
                        for b in range(4):
                            dst = vblk[32 * b:32 * b + 32, 0, 2 * gr + b // 2, 64 * (b % 2):64 * (b % 2) + 64]
                            ins = act.activation(dst, SB[1][32 * b:32 * b + 32, 64 * gr:64 * gr + 64], ACT.Copy)
                    ins.then_inc(s_kchi, 1)

                def compressed_exp():
                    for i in range(2):
                        act.wait_ge(s_cmax, l * 2 + (i + 1))
                        act.activation(F[:, 6 + i, :], F[:, 4 + i, :], ACT.Exp).then_inc(s_cexp, 1)

                act.wait_ge(s_par, l + 1)
                for u, (name, i) in enumerate(PREFIX):
                    for v in splits(u):
                        split_hi(half, v)
                    if u == 0:
                        act.wait_ge(s_init, 4)
                        root(l * 2, True)
                    if (name, i) in ROPED[1:5]:
                        q_hi(ROPED.index((name, i)) - 1)
                    if name == "KW":
                        k_hi(0)
                    if name == "KC":
                        k_hi(1)
                    if name == "VC":
                        copies(0)
                    if (name, i) == ("GATE", 7):
                        blocks_hi(0)
                    if (name, i) == ("V", 0):
                        copies(1)
                    if (name, i) == ("MISC", 0):
                        v_hi()
                        blocks_hi(1)
                    if (name, i) == ("CQ", 1):
                        hidden(0)
                        nsa_gates()
                        swap_key()
                    if (name, i) == ("CQ", 2):
                        hidden_hi(0)
                    if (name, i) == ("W1", 5):
                        c_squares()
                    if (name, i) == ("GATE", 9):
                        c_roots()
                    if (name, i) == ("GATE", 10):
                        hidden(1)
                    if (name, i) == ("GATE", 11):
                        hidden_hi(1)
                        kc_hi()
                    if (name, i) == ("GATE", 12):
                        vc_hi()
                    if (name, i) == ("GATE", 13):
                        c_hi()
                    if name == "GATE":
                        gate_tanh(l, i)
                        if i == 13:
                            compressed_exp()
                jobs(l)
                for m in range(KT):
                    ahead(U_WO + m)
                    act.wait_ge(s_mg, l * KT + (m + 1))
                    act.activation(H[:, 0, m, :], F[:, 6 + m % 2, :], ACT.Copy, scale=0.5).then_inc(s_mghi, 1)
                for m in range(KT):
                    ahead(U_OUT + m)
                    square(l * 2 + 1, m, l * NG + (G_OUT + m + 1 + GFREE0), par[:, PR_MLP + m:PR_MLP + m + 1])

                def up(f):
                    for m in range(KT):
                        split_hi(l * (NU // 2) + f * KT, U_MLP + m + 1)
                        if isinstance(f, int) and m == 0:
                            root(l * 2 + 1, False)
                        act.wait_ge(s_gfree, l * NG + f * U_QUARTER + (G_MLP + m + 1 + GFREE0))
                        act.activation(H[:, 0, m, :], Y[:, m % 2, :], ACT.Square).then_inc(s_hhi, 1)

                up(0)
                with act.Fori(0, QUARTERS - 1) as f:
                    for m in range(KT):
                        split_hi(l * (NU // 2) + f * KT, U_MLP + KT + m + 1)
                    up(f + 1)
                for m in range(KT):
                    split_hi(l * (NU // 2) + (QUARTERS - 1) * KT, U_MLP + KT + m + 1)
                    square(l * 2 + 2, m, (l + 1) * NG + (GFREE0 - KT + m + 1), nextgain[:, m:m + 1])
            root(L * 2, False)

        @block.vector
        def _(dve):
            chain = Chain(dve, s_dvec)

            def split_lo(half, u):
                s = u % 2
                dve.wait_ge(s_whi, half * 2 + (u + 1))
                dve.tensor_tensor(wslot(u)[:, 1, :], stage[:, s, :], wslot(u)[:, 0, :], ALU.subtract)\
                    .then_inc(s_wlo, 1)

            def rest(out_ap, full, scale, hi):
                return dve.scalar_tensor_tensor(out_ap, full, scale, hi, ALU.mult, ALU.subtract)

            def norm_sum(n, m, gain):
                dve.wait_ge(s_sq, n * KT + (m + 1))
                if m == 0:
                    dve.tensor_copy(F[:, 2, :], F[:, 0, :]).then_inc(s_sqadd, 1)
                else:
                    dve.wait_ge(s_sqadd, n * KT + m)
                    dve.tensor_tensor(F[:, 2, :], F[:, 2, :], F[:, m % 2, :], ALU.add).then_inc(s_sqadd, 1)
                dve.wait_ge(s_xhi, n * KT + (m + 1))
                rest(xg[:, 1, m, :], x[:, m, :], gain, xg[:, 0, m, :]).then_inc(s_xlo, 1)

            def norm_end(n, columns):
                dve.wait_ge(s_rms, n + 1)
                if columns:
                    dve.reciprocal(rc[:, 0, :], rc[:, 1, :])
                dve.reciprocal(rs[:, :], F[:, 3, :]).then_inc(s_rs, 1)
                dve.wait_ge(s_const, 48)
                dve.wait_ge(s_rs, n + 1)

            def jobs(l):
                for i in range(STEPS):
                    if i in QK_STEP:
                        mla_begin(l, QK_STEP[i])
                    for e in range(2):
                        if i - 1 - e in QK_STEP:
                            mla_rotate(l, QK_STEP[i - 1 - e], e)
                        if i - 3 - e in QK_STEP:
                            mla_q(l, QK_STEP[i - 3 - e], e)
                        if i - 4 - e in QK_STEP:
                            mla_k(l, QK_STEP[i - 4 - e], e)
                    if i in V_STEP:
                        mla_v(l, V_STEP[i])
                    if i < NJ:
                        w = (JOBS[i][3] + 1) * P
                        dve.wait_ge(s_scores, l * NJ + (i + 1))
                        dve.tensor_reduce(nmx[:, i % 4:i % 4 + 1], SB[i % 2][:, 0:w], AX.X, ALU.max, negate=True)\
                            .then_inc(s_max, 1)
                    j = i - LAG_SUM
                    if 0 <= j < NJ:
                        dve.wait_ge(s_exp, l * NJ + (j + 1))
                        dve.reciprocal(rsum[:, j % 8:j % 8 + 1], sums[:, j % 4:j % 4 + 1]).then_inc(s_rsum, 1)
                    if 0 <= j < 2:
                        dve.wait_ge(s_cThi, l * 2 + (j + 1))
                        dve.tensor_tensor(pcT[:, j, 1, :], TP[j][:, :], pcT[:, j, 0, :], ALU.subtract)\
                            .then_inc(s_cTlo, 1)
                    j = i - LAG_SPLIT
                    if 0 <= j < NJ:
                        slot, qt = (j // QT) % 2, JOBS[j][3]
                        dve.wait_ge(s_phi, l * NJ + (j + 1))
                        dve.tensor_tensor(pt_view(slot, 1, qt), tp_view(j % 2, qt), pt_view(slot, 0, qt), ALU.subtract)\
                            .then_inc(s_plo, 1)
                    j = i - LAG_O
                    if j >= 0:
                        n, last, src, dst, tile = output_of(j)
                        if last:
                            dve.wait_ge(s_ohi, l * NOUT + (n + 1))
                            dve.tensor_tensor(xg[dst, 1, tile, :], O[n % 2][src, :], xg[dst, 0, tile, :], ALU.subtract)\
                                .then_inc(s_olo, 1)

            def mla_begin(l, p):
                s = p % 2
                split_lo(l * (NU // 2), U_MLA + p + 1)
                if p < 2:
                    dve.wait_ge(s_mhi, l * NMHI + (MHI0[p] + 1))
                    for e in range(2):
                        ins = dve.tensor_tensor(MK[64:128, s, e, 1, :], kpe[64:128, :], MK[64:128, s, e, 0, :],
                                                ALU.subtract)
                    ins.then_inc(s_mlo, 1)

            def mla_rotate(l, p, e):
                if p == 0:
                    for y in range(2):
                        dve.wait_ge(s_gst[y], (l + 1) * (16 * STORES[y]))
                dve.wait_ge(s_mready, l * 12 + (3 * p + e + 1))
                dve.tensor_tensor(Y[:, e, :], G[e][:, :], tabM, ALU.mult).then_inc(s_gfree, 1)

            def mla_q(l, p, e):
                dve.wait_ge(s_mhi, l * NMHI + (MHI0[p] + (1 if p < 2 else 0) + e + 1))
                rest(MQ[:, p % 2, e, 1, :], Y[:, e, :], MLA_SCALE, MQ[:, p % 2, e, 0, :]).then_inc(s_mlo, 1)

            def mla_k(l, p, e):
                s = p % 2
                dve.wait_ge(s_mhi, l * NMHI + (MHI0[p] + (1 if p < 2 else 0) + 3))
                ins = dve.tensor_tensor(MK[0:64, s, e, 1, :], G[0][64 * e:64 * e + 64, :], MK[0:64, s, e, 0, :],
                                        ALU.subtract)
                if e == 1:
                    ins.then_inc(s_gfree, 1)

            def mla_v(l, p):
                dve.wait_ge(s_mhi, l * NMHI + (MHI0[p] + (5 if p < 2 else 4)))
                dve.tensor_tensor(MV[p % 2][:, 1, :], G[1][:, :], MV[p % 2][:, 0, :], ALU.subtract).then_inc(s_gfree, 1)

            dve.sem_inc(s_gfree, GFREE0)
            dve.memset(eps, EPS).then_inc(s_init, 1)
            dve.wait_ge(s_params, 16)
            split_lo(0, 0)
            for m in range(KT):
                norm_sum(0, m, par_all[:, PR_ATTN + m:PR_ATTN + m + 1])
            dve.wait_ge(s_const, 48)
            dve.tensor_copy(constb[:, :, :].rearrange("p c n -> p (c n)"), F[:, 4, 0:3 * P]).then_inc(s_init, 1)
            with dve.Fori(0, L) as l:
                half = l * (NU // 2)

                def ahead(u):
                    split_lo(half, u + 1)

                def evac(item, dst):
                    dve.wait_ge(s_wused, l * NU + (UNIT[item] + 1 + WUSED0))
                    dve.tensor_tensor(dst, G[TILE[item] % 2][:, :], rs[:, :], ALU.mult).then_inc(s_gfree, 1)

                def own(item):
                    dve.wait_ge(s_gfree, l * NG + (TILE[item] + 1 + GFREE0))

                def q_lo(r):
                    dve.wait_ge(s_rhi, l * 6 + (r + 1))
                    q = F[:, 3 + r % 2, :]
                    rest(QS[64:128, 2 * r, :], q[0:64], NSA_SCALE, QS[0:64, 2 * r, :])
                    rest(QS[0:64, 2 * r + 1, :], q[64:128], NSA_SCALE, QS[64:128, 2 * r + 1, :]).then_inc(s_rlo, 1)

                def rotated(r):
                    dve.wait_ge(s_rot, l * 7 + (r + 1))
                    if r == 6:
                        dve.wait_ge(s_kl, l * 2 + 1)
                    chain.wait()
                    dve.tensor_tensor(F[:, 3 + r % 2, :], F[:, 2, :], F[:, r % 2, :], ALU.add).then_inc(s_roped, 1)

                def v_lo():
                    dve.wait_ge(s_vhi, l + 1)
                    for tt in range(QT):
                        src = SB[tt // 2][:, 256 * (tt % 2):256 * (tt % 2) + 256]
                        src = src.rearrange("p (b g n) -> p b g n", b=2, g=2)
                        for br in range(2):
                            hi = VN[:, 0, br, tt, :].rearrange("p (z n) -> p z n", n=HD)[:, 1:4:2, :]
                            lo = VN[:, 1, br, tt, :].rearrange("p (z n) -> p z n", n=HD)[:, 1:4:2, :]
                            ins = rest(lo, src[:, br], rc[:, 0, tt:tt + 1], hi)
                    ins.then_inc(s_vlo, 1)

                def blocks(kind):
                    dve.wait_ge(s_cc, l * 2 + (kind + 1))
                    if kind == 1:
                        dve.wait_ge(s_tblo, l * 2 + 1)
                    tb = tbf.rearrange("p (j g n) -> p j g n", j=16, g=2)
                    dve.memset(tb[:, :, :, N_CMP:NC], 0.0)
                    tok = F[:, 5:7, :].rearrange("p g (n r) -> p r g n", r=16)[:, 0:16:2]
                    for hf in range(2):
                        pe = par[:, PR_PE + 16 * kind + 8 * hf:PR_PE + 16 * kind + 8 * hf + 8]
                        pe = pe.unsqueeze(2).unsqueeze(3).broadcast_to([P, 8, 2, N_CMP])
                        ins = dve.tensor_tensor(tb[:, 8 * hf:8 * hf + 8, :, 0:N_CMP], tok[:, :, :, hf:hf + N_CMP], pe,
                                                ALU.add)
                    ins.then_inc(s_tb, 1)

                def blocks_lo(kind):
                    dve.wait_ge(s_tbhi, l * 2 + (kind + 1))
                    dve.tensor_tensor(TB[:, kind, 1, :, :].rearrange("p j n -> p (j n)"), tbf,
                                      TB[:, kind, 0, :, :].rearrange("p j n -> p (j n)"), ALU.subtract)\
                        .then_inc(s_tblo, 1)

                def key_products():
                    own(("MISC", 0))
                    dve.wait_ge(s_kl, l * 2 + 2)
                    dve.tensor_tensor(kpe[64:128, :], Y[64:128, 0, :], tabM[64:128, :], ALU.mult).then_inc(s_pe1, 1)

                def key_sum():
                    dve.wait_ge(s_swap, l + 1)
                    dve.tensor_tensor(kpe[64:128, :], kpe[64:128, :], F[64:128, 4, :], ALU.add).then_inc(s_kpe, 1)

                def nsa_gates():
                    dve.wait_ge(s_tg, l + 1)
                    dve.tensor_scalar(gt[:, :, :], gt[:, :, :], 0.5, 0.5, ALU.mult, ALU.add).then_inc(s_gt, 1)

                def c_reciprocal(tile, half):
                    dve.wait_ge(s_crms, l + 1)
                    piece = F[:, tile, S // 2 * half:S // 2 * (half + 1)]
                    chain.mark(dve.reciprocal(piece, piece))

                def c_norm():
                    chain.wait()
                    for c in range(3):
                        gain = par[:, PR_QN + c:PR_QN + c + 1]
                        dve.scalar_tensor_tensor(F[:, c, :], F[:, c, :], gain, F[:, 3 + 3 * (c // 2), :],
                                                 ALU.mult, ALU.mult).then_inc(s_cf, 1)

                def c_lo():
                    for c in range(3):
                        dve.wait_ge(s_chi, l * 3 + (c + 1))
                        dve.tensor_tensor(cn[:, 1, c, :], F[:, c, :], cn[:, 0, c, :], ALU.subtract).then_inc(s_clo, 1)

                def hidden(kind):
                    h = F[0:64, 7, 256 * kind:256 * kind + 256]
                    dve.wait_ge(s_ht, l * 2 + (kind + 1))
                    dve.scalar_tensor_tensor(h, h, 1.0, O[kind][0:64, 0:256], ALU.add, ALU.mult).then_inc(s_hs, 1)

                def hidden_lo(kind):
                    dve.wait_ge(s_hThi, l * 2 + (kind + 1))
                    hT = TP[kind][:, 0:128]
                    if kind == 0:
                        rest(HK[:, 1, :, :].rearrange("p j n -> p (j n)"), hT, 0.5,
                             HK[:, 0, :, :].rearrange("p j n -> p (j n)")).then_inc(s_hTlo, 1)
                    else:
                        hi = HV[:, 0, :, :, :].rearrange("p j g (r n) -> p (j g) r n", n=NC)
                        lo = HV[:, 1, :, :, :].rearrange("p j g (r n) -> p (j g) r n", n=NC)
                        for r in range(4):
                            ins = rest(lo[:, :, r, :], hT.rearrange("p (a n) -> p a n", n=NC), 0.5, hi[:, :, r, :])
                        ins.then_inc(s_hTlo, 1)

                def kc_lo():
                    dve.wait_ge(s_kchi, l * 2 + 1)
                    dve.tensor_tensor(kcmp[:, 1, :], SB[0][:, 0:64], kcmp[:, 0, :], ALU.subtract).then_inc(s_kclo, 1)

                def vc_lo():
                    dve.wait_ge(s_kchi, l * 2 + 2)
                    for gr in range(2):
                        for b in range(4):
                            rows, cols = slice(32 * b, 32 * b + 32), slice(64 * (b % 2), 64 * (b % 2) + 64)
                            ins = dve.tensor_tensor(vblk[rows, 1, 2 * gr + b // 2, cols],
                                                    SB[1][rows, 64 * gr:64 * gr + 64],
                                                    vblk[rows, 0, 2 * gr + b // 2, cols], ALU.subtract)
                    ins.then_inc(s_kclo, 1)

                def compressed_max():
                    for i in range(2):
                        dve.wait_ge(s_cs, l * 2 + (i + 1))
                        sc = O[i][:, :].rearrange("p (a n) -> p a n", n=NC)
                        chain.mark(dve.tensor_reduce(small[:, i, 0:16], sc, AX.X, ALU.max, negate=True))
                        chain.wait()
                        dve.tensor_tensor(F[:, 4 + i, :].rearrange("p (a n) -> p a n", n=NC), sc,
                                          small[:, i, 0:16].unsqueeze(2).broadcast_to([P, 16, NC]), ALU.add).then_inc(s_cmax, 1)

                def compressed_weights():
                    dve.wait_ge(s_gt, l + 1)
                    for i in range(2):
                        dve.wait_ge(s_cexp, l * 2 + (i + 1))
                        e4 = F[:, 6 + i, :].rearrange("p (q h n) -> p q h n", q=2, h=HEADS)
                        e3 = F[:, 6 + i, :].rearrange("p (a n) -> p a n", n=NC)
                        m4 = mask01[:, 2 * i:2 * i + 2, :].unsqueeze(2).broadcast_to([P, 2, HEADS, NC])
                        tot = small[:, 2 + i, 0:16]
                        chain.mark(dve.tensor_tensor(e4, e4, m4, ALU.mult))
                        chain.wait()
                        chain.mark(dve.tensor_reduce(tot, e3, AX.X, ALU.add))
                        chain.wait()
                        chain.mark(dve.tensor_scalar(tot, tot, TINY, None, ALU.max))
                        chain.wait()
                        chain.mark(dve.reciprocal(tot, tot))
                        chain.wait()
                        chain.mark(dve.tensor_tensor(tot.rearrange("p (q h) -> p q h", q=2),
                                                     tot.rearrange("p (q h) -> p q h", q=2),
                                                     gt[:, 2 * i:2 * i + 2, 0:HEADS], ALU.mult))
                        chain.wait()
                        dve.tensor_tensor(e3, e3, tot.unsqueeze(2).broadcast_to([P, 16, NC]), ALU.mult).then_inc(s_cw, 1)

                chain.restart()
                dve.wait_ge(s_xlo, l * 16 + 8)
                dve.tensor_copy(nextgain[:, :], par_all[:, bass.ds(l * NPAR + NPAR, KT)])
                dve.tensor_copy(par[:, :], par_all[:, bass.ds(l * NPAR, NPAR)]).then_inc(s_par, 1)
                dve.wait_ge(s_par, l + 1)
                for u, item in enumerate(PREFIX):
                    name, i = item
                    for v in splits(u):
                        split_lo(half, v)
                    if u == 0:
                        norm_end(l * 2, True)
                    if item in ROPED:
                        r = ROPED.index(item)
                        evac(item, Y[:, 0, :])
                        own(item)
                        chain.mark(dve.tensor_tensor(F[:, 2, :], Y[:, 0, :], cosN, ALU.mult))
                        if 1 <= r <= 4:
                            q_lo(r - 1)
                    if name == "GATE":
                        if i == 8:
                            dve.wait_ge(s_csq, l * 3 + 2)
                            dve.tensor_tensor(F[:, 3, :], F[:, 3, :], F[:, 4, :], ALU.add).then_inc(s_csum, 1)
                        if i == 10:
                            hidden(1)
                        if i == 11:
                            hidden_lo(1)
                            kc_lo()
                        if i == 13:
                            compressed_max()
                        if i == 14:
                            compressed_weights()
                        if i == 12:
                            vc_lo()
                        y, before = GATE_Y[i], GATE_N[i]
                        if before > 0:
                            dve.wait_ge(s_gst[y], l * (16 * STORES[y]) + 16 * before)
                        evac(item, Y[:, y, :])
                        if i < 7:
                            rotated(i)
                        if i == 7:
                            blocks_lo(0)
                        if i == 9:
                            c_reciprocal(3, 0)
                        if i == 10:
                            c_reciprocal(3, 1)
                        if i == 11:
                            c_reciprocal(6, 1)
                        if i == 12:
                            c_norm()
                        if i == 13:
                            c_lo()
                    if name == "W2K":
                        c_reciprocal(6, 0)
                    if name == "VC":
                        blocks(0)
                        evac(item, Y[:, 0, :])
                    if item == ("V", 1):
                        blocks(1)
                    if name == "MISC":
                        v_lo()
                        blocks_lo(1)
                        evac(item, Y[:, 0, :])
                        key_products()
                    if name == "CQ":
                        if i == 1:
                            hidden(0)
                        if i == 2:
                            hidden_lo(0)
                        evac(item, F[:, i, :])
                        if i == 1:
                            nsa_gates()
                            key_sum()
                jobs(l)

                def merged_lo(m):
                    dve.wait_ge(s_mghi, l * KT + (m + 1))
                    rest(H[:, 1, m, :], F[:, 6 + m % 2, :], 0.5, H[:, 0, m, :]).then_inc(s_mglo, 1)

                for m in range(KT):
                    ahead(U_WO + m)
                    dve.wait_ge(s_wused, l * NU + (U_WO + m + 1 + WUSED0))
                    dve.wait_ge(s_gld[m % 2], l * 128 + 32 * (m // 2 + 1))
                    dve.scalar_tensor_tensor(F[:, 4 + m % 2, :], F[:, m % 2, :], 1.0, SB[m % 2][:, :], ALU.add, ALU.mult)
                    dve.scalar_tensor_tensor(F[:, 6 + m % 2, :], F[:, 2 + m % 2, :], 1.0, TP[m % 2][:, :], ALU.add,
                                             ALU.mult).then_inc(s_mab, 1)
                    if m > 0:
                        merged_lo(m - 1)
                    dve.wait_ge(s_mab, l * KT + (m + 1))
                    dve.tensor_tensor(F[:, 6 + m % 2, :], F[:, 6 + m % 2, :], F[:, 4 + m % 2, :], ALU.add)\
                        .then_inc(s_mg, 1)
                merged_lo(KT - 1)
                for m in range(KT):
                    ahead(U_OUT + m)
                    dve.wait_ge(s_wused, l * NU + (U_OUT + m + 1 + WUSED0))
                    dve.tensor_tensor(x[:, m, :], x[:, m, :], G[(G_OUT + m) % 2][:, :], ALU.add).then_inc(s_gfree, 1)
                    norm_sum(l * 2 + 1, m, par[:, PR_MLP + m:PR_MLP + m + 1])

                def up(f):
                    for m in range(KT):
                        split_lo(l * (NU // 2) + f * KT, U_MLP + m + 1)
                        if isinstance(f, int) and m == 0:
                            norm_end(l * 2 + 1, False)
                        dve.wait_ge(s_wused, l * NU + f * U_QUARTER + (U_MLP + m + 1 + WUSED0))
                        dve.scalar_tensor_tensor(Y[:, m % 2, :], G[m % 2][:, :], 0.0, rs[:, :], ALU.max, ALU.mult)\
                            .then_inc(s_gfree, 1)
                        dve.wait_ge(s_hhi, l * (QUARTERS * KT) + f * KT + (m + 1))
                        dve.wait_ge(s_hsq, l * (QUARTERS * KT) + f * KT + (m + 1))
                        dve.tensor_tensor(H[:, 1, m, :], F[:, m % 2, :], H[:, 0, m, :], ALU.subtract).then_inc(s_hlo, 1)

                def down(f, k):
                    split_lo(l * (NU // 2) + f * KT, U_MLP + KT + k + 1)
                    dve.wait_ge(s_wused, l * NU + f * U_QUARTER + (U_MLP + KT + k + 1 + WUSED0))
                    dve.tensor_tensor(x[:, k, :], x[:, k, :], G[k % 2][:, :], ALU.add).then_inc(s_gfree, 1)

                up(0)
                with dve.Fori(0, QUARTERS - 1) as f:
                    for k in range(KT):
                        down(f, k)
                    up(f + 1)
                for k in range(KT):
                    down(QUARTERS - 1, k)
                    norm_sum(l * 2 + 2, k, nextgain[:, k:k + 1])
            norm_end(L * 2, False)
            for m in range(KT):
                dve.scalar_tensor_tensor(final[m], x[:, m, :], par_all[:, L * NPAR + m:L * NPAR + m + 1], rs[:, :],
                                         ALU.mult, ALU.mult).then_inc(s_fin, 1)

        @block.tensor
        def _(pe):
            def three(dst, a, b, first, last, check=False):
                pe.matmul(dst, a(0), b(0), start=first, stop=False, skip_group_check=check)
                pe.matmul(dst, a(0), b(1), start=False, stop=False, skip_group_check=check)
                return pe.matmul(dst, a(1), b(0), start=False, stop=last, skip_group_check=check)

            def wtile(u, k, width=P):
                return lambda c: wslot(u)[:, c, k * width:(k + 1) * width]

            def rows(t, k):
                return lambda c: t[:, c, k, :]

            def tile(dst, u, t, first=None):
                for k in range(KT):
                    if first is not None:
                        first(k)
                    ins = three(dst, wtile(u, k), rows(t, k), k == 0, k == KT - 1)
                ins.then_inc(s_wused, 1)

            def mean_square(n, columns):
                pe.wait_ge(s_sqadd, n * KT + KT)
                if columns:
                    for tt in range(QT):
                        pe.matmul(TP[0][:, tt:tt + 1], F[:, 2, tt * P:(tt + 1) * P], ones[:, 0:1], start=True, stop=True)
                pe.matmul(SB[0][:, :], ones[:, :], F[:, 2, :], start=True, stop=True).then_inc(s_ms, 1)

            pe.sem_inc(s_wused, WUSED0)
            with pe.Fori(0, L) as l:
                def unit(u):
                    pe.wait_ge(s_wlo, l * NU + (u + 1))

                def free(g):
                    pe.wait_ge(s_gfree, l * NG + (g + 1 + GFREE0 - 2))

                def project(g, u, first=None):
                    unit(u)
                    free(g)
                    tile(G[g % 2][:, :], u, xg, first)

                def values_of(hf):
                    unit(UNIT["V", hf])
                    for tt in range(QT):
                        dst = SB[tt // 2][:, 256 * (tt % 2):256 * (tt % 2) + 256]
                        for k in range(4):
                            ins = three(dst, lambda c: xg[:, c, 4 * hf + k, tt * P:(tt + 1) * P],
                                        wtile(UNIT["V", hf], k, 256),
                                        hf == 0 and k == 0 and tt % 2 == 0, hf == 1 and k == 3, True)
                    ins.then_inc(s_wused, 1)

                def gates_T():
                    pe.wait_ge(s_pe1, l + 1)
                    pe.sem_inc(s_carry, 1)
                    for tt in range(QT):
                        ins = pe.transpose(TP[1][:, 24 * tt:24 * tt + 24], Y[0:24, 0, tt * P:(tt + 1) * P],
                                           ident[0:24, 0:24])
                    ins.then_inc(s_tgT, 1)

                def c_mean_squares():
                    pe.wait_ge(s_csum, l + 1)
                    pe.wait_ge(s_csq, l * 3 + 3)
                    pe.matmul(SB[0][:, :], ones[:, :], F[:, 3, :], start=True, stop=True)
                    pe.matmul(SB[1][:, :], ones[:, :], F[:, 5, :], start=True, stop=True).then_inc(s_cms, 1)

                def hidden_T(kind):
                    pe.wait_ge(s_hs, l * 2 + (kind + 1))
                    pe.sem_inc(s_carry, 1)
                    for c in range(2):
                        ins = pe.transpose(TP[kind][:, 64 * c:64 * c + 64],
                                           F[0:64, 7, 256 * kind + P * c:256 * kind + P * c + P], ident[0:64, 0:64])
                    ins.then_inc(s_hT, 1)

                def hidden(i):
                    kind = i // 4
                    if i % 4 == 0:
                        pe.wait_ge(s_tblo, l * 2 + (kind + 1))
                    unit(UNIT["W1", i])
                    for c in range(4):
                        j = 4 * (i % 4) + c
                        ins = three(O[kind][0:64, 0:256], lambda b: TB[:, kind, b, j, :], wtile(UNIT["W1", i], c, 256),
                                    j == 0, j == 15)
                    ins.then_inc(s_wused, 1)

                def compressed_keys():
                    unit(UNIT["W2K", 0])
                    pe.wait_ge(s_hTlo, l * 2 + 1)
                    pe.wait_ge(s_crms, l + 1)
                    for c in range(2):
                        ins = three(SB[0][:, 0:64], wtile(UNIT["W2K", 0], c), lambda b: HK[:, b, c, :], c == 0, c == 1)
                    ins.then_inc(s_wused, 1)

                def compressed_values():
                    unit(UNIT["W2V", 0])
                    pe.wait_ge(s_hTlo, l * 2 + 2)
                    for gr in range(2):
                        for c in range(2):
                            ins = three(SB[1][:, 64 * gr:64 * gr + 64], lambda b: HV[:, b, c, gr, :],
                                        wtile(UNIT["W2V", 0], c, 64), c == 0, c == 1)
                    ins.then_inc(s_wused, 1)

                def compressed_scores():
                    pe.wait_ge(s_kclo, l * 2 + 2)
                    pe.wait_ge(s_rlo, l * 4 + 4)
                    for i in range(2):
                        for q2 in range(2):
                            qt = 2 * i + q2
                            for h in range(HEADS):
                                for c in range(2):
                                    pe.matmul(O[i][:, q2 * 256 + h * NC:q2 * 256 + (h + 1) * NC],
                                              QS[:, h, qt * P:(qt + 1) * P], kcmp[:, c, (h // 4) * NC:(h // 4 + 1) * NC],
                                              start=(q2 == 0 and h == 0 and c == 0), stop=False, skip_group_check=True)
                            ins = pe.matmul(O[i][:, q2 * 256:(q2 + 1) * 256], identb,
                                            cmask[:, qt, :].unsqueeze(1).broadcast_to([P, HEADS, NC]),
                                            start=False, stop=(q2 == 1), skip_group_check=True)
                        ins.then_inc(s_cs, 1)

                def weights_T():
                    pe.wait_ge(s_cw, l * 2 + 2)
                    for gr in range(2):
                        for qt in range(QT):
                            cols = (qt % 2) * 256 + gr * P
                            ins = pe.transpose(TP[gr][:, qt * P:(qt + 1) * P], F[:, 6 + qt // 2, cols:cols + P], ident)
                        ins.then_inc(s_cT, 1)

                for item in PREFIX:
                    name, i = item
                    if name == "V":
                        values_of(i)
                    elif name == "W1":
                        hidden(i)
                    elif name == "W2K":
                        compressed_keys()
                    elif name == "W2V":
                        compressed_values()
                    else:
                        project(TILE[item], UNIT[item],
                                (lambda k: pe.wait_ge(s_xlo, l * 16 + (k + 1))) if item == ("Q", 0) else None)
                    if item == ("Q", 0):
                        pe.wait_ge(s_init, 4)
                        pe.wait_ge(s_const, 48)
                        mean_square(l * 2, True)
                    if item == ("CQ", 0):
                        gates_T()
                    if item == ("CQ", 1):
                        hidden_T(0)
                    if item == ("GATE", 8):
                        c_mean_squares()
                    if item == ("GATE", 10):
                        hidden_T(1)
                    if item == ("GATE", 12):
                        compressed_scores()
                weights_T()
                def scores(i):
                    t, e, br, qt = JOBS[i]
                    w = (qt + 1) * P
                    dst = SB[i % 2]
                    if i >= 2:
                        pe.wait_ge(s_exp, l * NJ + (i - 1))
                    if i < NSA_NJ:
                        for c in range(2):
                            pe.matmul(dst[:, 0:w], QS[:, 2 * t + e, qt * P:w], KN[:, br, t // 2, c, 0:w],
                                      start=(c == 0), stop=False)
                    else:
                        if qt == QT - 1:
                            pe.wait_ge(s_mlo, l * NMLO + (MLO0[t] + (1 if t < 2 else 0) + e + 1))
                            pe.wait_ge(s_gfree, l * NG + (G_MLA + 4 * t + 3 + GFREE0))
                        three(dst[:, 0:w], lambda c: MQ[:, t % 2, e, c, qt * P:w], lambda c: MK[:, t % 2, e, c, 0:w],
                              True, False)
                    pe.matmul(dst[:, qt * P:w], identb, causal, start=False, stop=True).then_inc(s_scores, 1)

                def turn(j):
                    if j == 0:
                        pe.wait_ge(s_cTlo, l * 2 + 2)
                    pe.wait_ge(s_scl, l * NJ + (j + 1))
                    if j >= 2:
                        pe.wait_ge(s_plo, l * NJ + (j - 1))
                    for kt in range(JOBS[j][3] + 1):
                        ins = pe.transpose(TP[j % 2][:, kt * P:(kt + 1) * P], F[:, j % FR, kt * P:(kt + 1) * P], ident)
                    ins.then_inc(s_trans, 1)

                def values(j):
                    t, e, br, kt = JOBS[j]
                    nsa, n, slot = j < NSA_NJ, output_of(j)[0], (j // QT) % 2
                    dst = O[n % 2]
                    opens = kt == QT - 1 and (not nsa or (e == 0 and br == 0))
                    pe.wait_ge(s_plo, l * NJ + (j + 1))
                    if opens and n >= 2:
                        pe.wait_ge(s_olo, l * NOUT + (n - 1))
                    if opens and not nsa:
                        pe.wait_ge(s_gfree, l * NG + (G_MLA + 4 * t + 4 + GFREE0))
                        pe.sem_inc(s_carry, 1)
                    if opens and nsa:
                        three(dst[:, :], lambda c: vblk[:, c, t, :], lambda c: pcT[:, t // 2, c, :], True, False)
                    w = lambda c: PT[:, slot, c, kt * S:(kt + 1) * S - kt * P]
                    if nsa:
                        col = 128 * (t // 2) + (64 if e == 0 else 0)
                        ins = three(dst[:, kt * P:S], lambda c: VN[:, c, br, kt, col:col + P], w, False,
                                    e == 1 and br == 1 and kt == 0)
                    else:
                        if not opens:
                            pe.sem_inc(s_carry, 1)
                        col = P * kt + HD * e
                        ins = three(dst[0:HD, kt * P:S], lambda c: MV[t % 2][:, c, col:col + HD], w, opens, kt == 0, True)
                    if kt == 0:
                        ins.then_inc(s_pv, 1)

                def mla_q(p):
                    u, g = U_MLA + p, G_MLA + 4 * p
                    pe.wait_ge(s_clo, l * 3 + 3)
                    unit(u)
                    for e in range(2):
                        free(g + e)
                        for k in range(2):
                            ins = three(G[e][:, :], wtile(u, 2 * k + e), rows(cn, k), k == 0, k == 1)
                        ins.then_inc(s_mready, 1)

                def mla_k(p):
                    free(G_MLA + 4 * p + 2)
                    three(G[0][:, :], wtile(U_MLA + p, 4), rows(cn, 2), True, True).then_inc(s_mready, 1)

                def mla_v(p):
                    u, g = U_MLA + p, G_MLA + 4 * p
                    free(g + 3)
                    for tt in range(QT):
                        ins = three(G[1][:, tt * P:(tt + 1) * P], lambda c: cn[:, c, 2, tt * P:(tt + 1) * P],
                                    wtile(u, 5), True, True)
                    ins.then_inc(s_wused, 1)

                pe.wait_ge(s_vlo, l + 1)
                pe.wait_ge(s_vz, l + 1)
                pe.wait_ge(s_kl, l * 2 + 2)
                for i in range(STEPS):
                    if i in QK_STEP:
                        mla_q(QK_STEP[i])
                    if i - 2 in QK_STEP:
                        mla_k(QK_STEP[i - 2])
                    if i in V_STEP:
                        mla_v(V_STEP[i])
                    if i < NJ:
                        scores(i)
                    if i >= LAG_PV and i - LAG_PV < NJ:
                        values(i - LAG_PV)
                    if 0 <= i - LAG_T < NJ:
                        turn(i - LAG_T)
                pe.wait_ge(s_olo, l * NOUT + NOUT)
                for m in range(KT):
                    unit(U_WO + m)
                    if m >= 2:
                        pe.wait_ge(s_mab, l * KT + (m - 1))
                    for k in range(KT):
                        dst = (SB if k < 4 else TP)[m % 2][:, :]
                        ins = three(dst, wtile(U_WO + m, k), rows(xg, k), k % 4 == 0, k % 4 == 3)
                    ins.then_inc(s_wused, 1)
                for m in range(KT):
                    unit(U_OUT + m)
                    free(G_OUT + m)
                    tile(G[m % 2][:, :], U_OUT + m, H,
                         (lambda k: pe.wait_ge(s_mglo, l * KT + (k + 1))) if m == 0 else None)

                def up(f):
                    for m in range(KT):
                        u = U_MLP + m
                        pe.wait_ge(s_wlo, l * NU + f * U_QUARTER + (u + 1))
                        pe.wait_ge(s_gfree, l * NG + f * U_QUARTER + (G_MLP + m + 1 + GFREE0 - 2))
                        tile(G[m % 2][:, :], u, xg,
                             (lambda k: pe.wait_ge(s_xlo, l * 16 + (8 + k + 1))) if isinstance(f, int) and m == 0 else None)
                        if isinstance(f, int) and m == 0:
                            mean_square(l * 2 + 1, False)

                def down(f):
                    for m in range(KT):
                        u = U_MLP + KT + m
                        pe.wait_ge(s_wlo, l * NU + f * U_QUARTER + (u + 1))
                        pe.wait_ge(s_gfree, l * NG + f * U_QUARTER + (G_MLP + KT + m + 1 + GFREE0 - 2))
                        tile(G[m % 2][:, :], u, H,
                             (lambda k: pe.wait_ge(s_hlo, l * (QUARTERS * KT) + f * KT + (k + 1))) if m == 0 else None)

                up(0)
                with pe.Fori(0, QUARTERS - 1) as f:
                    down(f)
                    up(f + 1)
                down(QUARTERS - 1)
            mean_square(L * 2, False)


def _columns(w, cols):
    import numpy as np
    w = w[:, cols]
    return np.ascontiguousarray(w.reshape(-1, P, w.shape[1]).transpose(1, 0, 2)).reshape(P, -1)


def _units(w):
    import numpy as np
    r = np.arange
    slabs = np.zeros((L * NU + 2, P, 1024), np.float32)
    for l in range(L):
        n = l * NU
        wi, w1, w2 = w["w_in"][l], w["cmp_w1"][l], w["cmp_w2"][l]

        def put(u, slab):
            slabs[n + u, :, :slab.shape[1]] = slab

        for t in range(4):
            put(UNIT["Q", t], _columns(wi, r(128 * t, 128 * t + 128)))
        put(UNIT["KS", 0], _columns(wi, r(768, 896)))
        put(UNIT["KW", 0], _columns(wi, r(1024, 1152)))
        v = _columns(wi, np.concatenate([r(896, 1024), r(1152, 1280)]))
        put(UNIT["V", 0], v[:, 0:1024])
        put(UNIT["V", 1], v[:, 1024:2048])
        put(UNIT["KC", 0], _columns(wi, r(512, 640)))
        put(UNIT["VC", 0], _columns(wi, r(640, 768)))
        put(UNIT["MISC", 0], _columns(wi, np.concatenate([r(1280, 1304), r(1264, 1304), r(1688, 1720), r(1704, 1720), r(1688, 1704)])))
        for t in range(2):
            put(UNIT["CQ", t], _columns(wi, r(1304 + 128 * t, 1432 + 128 * t)))
        put(UNIT["CQ", 2], _columns(wi, r(1560, 1688)))
        for i in range(2 * KT):
            put(UNIT["GATE", i], _columns(wi, r(1720 + 128 * i, 1848 + 128 * i)))
        for kind in range(2):
            slab = _columns(w1[kind], r(256))
            for i in range(4):
                put(UNIT["W1", 4 * kind + i], slab[:, 1024 * i:1024 * i + 1024])
        put(UNIT["W2K", 0], _columns(w2[0], np.concatenate([r(64), r(64)])))
        put(UNIT["W2V", 0], _columns(w2[1], r(64)))
        for p in range(PAIRS):
            head = np.concatenate([r(96), r(80, 96), r(64, 80)])
            uq = _columns(w["mla_w_uq"][l], np.concatenate([192 * p + head, 192 * p + 96 + head]))
            kv = [256 * p + 128 * e + o + r(64) for o in (0, 64) for e in range(2)]
            put(U_MLA + p, np.concatenate([uq, _columns(w["mla_w_ukv"][l], np.concatenate(kv))], axis=1))
        for m in range(KT):
            c = r(128 * m, 128 * m + 128)
            put(U_WO + m, np.concatenate([_columns(w["nsa_w_o"][l], c), _columns(w["mla_w_o"][l], c)], axis=1))
            put(U_OUT + m, _columns(w["w_out"][l], c))
            for f in range(QUARTERS):
                put(U_MLP + f * U_QUARTER + m, _columns(w["w_up"][l], D * f + c))
                put(U_MLP + f * U_QUARTER + KT + m, _columns(w["w_down"][l][D * f:D * f + D], c))
    return slabs


def _params(w):
    import numpy as np
    cols = []
    for l in range(L):
        for name in ("attn_norm", "mlp_norm", "mla_q_norm", "mla_kv_norm"):
            cols.append(w[name][l].reshape(-1, P).T)
        for kind in range(2):
            cols.append(w["cmp_pe"][l, kind].reshape(16, P).T)
    cols.append(w["final_norm"].reshape(-1, P).T)
    return np.ascontiguousarray(np.concatenate(cols, axis=1))


def _constants():
    import numpy as np

    def angles(d):
        inv = np.float32(10000.0) ** (-np.arange(0, d, 2, dtype=np.float32) / np.float32(d))
        a = np.arange(S, dtype=np.float32)[None, :] * inv.astype(np.float32)[:, None]
        return np.cos(a).astype(np.float32), np.sin(a).astype(np.float32)

    c, s = angles(64)
    cm, sm = angles(32)
    tables = np.stack([np.concatenate([c, c, c, c]), np.concatenate([s, -s, s, -s]),
                       np.concatenate([np.ones((64, S), np.float32), cm, cm, -sm, sm])], axis=1)
    q = np.arange(P)
    seen = (16 * np.arange(NC) + 31)[None, None, :] <= (P * np.arange(QT)[None, :, None] + q[:, None, None])
    seen &= (np.arange(NC) < N_CMP)[None, None, :]
    eye = np.eye(P, dtype=np.float32)
    cf = np.stack([eye, seen.reshape(P, P).astype(np.float32)], axis=1)
    neg = np.float32(-1e30)
    cb = np.stack([eye, np.where(q[None, :] <= q[:, None], 0, neg), np.where(seen.reshape(P, P), 0, neg)], axis=1)
    return np.ascontiguousarray(tables.astype(np.float32)), cf, np.ascontiguousarray(cb.astype(np.float32))


def kernel(**inputs):
    import numpy as np
    import concourse.bacc as bacc
    from concourse import mybir as mb
    from concourse.bass_utils import run_bass_kernel_spmd as run

    w = {k: np.asarray(v) for k, v in inputs.items()}
    tables, cf, cb = _constants()
    arrays = {
        "units": _units(w), "params": _params(w), "tables": tables, "cf32": cf, "cmasks": cb,
        "x_in": np.ascontiguousarray(w["x"][0].T.reshape(KT, P, S).transpose(1, 0, 2)),
    }
    nc = bacc.Bacc("TRN2", target_bir_lowering=False, num_devices=1)
    ins = {k: nc.dram_tensor(k, v.shape, mb.dt.from_np(v.dtype), kind="ExternalInput").ap() for k, v in arrays.items()}
    gates = nc.dram_tensor("gates", (2 * KT, P, S), mb.dt.float32, kind="Internal").ap()
    out = nc.dram_tensor("out", (KT, P, S), mb.dt.float32, kind="ExternalOutput").ap()
    build(nc, ins["units"], ins["params"], ins["x_in"], ins["tables"], ins["cf32"], ins["cmasks"], gates, out)
    r = run(nc, [arrays], core_ids=[0])
    return np.ascontiguousarray(r.results[0]["out"].reshape(D, S).T).reshape(1, S, D)
```
